# Optimizing a Trainium2 kernel written in Bass

```python
import jax, jax.numpy as jnp
from jax import lax
import numpy as np

D_MODEL = 1024
BATCH = 1
SEQ = 1024
DEPTH = 1

CHUNK = 64
LEFT_CHUNKS = 8
BAND = (LEFT_CHUNKS + 1) * CHUNK
REL_CLIP = 128
REL_TABLE = CHUNK + REL_CLIP

RWKV_HEAD_DIM = 64
RWKV_WIDTH = D_MODEL
RWKV_HEADS = RWKV_WIDTH // RWKV_HEAD_DIM
DECAY_LORA = 64
ICLR_LORA = 64
GATE_LORA = 160
RWKV_IN = 3 * RWKV_WIDTH + DECAY_LORA + ICLR_LORA + GATE_LORA

ATT_HEAD_DIM = 64
ATT_WIDTH = D_MODEL
ATT_HEADS = ATT_WIDTH // ATT_HEAD_DIM

IN_WIDTH = RWKV_IN + 3 * ATT_WIDTH + 2 * D_MODEL

MEM_TOKENS = 256
MEM_HEADS = 4
MEM_WIDTH = D_MODEL // 2
MEM_HEAD_DIM = MEM_WIDTH // MEM_HEADS

FFN_HIDDEN = ((8 * D_MODEL) // 3 + 255) // 256 * 256

NORM_EPS = 1e-6
GROUP_NORM_EPS = 64e-5
MASK_VALUE = -1e30

kernel_name = "hybrid_rwkv7_chunkattn_gated_block"

def rms_norm(x, gain):
    xf = x.astype(jnp.float32)
    y = xf * lax.rsqrt(jnp.mean(xf * xf, axis=-1, keepdims=True) + NORM_EPS)
    return (y * gain.astype(jnp.float32)).astype(x.dtype)

def token_shift(p):
    return jnp.pad(p, ((0, 0), (1, 0), (0, 0)))[:, :-1]

def wkv7_scan(r, decay, k, v, kk, a):
    B, S, H, N = r.shape

    def step(state, inp):
        r_t, w_t, k_t, v_t, kk_t, a_t = inp
        sa = jnp.einsum('bhvk,bhk->bhv', state, kk_t)
        state = (state * w_t[:, :, None, :]
                 - sa[..., None] * (kk_t * a_t)[:, :, None, :]
                 + v_t[..., None] * k_t[:, :, None, :])
        return state, jnp.einsum('bhvk,bhk->bhv', state, r_t)

    xs = tuple(jnp.swapaxes(t, 0, 1) for t in (r, decay, k, v, kk, a))
    s0 = jnp.zeros((B, H, N, N), jnp.float32)
    _, ys = lax.scan(step, s0, xs)
    return jnp.swapaxes(ys, 0, 1)

def rwkv7_time_mix(p, shift_mix, decay_base, decay_up, iclr_base, iclr_up, gate_up,
                   key_norm_scale, key_iclr_scale, bonus_scale, lnx_w, lnx_b):
    B, S, _ = p.shape
    f32 = jnp.float32
    z = p + (token_shift(p) - p) * shift_mix
    W = RWKV_WIDTH
    r, k, v, zw, za, zg = jnp.split(
        z, [W, 2 * W, 3 * W, 3 * W + DECAY_LORA, 3 * W + DECAY_LORA + ICLR_LORA], axis=-1)
    w_log = -jax.nn.softplus(-(decay_base + jnp.tanh(zw) @ decay_up)) - 0.5
    decay = jnp.exp(-jnp.exp(w_log.astype(f32)))
    a = jax.nn.sigmoid(iclr_base + za @ iclr_up)
    g = jax.nn.sigmoid(zg) @ gate_up

    def heads(t):
        return t.astype(f32).reshape(B, S, RWKV_HEADS, RWKV_HEAD_DIM)

    kk = heads(k * key_norm_scale)
    kk = kk * lax.rsqrt(jnp.maximum(jnp.sum(kk * kk, axis=-1, keepdims=True), 1e-24))
    k = k * (1.0 + (a - 1.0) * key_iclr_scale)
    rh, kh, vh, ah = heads(r), heads(k), heads(v), heads(a)
    y = wkv7_scan(rh, heads(decay), kh, vh, kk, ah)
    mu = jnp.mean(y, axis=-1, keepdims=True)
    var = jnp.mean(jnp.square(y - mu), axis=-1, keepdims=True)
    y = ((y - mu) * lax.rsqrt(var + GROUP_NORM_EPS)).reshape(B, S, W)
    y = y * lnx_w.astype(f32) + lnx_b.astype(f32)
    bonus = jnp.sum(rh * kh * bonus_scale.astype(f32), axis=-1, keepdims=True) * vh
    out = (y + bonus.reshape(B, S, W)) * g.astype(f32)
    return out.astype(p.dtype)

def chunk_attention(q, k, v, rel_bias):
    B, S, _ = q.shape
    n_chunks = S // CHUNK
    pad = LEFT_CHUNKS * CHUNK
    q = q.reshape(B, S, ATT_HEADS, ATT_HEAD_DIM)
    k_pad = jnp.pad(k.reshape(B, S, ATT_HEADS, ATT_HEAD_DIM), ((0, 0), (pad, 0), (0, 0), (0, 0)))
    v_pad = jnp.pad(v.reshape(B, S, ATT_HEADS, ATT_HEAD_DIM), ((0, 0), (pad, 0), (0, 0), (0, 0)))
    dist = jnp.arange(CHUNK)[:, None] - jnp.arange(BAND)[None, :] + pad
    idx = jnp.minimum(dist, REL_CLIP) + (CHUNK - 1)
    bias = rel_bias.astype(jnp.float32)[:, idx]
    scale = ATT_HEAD_DIM ** -0.5

    def one_chunk(c):
        start = c * CHUNK
        qc = lax.dynamic_slice_in_dim(q, start, CHUNK, axis=1)
        kc = lax.dynamic_slice_in_dim(k_pad, start, BAND, axis=1)
        vc = lax.dynamic_slice_in_dim(v_pad, start, BAND, axis=1)
        s = jnp.einsum('bqhd,bkhd->bhqk', qc, kc).astype(jnp.float32) * scale + bias
        valid = (start - pad + jnp.arange(BAND)) >= 0
        s = jnp.where(valid[None, None, None, :], s, MASK_VALUE)
        pr = jax.nn.softmax(s, axis=-1).astype(vc.dtype)
        return jnp.einsum('bhqk,bkhd->bqhd', pr, vc)

    out = lax.map(one_chunk, jnp.arange(n_chunks))
    return jnp.transpose(out, (1, 0, 2, 3, 4)).reshape(B, S, ATT_WIDTH)

def memory_cross_attention(h, mem_n, w_q, w_kv, w_o):
    B, S, _ = h.shape
    M = mem_n.shape[1]
    q = (h @ w_q).reshape(B, S, MEM_HEADS, MEM_HEAD_DIM)
    k, v = jnp.split(mem_n @ w_kv, 2, axis=-1)
    k = k.reshape(B, M, MEM_HEADS, MEM_HEAD_DIM)
    v = v.reshape(B, M, MEM_HEADS, MEM_HEAD_DIM)
    s = jnp.einsum('bshd,bmhd->bhsm', q, k).astype(jnp.float32) * (MEM_HEAD_DIM ** -0.5)
    pr = jax.nn.softmax(s, axis=-1).astype(v.dtype)
    o = jnp.einsum('bhsm,bmhd->bshd', pr, v).reshape(B, S, MEM_WIDTH)
    return o @ w_o

def swiglu_ffn(h, w_in, w_out):
    gate, up = jnp.split(h @ w_in, 2, axis=-1)
    return (jax.nn.silu(gate) * up) @ w_out

def setup_inputs(seed: int = 0) -> dict:
    key = jax.random.key(seed)
    ks = iter(jax.random.split(key, 48))

    def nrm(shape, scale):
        return jax.random.normal(next(ks), shape, jnp.float32) * scale

    def gain(width=D_MODEL):
        return 1.0 + nrm((DEPTH, width), 0.02)

    L = DEPTH
    return {
        "x": nrm((BATCH, SEQ, D_MODEL), 1.0),
        "mem": nrm((BATCH, MEM_TOKENS, D_MODEL), 1.0),
        "g_pre_mix": gain(),
        "g_post_mix": gain(),
        "w_in": nrm((L, D_MODEL, IN_WIDTH), D_MODEL ** -0.5),
        "shift_mix": jax.random.uniform(next(ks), (L, RWKV_IN), jnp.float32),
        "decay_base": jax.random.uniform(next(ks), (L, RWKV_WIDTH), jnp.float32, -6.0, -1.0),
        "decay_up": nrm((L, DECAY_LORA, RWKV_WIDTH), DECAY_LORA ** -0.5),
        "iclr_base": nrm((L, RWKV_WIDTH), 0.5),
        "iclr_up": nrm((L, ICLR_LORA, RWKV_WIDTH), ICLR_LORA ** -0.5),
        "gate_up": nrm((L, GATE_LORA, RWKV_WIDTH), GATE_LORA ** -0.5),
        "key_norm_scale": 0.85 + nrm((L, RWKV_WIDTH), 0.02),
        "key_iclr_scale": 1.0 + nrm((L, RWKV_WIDTH), 0.02),
        "bonus_scale": nrm((L, RWKV_HEADS, RWKV_HEAD_DIM), 0.1),
        "lnx_w": gain(RWKV_WIDTH),
        "lnx_b": nrm((L, RWKV_WIDTH), 0.02),
        "rel_bias": nrm((L, ATT_HEADS, REL_TABLE), 0.1),
        "w_branch_a": nrm((L, RWKV_WIDTH, D_MODEL), RWKV_WIDTH ** -0.5),
        "w_branch_b": nrm((L, ATT_WIDTH, D_MODEL), ATT_WIDTH ** -0.5),
        "w_out": nrm((L, D_MODEL, D_MODEL), D_MODEL ** -0.5),
        "g_pre_cross": gain(),
        "g_post_cross": gain(),
        "g_mem": gain(),
        "w_q_mem": nrm((L, D_MODEL, MEM_WIDTH), D_MODEL ** -0.5),
        "w_kv_mem": nrm((L, D_MODEL, 2 * MEM_WIDTH), D_MODEL ** -0.5),
        "w_o_mem": nrm((L, MEM_WIDTH, D_MODEL), MEM_WIDTH ** -0.5),
        "g_pre_ffn": gain(),
        "g_post_ffn": gain(),
        "w_ffn_in": nrm((L, D_MODEL, 2 * FFN_HIDDEN), D_MODEL ** -0.5),
        "w_ffn_out": nrm((L, FFN_HIDDEN, D_MODEL), FFN_HIDDEN ** -0.5),
    }

def reference(x, mem, g_pre_mix, g_post_mix, w_in, shift_mix, decay_base, decay_up,
              iclr_base, iclr_up, gate_up, key_norm_scale, key_iclr_scale, bonus_scale,
              lnx_w, lnx_b, rel_bias, w_branch_a, w_branch_b, w_out,
              g_pre_cross, g_post_cross, g_mem, w_q_mem, w_kv_mem, w_o_mem,
              g_pre_ffn, g_post_ffn, w_ffn_in, w_ffn_out):
    split_at = [RWKV_IN,
                RWKV_IN + ATT_WIDTH,
                RWKV_IN + 2 * ATT_WIDTH,
                RWKV_IN + 3 * ATT_WIDTH,
                RWKV_IN + 3 * ATT_WIDTH + D_MODEL]
    for l in range(DEPTH):
        h = rms_norm(x, g_pre_mix[l])
        proj = h @ w_in[l]
        p_rwkv, q, k, v, z_ga, z_gb = jnp.split(proj, split_at, axis=-1)
        y_a = rwkv7_time_mix(p_rwkv, shift_mix[l], decay_base[l], decay_up[l],
                             iclr_base[l], iclr_up[l], gate_up[l], key_norm_scale[l],
                             key_iclr_scale[l], bonus_scale[l], lnx_w[l], lnx_b[l])
        y_b = chunk_attention(q, k, v, rel_bias[l])
        mixed = (jax.nn.sigmoid(z_ga) * (y_a @ w_branch_a[l])
                 + jax.nn.sigmoid(z_gb) * (y_b @ w_branch_b[l]))
        x = x + rms_norm(mixed @ w_out[l], g_post_mix[l])
        h = rms_norm(x, g_pre_cross[l])
        m = rms_norm(mem, g_mem[l])
        x = x + rms_norm(memory_cross_attention(h, m, w_q_mem[l], w_kv_mem[l], w_o_mem[l]),
                         g_post_cross[l])
        h = rms_norm(x, g_pre_ffn[l])
        x = x + rms_norm(swiglu_ffn(h, w_ffn_in[l], w_ffn_out[l]), g_post_ffn[l])
    return x


_drawn_inputs = setup_inputs


def setup_inputs(seed=0):
    import zlib

    import numpy as np

    out = dict(_drawn_inputs(seed))
    spreads = {}
    factors = {'g_post_mix': 3.771,
     'key_norm_scale': 3.572,
     'key_iclr_scale': 3.351,
     'lnx_w': 3.913,
     'lnx_b': 3.724,
     'rel_bias': 5.006,
     'g_pre_cross': 4.537,
     'g_post_cross': 12.656,
     'g_mem': 2.949,
     'g_pre_ffn': 3.923,
     'g_post_ffn': 26.455}
    for name, (base, spread) in spreads.items():
        noise = np.random.default_rng([zlib.crc32(name.encode()), seed]).standard_normal(out[name].shape)
        drawn = base * np.exp(spread * noise) if base else spread * noise
        out[name] = __import__('jax').numpy.asarray(drawn.astype(out[name].dtype))
    for name, factor in factors.items():
        out[name] = (out[name] * factor).astype(out[name].dtype)
    return out
```

```python
from contextlib import ExitStack

import concourse.bass as bass
from concourse import mybir

P = 128
D = 1024
SEQ = 1024
KT = D // P
NT = SEQ // P
HALF = 512
HP = 8
C = 64
NC_ = SEQ // C
G = 2
GC = NC_ // G
MEM = 256
MH = 4
FFN = 2816
FT = FFN // P
FGROUPS = [(0, 8), (8, 8), (16, 6)]
BANDT = 5
BAND = BANDT * P
EXT = 768
PP = 10
EXP_HALF = 0.6065306597126334
LEVELS = [2, 4, 8, 16, 32]
EPS = 1e-6
GN_EPS = 64e-5
MASKED = -1e30

F32 = mybir.dt.float32
F32R = mybir.dt.float32r
ALU = mybir.AluOpType
ACT = mybir.ActivationFunctionType

C_ID = 0
C_MASK = C_ID + P
C_EYE = C_MASK + P
C_NL1 = C_EYE + C
C_NL1T = C_NL1 + C
C_LV = C_NL1T + C
C_ONES = C_LV + C * len(LEVELS)
C_RST = C_ONES + P
C_N = C_RST + SEQ

(MIX_R, MIX_K, MIX_V, DEC_B, ICL_B, KNS, KIS, BON, LNW, LNB) = range(PP)
Q_PRE = HP * PP
Q_CROSS = Q_PRE + KT
Q_FFN = Q_CROSS + KT
Q_MEM = Q_FFN + KT
Q_LORA = Q_MEM + KT
Q_N = Q_LORA + 3
OM_R, OM_K, OM_V, OM_KIS = PP, PP + 1, PP + 2, PP + 3

NB_LORA = 0
NB_HEAD = 3
NB_GA = NB_HEAD + 6 * HP
NB_GB = NB_GA + 2 * KT
NB_OUT = NB_GB + 2 * KT
NB_MEM = NB_OUT + KT
NB_Q = NB_MEM + 8
NB_O = NB_Q + MH
NB_FFN = NB_O + 4
NB_N = NB_FFN + 2 * FT + 8 * len(FGROUPS)


class Steps:

    def __init__(self, sem, names, looped=False):
        self.sem, self.n, self.looped = sem, len(names), looped
        self.index = {name: i + 1 for i, name in enumerate(names)}
        assert len(self.index) == self.n
        self.at = 0

    def done(self, name, rnd=0, back=0):
        return (rnd + 1 - back) * self.n + self.index[name] if self.looped else self.index[name]

    def one(self, name):
        self.at += 1
        assert self.index[name] == self.at, (name, self.at)
        return 1

    def close(self):
        assert self.at == self.n, (self.at, self.n)


def settle(eng, passed):
    eng.sem_inc(passed, 1)


def weight_stream(nc, block, wblocks, first, count, raw, whi, wlo, loaded, split, used):
    assert count >= 4

    @block.sync
    def _(sp):
        for s in range(2):
            sp.dma_start(raw[:, s], wblocks[first + s]).then_inc(loaded[s], 16)
        with sp.Fori(1, count // 2) as i:
            for s in range(2):
                sp.wait_ge(split, i * 2 + s - 1)
                sp.dma_start(raw[:, s], wblocks[bass.ds(i * 2 + (s + first), 1)].rearrange("a p k m -> p (a k) m")).then_inc(loaded[s], 16)
        if count % 2:
            sp.wait_ge(split, count - 2)
            sp.dma_start(raw[:, 0], wblocks[first + count - 1]).then_inc(loaded[0], 16)

    @block.gpsimd
    def _(pool):
        def one(s, i):
            pool.wait_ge(loaded[s], i * 16 + 16)
            settle(pool, passed)
            pool.tensor_copy(whi[:, s], raw[:, s]).then_inc(split_hi, 1)
            pool.wait_ge(split_hi, i * 2 + s + 1)
            pool.tensor_tensor(wlo[:, s], raw[:, s], whi[:, s].bitcast(F32), ALU.subtract).then_inc(split, 1)

        split_hi, passed = used[1:]
        for s in range(2):
            one(s, 0)
        with pool.Fori(1, count // 2) as i:
            for s in range(2):
                pool.wait_ge(used[0], i * 2 + s - 1)
                one(s, i)
        if count % 2:
            pool.wait_ge(used[0], count - 2)
            one(0, count // 2)


def mm3(nc, out, whi, wlo, ahi, alo, start, stop):
    nc.tensor.matmul(out, whi, ahi, start=start, stop=False)
    nc.tensor.matmul(out, whi, alo, start=False, stop=False)
    return nc.tensor.matmul(out, wlo, ahi, start=False, stop=stop)


def gemm(nc, out, whi, wlo, ahi, alo, kts, cols):
    last = None
    for n, kt in enumerate(kts):
        last = mm3(nc, out, whi[:, n], wlo[:, n], ahi[:, kt, cols], alo[:, kt, cols], n == 0, n == len(kts) - 1)
    return last


def hybrid_block(nc, x, mem, wblocks, lora_up, gate_up2, params, consts, rel_rev, g_rows, out):
    ctx = ExitStack()
    with ctx:
        env = Env(nc, ctx)
        e = env
        e.x, e.mem, e.wblocks, e.lora_up, e.gate_up2 = x, mem, wblocks, lora_up, gate_up2
        e.params_d, e.consts_d, e.rel_rev, e.g_rows, e.out = params, consts, rel_rev, g_rows, out
        dram = lambda name, shape: nc.dram_tensor(name, shape, F32, kind="Internal").ap()
        e.ya_d = dram("ya_scratch", (HP, P, SEQ))
        e.yb_d = dram("yb_scratch", (HP, P, SEQ))
        e.ext_d = dram("ext_scratch", (2 * HP, EXT))
        e.bias_d = dram("bias_scratch", (2 * HP, P, BAND))
        e.x1_d = dram("x1_scratch", (SEQ, D))
        e.x2_d = dram("x2_scratch", (SEQ, D))
        e.consts = e.sb("consts", [P, C_RST])
        e.par = e.sb("par", [P, Q_N])
        e.ahi = e.sb("act_hi", [P, KT, SEQ], F32R)
        e.alo = e.sb("act_lo", [P, KT, SEQ], F32R)
        e.raw = e.sb("w_raw", [P, 2, KT, P])
        e.whi = e.sb("w_hi", [P, 2, KT, P], F32R)
        e.wlo = e.sb("w_lo", [P, 2, KT, P], F32R)
        psum = ctx.enter_context(nc.psum_tensor("banks", [P, 8 * HALF], F32))
        e.banks = psum
        e.ps = [psum[:, b * HALF:(b + 1) * HALF] for b in range(8)]
        e.x_loaded = sems(nc, ctx, *[f"x_loaded{i}" for i in range(NT)])
        e.x_stored = sems(nc, ctx, *[f"x_stored{i}" for i in range(NT)])
        e.ident = e.consts[:, C_ID:C_ID + P]
        norm_phase(e)
        mix_phase(e)
        e.mo = e.sb("mixed", [P, KT, SEQ])
        merge_phase(e)
        project_phase(e, "out", NB_OUT, 1, True)
        finish_phase(e, "mixfin", 0, e.x, e.x1_d, e.par[:, Q_CROSS:Q_CROSS + KT])
        cross_phase(e)
        project_phase(e, "cross_o", NB_O, 2, False)
        finish_phase(e, "crossfin", 1, e.x1_d, e.x2_d, e.par[:, Q_FFN:Q_FFN + KT])
        ffn_phase(e)
        finish_phase(e, "ffnfin", 2, e.x2_d, e.out, None)


class Env:

    def __init__(self, nc, ctx):
        self.nc, self.ctx = nc, ctx

    def sb(self, name, shape, dt=F32, ctx=None):
        return (ctx or self.ctx).enter_context(self.nc.sbuf_tensor(name, shape, dt))


def sems(nc, ctx, *names):
    return [ctx.enter_context(nc.semaphore(n)) for n in names]


def weight_sems(e, ctx, tag):
    nc = e.nc
    loaded = sems(nc, ctx, f"{tag}_w_loaded0", f"{tag}_w_loaded1")
    split, used, split_hi, passed = sems(nc, ctx, f"{tag}_w_split", f"{tag}_w_used", f"{tag}_w_split_hi", f"{tag}_pool_passed")
    return loaded, split, (used, split_hi, passed)


def start_weights(e, block, first, count, w):
    weight_stream(e.nc, block, e.wblocks, first, count, e.raw, e.whi, e.wlo, w[0], w[1], w[2])


def norm_steps(tag, tiles):
    halves = range(max(1, tiles // 4))
    act = [(tag, "sq", i) for i in range(tiles)] + [(tag, "sd")]
    act += [(tag, "scaled", kt, h) for kt in range(KT) for h in halves]
    vec = [(tag, "ms"), (tag, "rs")] + [(tag, "xn", i) for i in range(tiles)]
    vec += [(tag, s, kt, h) for kt in range(KT) for h in halves for s in ("hi", "lo")]
    pe = [(tag, "T", kt, h) for kt in range(KT) for h in halves]
    return act, vec, pe


def norm_act(e, act, A, V, PE, tag, xb, tiles, st, junk, stage, gain, loaded, first=True):
    nc, width = e.nc, min(4, tiles) * P
    if first:
        for i in range(tiles):
            loaded(act, i)
            if i:
                act.wait_ge(A.sem, A.done((tag, "sq", i - 1)))
            nc.scalar.activation(junk, xb[:, i], ACT.Square, accum_out=st[:, i:i + 1]).then_inc(A.sem, A.one((tag, "sq", i)))
    act.wait_ge(V.sem, V.done((tag, "ms")))
    nc.scalar.activation(st[:, 8:8 + tiles], st[:, 0:tiles], ACT.Sqrt).then_inc(A.sem, A.one((tag, "sd")))
    halves = max(1, tiles // 4)
    for kt in range(KT):
        for h in range(halves):
            n = kt * halves + h
            act.wait_ge(PE.sem, PE.done((tag, "T", kt, h)))
            if n >= 2:
                act.wait_ge(V.sem, V.done((tag, "lo", (n - 2) // halves, (n - 2) % halves)))
            nc.scalar.activation(stage[:, n % 2, 0:width], e.ps[n % 4][:, 0:width], ACT.Copy,
                                 scale=gain[:, kt:kt + 1]).then_inc(A.sem, A.one((tag, "scaled", kt, h)))


def norm_vec(e, vec, A, V, tag, xb, tiles, st, stage, hi, lo, stored=None):
    nc, width = e.nc, min(4, tiles) * P
    vec.wait_ge(A.sem, A.done((tag, "sq", tiles - 1)))
    nc.vector.tensor_scalar(st[:, 0:tiles], st[:, 0:tiles], 1.0 / D, EPS, ALU.mult, ALU.add).then_inc(V.sem, V.one((tag, "ms")))
    vec.wait_ge(A.sem, A.done((tag, "sd")))
    nc.vector.reciprocal(st[:, 0:tiles], st[:, 8:8 + tiles]).then_inc(V.sem, V.one((tag, "rs")))
    vec.wait_ge(V.sem, V.done((tag, "rs")))
    for i in range(tiles):
        if stored:
            stored(vec, i)
        nc.vector.tensor_scalar(xb[:, i], xb[:, i], st[:, i:i + 1], None, ALU.mult).then_inc(V.sem, V.one((tag, "xn", i)))
    halves = max(1, tiles // 4)
    for kt in range(KT):
        for h in range(halves):
            n = kt * halves + h
            cols = slice(h * HALF, h * HALF + width)
            vec.wait_ge(A.sem, A.done((tag, "scaled", kt, h)))
            nc.vector.tensor_copy(hi[:, kt, cols], stage[:, n % 2, 0:width]).then_inc(V.sem, V.one((tag, "hi", kt, h)))
            vec.wait_ge(V.sem, V.done((tag, "hi", kt, h)))
            nc.vector.tensor_tensor(lo[:, kt, cols], stage[:, n % 2, 0:width], hi[:, kt, cols].bitcast(F32),
                                    ALU.subtract).then_inc(V.sem, V.one((tag, "lo", kt, h)))


def norm_pe(e, pe, A, V, PE, tag, xb, tiles):
    nc = e.nc
    halves = max(1, tiles // 4)
    for kt in range(KT):
        for h in range(halves):
            n = kt * halves + h
            if kt == 0:
                pe.wait_ge(V.sem, V.done((tag, "xn", min(4 * h + 3, tiles - 1))))
            if n >= 4:
                pe.wait_ge(A.sem, A.done((tag, "scaled", (n - 4) // halves, (n - 4) % halves)))
            for i in range(min(4, tiles)):
                last = nc.tensor.transpose(e.ps[n % 4][:, i * P:(i + 1) * P], xb[:, 4 * h + i, kt * P:(kt + 1) * P], e.ident)
            last.then_inc(PE.sem, PE.one((tag, "T", kt, h)))


def norm_phase(e):
    nc = e.nc
    with ExitStack() as ctx:
        xb = e.sb("x_tok", [P, NT, D], ctx=ctx)
        junk = e.sb("squares", [P, D], ctx=ctx)
        stage = e.sb("stage", [P, 2, HALF], ctx=ctx)
        st = e.sb("stats", [P, 16], ctx=ctx)
        ext = e.sb("ext", [2 * HP, EXT], ctx=ctx)
        x_in = e.x_loaded
        const_in, par_in, rel_in, ext_out, bias_out = sems(nc, e.ctx, "const_in", "par_in", "rel_in", "ext_out", "bias_out")
        a_s, v_s, p_s = sems(nc, e.ctx, "norm_act", "norm_vec", "norm_pe")
        na, nv, np_ = norm_steps("x", NT)
        A, V, PE = Steps(a_s, na), Steps(v_s, [("ext", 0), ("ext", 1)] + nv), Steps(p_s, np_)
        block = ctx.enter_context(nc.Block())

        @block.sync
        def _(sp):
            for i in range(NT):
                sp.dma_start(xb[:, i], e.x[i * P:(i + 1) * P, :]).then_inc(x_in[i], 16)
            sp.dma_start(e.consts[:], e.consts_d[:, 0:C_RST]).then_inc(const_in, 16)
            sp.dma_start(e.par[:], e.params_d).then_inc(par_in, 16)
            sp.dma_start(ext[:, 511:703], e.rel_rev).then_inc(rel_in, 16)
            sp.wait_ge(V.sem, V.done(("ext", 1)))
            sp.dma_start(e.ext_d, ext[:]).then_inc(ext_out, 16)
            sp.wait_ge(ext_out, 16)
            sp.dma_start(e.bias_d, bass.AP(tensor=e.ext_d.tensor, offset=P - 1, ap=[[EXT, 2 * HP], [-1, P], [1, BAND]])).then_inc(bias_out, 16)
            sp.wait_ge(bias_out, 16)

        @block.scalar
        def _(act):
            act.wait_ge(par_in, 16)
            norm_act(e, act, A, V, PE, "x", xb, NT, st, junk[:], stage, e.par[:, Q_PRE:Q_PRE + KT],
                     lambda eng, i: eng.wait_ge(x_in[i], 16))
            A.close()

        @block.vector
        def _(vec):
            vec.wait_ge(rel_in, 16)
            nc.vector.tensor_copy(ext[:, 0:511], ext[:, 511:512].broadcast_to([2 * HP, 511])).then_inc(v_s, V.one(("ext", 0)))
            nc.vector.memset(ext[:, 703:EXT], 0.0).then_inc(v_s, V.one(("ext", 1)))
            norm_vec(e, vec, A, V, "x", xb, NT, st, stage, e.ahi, e.alo)
            V.close()

        @block.tensor
        def _(pe):
            pe.wait_ge(const_in, 16)
            norm_pe(e, pe, A, V, PE, "x", xb, NT)
            PE.close()


def mix_phase(e):
    nc = e.nc
    with ExitStack() as ctx:
        sb = lambda name, shape, dt=F32: e.sb(name, shape, dt, ctx)
        rst = sb("chunk_restart", [P, SEQ])
        lora = sb("lora", [P, SEQ])
        sg = sb("sig_gate", [P, 2, SEQ])
        lup = sb("lora_up", [P, P])
        gup = sb("gate_up", [P, 2, P])
        bias = sb("bias", [P, 2, BAND])
        cur = sb("cur", [P, PP + 4])
        Z = sb("work", [P, 7172])
        r_t, k_t, a_t, kk_t = (sb(n, [P, SEQ]) for n in ("r_cm", "k_cm", "a_cm", "kk_cm"))
        v_t = sb("v_cm", [P, SEQ])
        QR = sb("kq_rt", [P, NC_, 2 * C])
        BK = sb("bt_kt", [P, NC_, 2 * C])
        qT, kT, vT = (sb(n, [P, SEQ]) for n in ("att_q", "att_k", "att_v"))
        vtm = sb("att_v_tok", [P, NT, P])
        yb = sb("att_out", [P, SEQ])
        pe_s = sb("probs", [P, 2, BAND])
        pT = sb("probs_T", [P, BAND])
        small = sb("small", [P, 8])
        st_S = sb("state", [P, 2, C])
        st_L = sb("state_decayed", [P, C])
        Wt = sb("w_tok", [P, C])
        Ut = sb("u_tok", [P, C])
        lamC = sb("chunk_decay", [P, NC_])

        Pb = [Z[:, 0:1025], Z[:, 5122:6147]]
        Tb = [Z[:, 1026:2050], Z[:, 6148:7172]]
        sig, Ls, Linv, Lam, Lamx = (Z[:, 2050 + 1024 * i:3074 + 1024 * i] for i in range(5))
        sq, rs_kk = Z[:, 1026:2050], Z[:, 0:1024]
        M1 = Z[:, 0:2048].rearrange("p (c t) -> p c t", t=2 * C)
        M2 = Z[:, 2048:4096].rearrange("p (c t) -> p c t", t=2 * C)
        T, TT, X = (Z[:, 4096 + 1024 * i:5120 + 1024 * i].rearrange("p (c t) -> p c t", t=C) for i in range(3))
        Vm, Bm, Km = (t[:].rearrange("p (c t) -> p c t", t=C) for t in (k_t, kk_t, a_t))
        yT = Z[:, 4096:5120]
        gsq, grs = Z[:, 6144:6656], Z[:, 6656:7168]

        mask2 = e.consts[:, C_MASK:C_MASK + P]
        bc = lambda ap, n: ap.rearrange("p (a t) -> p a t", a=1).broadcast_to([P, n, ap.shape[1]])
        eye8 = bc(e.consts[:, C_EYE:C_EYE + C], GC)
        level = {m: bc(e.consts[:, C_LV + C * n:C_LV + C * (n + 1)], GC) for n, m in enumerate(LEVELS)}
        ones = e.consts[:, C_ONES:C_ONES + P]
        param = lambda i: cur[:, i:i + 1]

        w = weight_sems(e, e.ctx, "mix")
        loaded, w_split, (w_used, _, _) = w
        pro_act, pro_vec, pro_pe = sems(nc, e.ctx, "lora_act", "lora_vec", "lora_pe")
        act_done, vec_done, pe_done = sems(nc, e.ctx, "act_done", "vec_done", "pe_done")
        pe_passed, vec_passed = sems(nc, e.ctx, "pe_passed", "vec_passed")
        rst_in, lup_in, gup_in, ya_out, yb_out = sems(nc, e.ctx, "rst_in", "lup_in", "gup_in", "ya_out", "yb_out")
        bias_in = sems(nc, e.ctx, "bias_in0", "bias_in1")

        def unit(u):
            j, i = u % 2, u // 2
            return j, i, min(i + 1, BANDT)

        NU = 16
        halves = (0, 1)
        a_names = [("aq", h) for h in halves] + [("ak", h) for h in halves] + [("av", h) for h in halves]
        for n in "rkv":
            for h in halves:
                a_names += [("P", n, h), ("T", n, h)]
        a_names += [("sig", h) for h in halves] + [("a", h) for h in halves]
        a_names += ["kksq", "Linv", "Lam", "Lamx", ("kksd", 0), ("kksd", 1), ("vtm", 0), ("vtm", 1)]
        a_names += [(n, g) for g in range(G) for n in ("Vm", "Bm", "Km")]
        for m in LEVELS:
            for g in range(G):
                a_names += ([("T", m, g)] if m != LEVELS[-1] else []) + [("TT", m, g)]
        v_names = ["cur", "om", "omk", "pz0", "pz1", ("bmask", 0), ("bmask", 1)] + [("z", n) for n in "rkv"]
        v_names += ["scan", "Lx", "lamC", ("kkmax", 0), ("kkmax", 1), "kkrs", "kk", "b", "bt", "am", "kp", "kt", "kq", "rt", "rk"]
        for g in range(G):
            v_names += [("X1", g, 0), ("X1", g, 1), ("X2", g, 0), ("X2", g, 1), ("A", g)]
            v_names += [("T2", g), ("T2T0", g), ("T2T", g), ("ATI", g)]
        for m in LEVELS:
            v_names += [("X", m, g) for g in range(G)]
        p_names = [(n, h) for n in ("aq", "ak", "av", "r", "k", "v") for h in halves]
        p_names += [("dec", h) for h in halves] + [("icl", h) for h in halves] + [("avT", 0), ("avT", 1)]
        p_names += [("kkss", h) for h in halves]
        for g in range(G):
            p_names += [("X1", g, 0), ("X1", g, 1), ("X2", g, 0), ("X2", g, 1), ("A", g)]
        p_names += [(n, g) for g in range(G) for n in ("Vm", "Bm", "Km")]
        for m in LEVELS:
            p_names += [("X", m, g) for g in range(G)]
            for g in range(G):
                p_names += ([("T", m, g)] if m != LEVELS[-1] else []) + [("TT", m, g)]
        E_AT = {9: 0, NU: 1}
        ELEN = 4

        def e_stage(c):
            return (0, c - 9) if 9 <= c < 9 + ELEN else (None, None)

        def slots_act(c):
            out = []
            if c > 0:
                out += [("pT", c - 1)] + ([("pT5", c - 1)] if unit(c - 1)[2] == 5 else [])
            if c < NC_:
                out += [("Y", c)]
            if c > 0:
                out += [("out", c - 1)]
            if c < NC_:
                out += [("exp", c)]
            return out

        def slots_vec(c):
            out = []
            if c < NC_:
                out += [("W", c), ("ttr", c), ("nmx", c), ("U", c)]
            if c > 0:
                out += [("rin", c - 1), ("pn", c - 1)]
            if c < NC_:
                out += [("SL", c)] * (c > 0) + [("S", c)]
            return out

        def slots_pe(c):
            out = []
            if c < NC_:
                out += [("W", c), ("sc", c), ("U", c)]
            if c > 0:
                out += [("pT", c - 1)]
            if c < NC_:
                out += [("S", c), ("Y", c)]
            if c > 0:
                out += [("out", c - 1)]
            return out

        E_ACT = [["gsq"], ["gsd"], [], []]
        E_VEC = [["yc"], ["gms", "grs", "yn", "yw"], ["bov", "yb"], ["yg"]]
        E_PE = [["mu"], ["var"], ["bo"], ["gt"]]
        for c in range(NC_ + 1):
            a_names += slots_act(c)
            v_names += slots_vec(c)
            p_names += slots_pe(c)
            h, s = e_stage(c)
            if h is not None:
                a_names += [(n, h) for n in E_ACT[s]]
                v_names += [(n, h) for n in E_VEC[s]]
                p_names += [(n, h) for n in E_PE[s]]
        for s in range(ELEN):
            a_names += [(n, 1) for n in E_ACT[s]]
            v_names += [(n, 1) for n in E_VEC[s]]
            p_names += [(n, 1) for n in E_PE[s]]
        A = Steps(act_done, a_names, True)
        V = Steps(vec_done, v_names, True)
        PE = Steps(pe_done, p_names, True)
        LA = Steps(pro_act, [("pc", n, h) for n in range(3) for h in halves] + ["tanh", ("sg", 0), ("sg", 1)])
        LV = Steps(pro_vec, ["zero0", "zero1", "omm", ("t", 0), ("z", 0), ("t", 1), ("z", 1), ("t", 2), ("z", 2)])
        LP = Steps(pro_pe, [("l", n, h) for n in range(3) for h in halves])

        bank = e.ps
        block = ctx.enter_context(nc.Block())
        start_weights(e, block, NB_LORA, NB_GA, w)

        hs = [slice(0, HALF), slice(HALF, SEQ)]
        rows = [slice(0, C), slice(C, P)]

        def gn_pe(pe, hp, h, s):
            if s == 0:
                pe.wait_ge(act_done, A.done(("Y", NC_ // 2 * (h + 1) - 1), hp))
                if h == 1:
                    pe.wait_ge(vec_done, V.done(("yg", 0), hp))
                nc.tensor.matmul(bank[3], ones, yT[:, hs[h]], start=True, stop=True).then_inc(pe_done, PE.one(("mu", h)))
            elif s == 1:
                pe.wait_ge(act_done, A.done(("gsq", h), hp))
                nc.tensor.matmul(bank[3], ones, gsq, start=True, stop=True).then_inc(pe_done, PE.one(("var", h)))
            elif s == 2:
                pe.wait_ge(act_done, A.done(("gsd", h), hp))
                nc.tensor.matmul(bank[3], ones, r_t[:, hs[h]], start=True, stop=True).then_inc(pe_done, PE.one(("bo", h)))
            else:
                pe.wait_ge(vec_done, V.done(("bov", h), hp))
                pe.wait_ge(gup_in, hp * 16 + 16)
                nc.tensor.matmul(bank[3], gup[:, 0, :], sg[:, 0, hs[h]], start=True, stop=False)
                nc.tensor.matmul(bank[3], gup[0:32, 1, :], sg[0:32, 1, hs[h]], start=False, stop=True).then_inc(pe_done, PE.one(("gt", h)))

        def gn_act(act, hp, h, s):
            if s == 0:
                act.wait_ge(vec_done, V.done(("yc", h), hp))
                nc.scalar.activation(gsq, yT[:, hs[h]], ACT.Square).then_inc(act_done, A.one(("gsq", h)))
            elif s == 1:
                act.wait_ge(vec_done, V.done(("gms", h), hp))
                nc.scalar.activation(grs, grs, ACT.Sqrt).then_inc(act_done, A.one(("gsd", h)))
            elif s == 3:
                act.wait_ge(vec_done, V.done(("yg", h), hp))
                act.dma_start(e.ya_d[bass.ds(hp, 1), :, hs[h]].rearrange("a p t -> p (a t)"), yT[:, hs[h]]).then_inc(ya_out, 16)

        def gn_vec(vec, hp, h, s):
            tt, ts, stt = nc.vector.tensor_tensor, nc.vector.tensor_scalar, nc.vector.scalar_tensor_tensor
            y = yT[:, hs[h]]
            if s == 0:
                vec.wait_ge(pe_done, PE.done(("mu", h), hp))
                stt(out=y, in0=bank[3], scalar=-1.0 / C, in1=y, op0=ALU.mult, op1=ALU.add).then_inc(vec_done, V.one(("yc", h)))
                vec.wait_ge(vec_done, V.done(("yc", h), hp))
            elif s == 1:
                vec.wait_ge(pe_done, PE.done(("var", h), hp))
                ts(grs, bank[3], 1.0 / C, GN_EPS, ALU.mult, ALU.add).then_inc(vec_done, V.one(("gms", h)))
                vec.wait_ge(vec_done, V.done(("gms", h), hp))
                vec.wait_ge(act_done, A.done(("gsd", h), hp))
                nc.vector.reciprocal(grs, grs).then_inc(vec_done, V.one(("grs", h)))
                vec.wait_ge(vec_done, V.done(("grs", h), hp))
                tt(y, y, grs, ALU.mult).then_inc(vec_done, V.one(("yn", h)))
                vec.wait_ge(vec_done, V.done(("yn", h), hp))
                ts(y, y, param(LNW), param(LNB), ALU.mult, ALU.add).then_inc(vec_done, V.one(("yw", h)))
                vec.wait_ge(vec_done, V.done(("yw", h), hp))
            elif s == 2:
                vec.wait_ge(pe_done, PE.done(("bo", h), hp))
                tt(gsq, bank[3], v_t[:, hs[h]], ALU.mult).then_inc(vec_done, V.one(("bov", h)))
                vec.wait_ge(vec_done, V.done(("bov", h), hp))
                tt(y, y, gsq, ALU.add).then_inc(vec_done, V.one(("yb", h)))
                vec.wait_ge(vec_done, V.done(("yb", h), hp))
            else:
                vec.wait_ge(pe_done, PE.done(("gt", h), hp))
                tt(y, bank[3], y, ALU.mult).then_inc(vec_done, V.one(("yg", h)))
                vec.wait_ge(vec_done, V.done(("yg", h), hp))

        def mix_pe(pe, hp):
            blk = 3
            proj = [("aq", 0, ("ttr", NU - 1), V, 1), ("ak", 2, ("yg", 1), V, 1), ("av", 0, ("aq", 1), A, 0),
                    ("r", 2, ("ak", 1), A, 0), ("k", 0, ("av", 1), A, 0), ("v", 2, ("T", "r", 1), A, 0)]
            for n, (name, b0, prev, S, back) in enumerate(proj):
                pe.wait_ge(w_split, hp * 6 + blk + n + 1)
                pe.wait_ge(S.sem, S.done(prev, hp, back))
                if name == "ak":
                    pe.wait_ge(act_done, A.done(("pT", NU - 1), hp, 1))
                s = (blk + n) % 2
                for h in halves:
                    last = gemm(nc, bank[b0 + h], e.whi[:, s], e.wlo[:, s], e.ahi, e.alo, range(KT), hs[h])
                    last.then_inc(pe_done, PE.one((name, h)))
            pe.wait_ge(lup_in, hp * 16 + 16)
            pe.wait_ge(vec_done, V.done(("S", NC_ - 1), hp, 1))
            pe.wait_ge(act_done, A.done(("out", NU - 1), hp, 1))
            for h in halves:
                nc.tensor.matmul(bank[4 + h], lup[0:C, :], lora[0:C, hs[h]], start=True, stop=True).then_inc(pe_done, PE.one(("dec", h)))
            for h in halves:
                nc.tensor.matmul(bank[6 + h], lup[C:P, :], lora[C:P, hs[h]], start=True, stop=True).then_inc(pe_done, PE.one(("icl", h)))
            for g in range(2):
                pe.wait_ge(act_done, A.done(("a", g), hp))
                for i in range(4):
                    last = nc.tensor.transpose(bank[6 + g][:, i * P:(i + 1) * P], vT[:, (4 * g + i) * P:(4 * g + i + 1) * P], e.ident)
                last.then_inc(pe_done, PE.one(("avT", g)))
            pe.wait_ge(act_done, A.done("kksq", hp))
            for h in halves:
                nc.tensor.matmul(bank[4 + h], ones, sq[:, hs[h]], start=True, stop=True).then_inc(pe_done, PE.one(("kkss", h)))
            xb = {0: (0, 1, 2, 3, 4), 1: (5, 6, 7, 0, 1)}
            for g in range(G):
                for q in range(2):
                    b = bank[xb[g][q]]
                    if g == 0 and q == 0:
                        pe.wait_ge(vec_done, V.done("rt", hp))
                        pe.wait_ge(act_done, A.done(("T", "k", 1), hp))
                    if g == 1 and q == 0:
                        pe.wait_ge(act_done, A.done(("vtm", 1), hp))
                    settle(pe, pe_passed)
                    for cc in range(4):
                        c = g * GC + q * 4 + cc
                        for j in range(2):
                            last = nc.tensor.matmul(b[rows[j], cc * P:(cc + 1) * P], BK[rows[j], c, 0:C], QR[rows[j], c, :], start=True, stop=True, skip_group_check=True)
                    last.then_inc(pe_done, PE.one(("X1", g, q)))
                for q in range(2):
                    b = bank[xb[g][2 + q]]
                    if g == 0:
                        pe.wait_ge(act_done, A.done(("T", "v", 1), hp))
                    if g == 1 and q == 1:
                        pe.wait_ge(vec_done, V.done(("X1", 0, 0), hp))
                    settle(pe, pe_passed)
                    for cc in range(4):
                        c = g * GC + q * 4 + cc
                        for j in range(2):
                            last = nc.tensor.matmul(b[rows[j], cc * P:(cc + 1) * P], BK[rows[j], c, C:P], QR[rows[j], c, :], start=True, stop=True, skip_group_check=True)
                    last.then_inc(pe_done, PE.one(("X2", g, q)))
                b = bank[xb[g][4]]
                if g == 0:
                    pe.wait_ge(act_done, A.done(("kksd", 0), hp))
                else:
                    pe.wait_ge(vec_done, V.done(("X1", 0, 1), hp))
                settle(pe, pe_passed)
                for cc in range(GC):
                    c = g * GC + cc
                    for j in range(2):
                        last = nc.tensor.matmul(b[rows[j], cc * C:(cc + 1) * C], QR[rows[j], c, 0:C], BK[rows[j], c, 0:C], start=True, stop=True, skip_group_check=True)
                last.then_inc(pe_done, PE.one(("A", g)))
            prev = {(0, 0): ("X2", 0, 0), (0, 1): ("X2", 0, 1), (0, 2): ("A", 0), (1, 0): ("X1", 1, 0), (1, 1): ("X1", 1, 1), (1, 2): ("X2", 1, 0)}
            for g in range(G):
                for n, name in enumerate(("Vm", "Bm", "Km")):
                    b = bank[2 + 3 * g + n]
                    pe.wait_ge(vec_done, V.done(prev[g, n], hp))
                    settle(pe, pe_passed)
                    for cc in range(GC):
                        c = g * GC + cc
                        for j in range(2):
                            src = {"Vm": v_t[rows[j], c * C:(c + 1) * C], "Bm": BK[rows[j], c, 0:C], "Km": BK[rows[j], c, C:P]}[name]
                            last = nc.tensor.matmul(b[rows[j], cc * C:(cc + 1) * C], src, e.consts[rows[j], C_EYE:C_EYE + C], start=True, stop=True, skip_group_check=True)
                    last.then_inc(pe_done, PE.one((name, g)))
            for m in LEVELS:
                for g in range(G):
                    if m == 2:
                        pe.wait_ge(vec_done, V.done(("X2", 1, 1) if g == 0 else ("ATI", 1), hp))
                        pe.wait_ge(act_done, A.done(("Bm", 0), hp))
                    else:
                        pe.wait_ge(act_done, A.done(("T", m // 2, g), hp))
                        pe.wait_ge(vec_done, V.done(("X", m // 2, g), hp))
                    settle(pe, pe_passed)
                    for cc in range(GC):
                        c = g * GC + cc
                        for j in range(2):
                            last = nc.tensor.matmul(bank[3 * g][rows[j], cc * C:(cc + 1) * C], M1[rows[j], c, 0:C], T[rows[j], c, :], start=True, stop=True, skip_group_check=True)
                    last.then_inc(pe_done, PE.one(("X", m, g)))
                for g in range(G):
                    pe.wait_ge(vec_done, V.done(("X", m, g), hp))
                    if m == 2:
                        pe.wait_ge(act_done, A.done(("Vm", 1), hp))
                    else:
                        pe.wait_ge(act_done, A.done(("TT", m // 2, g), hp))
                    if m != LEVELS[-1]:
                        settle(pe, pe_passed)
                        for cc in range(GC):
                            c = g * GC + cc
                            for j in range(2):
                                last = nc.tensor.matmul(bank[3 * g + 1][rows[j], cc * C:(cc + 1) * C], TT[rows[j], c, :], X[rows[j], c, :], start=True, stop=True, skip_group_check=True)
                        last.then_inc(pe_done, PE.one(("T", m, g)))
                    settle(pe, pe_passed)
                    for cc in range(GC):
                        c = g * GC + cc
                        for j in range(2):
                            last = nc.tensor.matmul(bank[3 * g + 2][rows[j], cc * C:(cc + 1) * C], X[rows[j], c, :], TT[rows[j], c, :], start=True, stop=True, skip_group_check=True)
                    last.then_inc(pe_done, PE.one(("TT", m, g)))
            for c in range(NC_ + 1):
                cs = slice(c * C, (c + 1) * C)
                if c < NC_:
                    if c == 0:
                        pe.wait_ge(act_done, A.done(("TT", 32, 1), hp))
                    else:
                        pe.wait_ge(vec_done, V.done(("U", c - 1), hp))
                    settle(pe, pe_passed)
                    for j in range(2):
                        last = nc.tensor.matmul(bank[4][rows[j], 0:C], M2[rows[j], c, 0:C], Vm[rows[j], c, :], start=True, stop=c == 0)
                    if c > 0:
                        pe.wait_ge(vec_done, V.done(("S", c - 1), hp))
                        settle(pe, pe_passed)
                        for j in range(2):
                            last = nc.tensor.matmul(bank[4][rows[j], 0:C], QR[rows[j], c, 0:C], st_S[rows[j], c % 2, :], start=False, stop=True)
                    last.then_inc(pe_done, PE.one(("W", c)))
                    j, i, nk = unit(c)
                    if c == 0:
                        pe.wait_ge(vec_done, V.done(("X", 32, 0), hp))
                    else:
                        pe.wait_ge(vec_done, V.done(("ttr", c - 1), hp))
                    k0 = (i + 1 - nk) * P
                    n0 = min(nk, 4) * P
                    last = nc.tensor.matmul(bank[0][:, 0:n0], qT[rows[j], i * P:(i + 1) * P], kT[rows[j], k0:k0 + n0], start=True, stop=True)
                    if nk == 5:
                        last = nc.tensor.matmul(bank[1][:, 0:P], qT[rows[j], i * P:(i + 1) * P], kT[rows[j], k0 + n0:k0 + n0 + P], start=True, stop=True)
                    last.then_inc(pe_done, PE.one(("sc", c)))
                    pe.wait_ge(vec_done, V.done(("W", c), hp))
                    settle(pe, pe_passed)
                    for j in range(2):
                        last = nc.tensor.matmul(bank[4][rows[j], 0:C], TT[rows[j], c, :], Wt[rows[j], :], start=True, stop=True)
                    last.then_inc(pe_done, PE.one(("U", c)))
                if c > 0:
                    u = c - 1
                    j, i, nk = unit(u)
                    pe.wait_ge(vec_done, V.done(("pn", u), hp))
                    if u > 0:
                        pe.wait_ge(act_done, A.done(("out", u - 1), hp))
                    for t in range(nk):
                        dst = bank[2][:, t * P:(t + 1) * P] if t < 4 else bank[7][:, P:2 * P]
                        last = nc.tensor.transpose(dst, pe_s[:, u % 2, t * P:(t + 1) * P], e.ident)
                    last.then_inc(pe_done, PE.one(("pT", u)))
                if c < NC_:
                    pe.wait_ge(vec_done, V.done(("U", c), hp))
                    settle(pe, pe_passed)
                    for j in range(2):
                        nc.tensor.matmul(bank[5][rows[j], 0:C], Km[rows[j], c, :], Vm[rows[j], c, :], start=True, stop=False)
                    for j in range(2):
                        last = nc.tensor.matmul(bank[5][rows[j], 0:C], Bm[rows[j], c, :], Ut[rows[j], :], start=False, stop=True)
                    last.then_inc(pe_done, PE.one(("S", c)))
                    if c > 0:
                        pe.wait_ge(act_done, A.done(("Y", c - 1), hp))
                    settle(pe, pe_passed)
                    for j in range(2):
                        nc.tensor.matmul(bank[6][rows[j], 0:C], Vm[rows[j], c, :], M2[rows[j], c, C:P], start=True, stop=False)
                    for j in range(2):
                        last = nc.tensor.matmul(bank[6][rows[j], 0:C], Ut[rows[j], :], M1[rows[j], c, C:P], start=False, stop=c == 0)
                    if c > 0:
                        for j in range(2):
                            last = nc.tensor.matmul(bank[6][rows[j], 0:C], st_S[rows[j], c % 2, :], QR[rows[j], c, C:P], start=False, stop=True)
                    last.then_inc(pe_done, PE.one(("Y", c)))
                if c > 0:
                    u = c - 1
                    j, i, nk = unit(u)
                    pe.wait_ge(act_done, A.done(("pT5", u) if nk == 5 else ("pT", u), hp))
                    for t in range(nk):
                        kt = i + 1 - nk + t
                        last = nc.tensor.matmul(bank[7][rows[j], 0:P], vtm[:, kt, rows[j]], pT[:, t * P:(t + 1) * P], start=t == 0, stop=t == nk - 1)
                    last.then_inc(pe_done, PE.one(("out", u)))
                h, s = e_stage(c)
                if h is not None:
                    gn_pe(pe, hp, h, s)
            for s in range(ELEN):
                gn_pe(pe, hp, 1, s)

        def mix_act(act, hp):
            act.wait_ge(pe_done, PE.done(("gt", 1), hp, 1))
            act.dma_start(lup[:], e.lora_up[bass.ds(hp, 1)].rearrange("a p m -> p (a m)")).then_inc(lup_in, 16)
            act.dma_start(gup[:], e.gate_up2[bass.ds(hp, 1)].rearrange("a p g m -> p (a g) m")).then_inc(gup_in, 16)
            act.wait_ge(vec_done, V.done(("ttr", NU - 1), hp, 1))
            for j in range(2):
                act.dma_start(bias[:, j], e.bias_d[bass.ds(hp * 2 + j, 1)].rearrange("a p c -> p (a c)")).then_inc(bias_in[j], 16)
            for name, dst, b0 in (("aq", qT, 0), ("ak", kT, 2), ("av", vT, 0)):
                for h in halves:
                    act.wait_ge(pe_done, PE.done((name, h), hp))
                    if h == 1:
                        act.sem_inc(w_used, 1)
                    nc.scalar.activation(dst[:, hs[h]], bank[b0 + h], ACT.Copy, scale=0.125 if name == "aq" else 1.0).then_inc(act_done, A.one((name, h)))
            act.wait_ge(vec_done, V.done("pz1", hp))
            for n, (name, b0) in enumerate((("r", 2), ("k", 0), ("v", 2))):
                if n == 2:
                    act.wait_ge(vec_done, V.done(("z", "r"), hp))
                for h in halves:
                    act.wait_ge(pe_done, PE.done((name, h), hp))
                    if h == 1:
                        act.sem_inc(w_used, 1)
                    nc.scalar.activation(Pb[n % 2][:, 1 + h * HALF:1 + (h + 1) * HALF], bank[b0 + h], ACT.Copy).then_inc(act_done, A.one(("P", name, h)))
                    nc.scalar.activation(Tb[n % 2][:, hs[h]], bank[b0 + h], ACT.Copy, scale=param(OM_R + n)).then_inc(act_done, A.one(("T", name, h)))
            for h in halves:
                act.wait_ge(pe_done, PE.done(("dec", h), hp))
                nc.scalar.activation(sig[:, hs[h]], bank[4 + h], ACT.Sigmoid, bias=param(DEC_B)).then_inc(act_done, A.one(("sig", h)))
            for h in halves:
                act.wait_ge(pe_done, PE.done(("icl", h), hp))
                nc.scalar.activation(a_t[:, hs[h]], bank[6 + h], ACT.Sigmoid, bias=param(ICL_B)).then_inc(act_done, A.one(("a", h)))
            act.wait_ge(vec_done, V.done(("z", "v"), hp))
            nc.scalar.activation(sq, k_t[:], ACT.Square, scale=param(KNS)).then_inc(act_done, A.one("kksq"))
            act.wait_ge(vec_done, V.done("scan", hp))
            nc.scalar.activation(Linv, Ls, ACT.Exp, scale=EXP_HALF).then_inc(act_done, A.one("Linv"))
            nc.scalar.activation(Lam, Ls, ACT.Exp, scale=-EXP_HALF).then_inc(act_done, A.one("Lam"))
            act.wait_ge(vec_done, V.done("Lx", hp))
            nc.scalar.activation(Lamx, sig, ACT.Exp, scale=-EXP_HALF).then_inc(act_done, A.one("Lamx"))
            for h in halves:
                act.wait_ge(vec_done, V.done(("kkmax", h), hp))
                nc.scalar.activation(rs_kk[:, hs[h]], rs_kk[:, hs[h]], ACT.Sqrt).then_inc(act_done, A.one(("kksd", h)))
            for g in range(2):
                act.wait_ge(pe_done, PE.done(("avT", g), hp))
                nc.scalar.activation(vtm[:, 4 * g:4 * g + 4, :].rearrange("p i m -> p (i m)"), bank[6 + g], ACT.Copy).then_inc(act_done, A.one(("vtm", g)))
            act.wait_ge(vec_done, V.done("rk", hp))
            for g in range(G):
                for n, (name, dst) in enumerate((("Vm", Vm), ("Bm", Bm), ("Km", Km))):
                    act.wait_ge(pe_done, PE.done((name, g), hp))
                    nc.scalar.activation(dst[:, g * GC:(g + 1) * GC, :].rearrange("p c t -> p (c t)"), bank[2 + 3 * g + n], ACT.Copy).then_inc(act_done, A.one((name, g)))
            for m in LEVELS:
                for g in range(G):
                    gs = slice(g * GC, (g + 1) * GC)
                    if m != LEVELS[-1]:
                        act.wait_ge(pe_done, PE.done(("T", m, g), hp))
                        nc.scalar.activation(T[:, gs, :].rearrange("p c t -> p (c t)"), bank[3 * g + 1], ACT.Copy).then_inc(act_done, A.one(("T", m, g)))
                    act.wait_ge(pe_done, PE.done(("TT", m, g), hp))
                    nc.scalar.activation(TT[:, gs, :].rearrange("p c t -> p (c t)"), bank[3 * g + 2], ACT.Copy).then_inc(act_done, A.one(("TT", m, g)))
            for c in range(NC_ + 1):
                if c > 0:
                    u = c - 1
                    j, i, nk = unit(u)
                    act.wait_ge(pe_done, PE.done(("pT", u), hp))
                    n0 = min(nk, 4) * P
                    nc.scalar.activation(pT[:, 0:n0], bank[2][:, 0:n0], ACT.Copy).then_inc(act_done, A.one(("pT", u)))
                    if nk == 5:
                        nc.scalar.activation(pT[:, 4 * P:], bank[7][:, P:2 * P], ACT.Copy).then_inc(act_done, A.one(("pT5", u)))
                if c < NC_:
                    act.wait_ge(pe_done, PE.done(("Y", c), hp))
                    nc.scalar.activation(yT[:, c * C:(c + 1) * C], bank[6][:, 0:C], ACT.Copy).then_inc(act_done, A.one(("Y", c)))
                if c > 0:
                    act.wait_ge(pe_done, PE.done(("out", u), hp))
                    nc.scalar.activation(yb[rows[j], i * P:(i + 1) * P], bank[7][rows[j], 0:P], ACT.Copy).then_inc(act_done, A.one(("out", u)))
                if c < NC_:
                    act.wait_ge(vec_done, V.done(("nmx", c), hp))
                    nk = unit(c)[2]
                    nc.scalar.activation(pe_s[:, c % 2, 0:nk * P], pe_s[:, c % 2, 0:nk * P], ACT.Exp,
                                             bias=small[:, 2 + c % 2:3 + c % 2], accum_out=small[:, 4 + c % 2:5 + c % 2]).then_inc(act_done, A.one(("exp", c)))
                h, s = e_stage(c)
                if h is not None:
                    gn_act(act, hp, h, s)
            act.wait_ge(act_done, A.done(("out", NU - 1), hp))
            act.dma_start(e.yb_d[bass.ds(hp, 1)].rearrange("a p t -> p (a t)"), yb[:]).then_inc(yb_out, 16)
            for s in range(ELEN):
                gn_act(act, hp, 1, s)
            act.wait_ge(yb_out, hp * 16 + 16)
            act.wait_ge(ya_out, hp * 32 + 32)

        def mix_vec(vec, hp):

            tt = nc.vector.tensor_tensor
            ts = nc.vector.tensor_scalar
            stt = nc.vector.scalar_tensor_tensor
            nc.vector.tensor_copy(cur[:, 0:PP], e.par[:, bass.ds(hp * PP, PP)]).then_inc(vec_done, V.one("cur"))
            vec.wait_ge(vec_done, V.done("cur", hp))
            ts(cur[:, OM_R:OM_R + 3], cur[:, MIX_R:MIX_R + 3], -1.0, 1.0, ALU.mult, ALU.add).then_inc(vec_done, V.one("om"))
            vec.wait_ge(vec_done, V.done("om", hp))
            ts(cur[:, OM_KIS:OM_KIS + 1], param(KIS), -1.0, 1.0, ALU.mult, ALU.add).then_inc(vec_done, V.one("omk"))
            vec.wait_ge(vec_done, V.done("omk", hp))
            nc.vector.memset(Pb[0][:, 0:1], 0.0).then_inc(vec_done, V.one("pz0"))
            vec.wait_ge(vec_done, V.done("pz0", hp))
            nc.vector.memset(Pb[1][:, 0:1], 0.0).then_inc(vec_done, V.one("pz1"))
            vec.wait_ge(vec_done, V.done("pz1", hp))
            for j in range(2):
                vec.wait_ge(bias_in[j], hp * 16 + 16)
            nc.vector.memset(bias[0:C, :, BAND - C:], MASKED).then_inc(vec_done, V.one(("bmask", 0)))
            vec.wait_ge(vec_done, V.done(("bmask", 0), hp))
            nc.vector.memset(bias[C:P, :, 0:C], MASKED).then_inc(vec_done, V.one(("bmask", 1)))
            vec.wait_ge(vec_done, V.done(("bmask", 1), hp))
            for n, (name, dst) in enumerate((("r", r_t), ("k", k_t), ("v", v_t))):
                vec.wait_ge(act_done, A.done(("T", name, 1), hp))
                stt(out=dst[:], in0=Pb[n % 2][:, 0:SEQ], scalar=param(MIX_R + n), in1=Tb[n % 2], op0=ALU.mult, op1=ALU.add).then_inc(vec_done, V.one(("z", name)))
                vec.wait_ge(vec_done, V.done(("z", name), hp))
            vec.wait_ge(act_done, A.done(("sig", 1), hp))
            nc.vector.tensor_tensor_scan(Ls, rst[:], sig, 0.0, ALU.mult, ALU.add).then_inc(vec_done, V.one("scan"))
            vec.wait_ge(vec_done, V.done("scan", hp))
            tt(sig, Ls, sig, ALU.subtract).then_inc(vec_done, V.one("Lx"))
            vec.wait_ge(vec_done, V.done("Lx", hp))
            vec.wait_ge(act_done, A.done("Lam", hp))
            nc.vector.tensor_copy(lamC[:], Lam.rearrange("p (c t) -> p c t", t=C)[:, :, C - 1]).then_inc(vec_done, V.one("lamC"))
            vec.wait_ge(vec_done, V.done("lamC", hp))
            for h in halves:
                vec.wait_ge(pe_done, PE.done(("kkss", h), hp))
                ts(rs_kk[:, hs[h]], bank[4 + h], 1e-24, None, ALU.max).then_inc(vec_done, V.one(("kkmax", h)))
                vec.wait_ge(vec_done, V.done(("kkmax", h), hp))
            vec.wait_ge(act_done, A.done(("kksd", 1), hp))
            nc.vector.reciprocal(rs_kk, rs_kk).then_inc(vec_done, V.one("kkrs"))
            vec.wait_ge(vec_done, V.done("kkrs", hp))
            stt(out=kk_t[:], in0=k_t[:], scalar=param(KNS), in1=rs_kk, op0=ALU.mult, op1=ALU.mult).then_inc(vec_done, V.one("kk"))
            vec.wait_ge(vec_done, V.done("kk", hp))
            b_t = sq
            vec.wait_ge(act_done, A.done(("a", 1), hp))
            tt(b_t, kk_t[:], a_t[:], ALU.mult).then_inc(vec_done, V.one("b"))
            vec.wait_ge(vec_done, V.done("b", hp))
            by_chunk = lambda ap: ap.rearrange("p (c t) -> p c t", t=C)
            vec.wait_ge(act_done, A.done("Linv", hp))
            tt(BK[:, :, 0:C], by_chunk(b_t), by_chunk(Linv), ALU.mult).then_inc(vec_done, V.one("bt"))
            vec.wait_ge(vec_done, V.done("bt", hp))
            ts(a_t[:], a_t[:], param(KIS), param(OM_KIS), ALU.mult, ALU.add).then_inc(vec_done, V.one("am"))
            vec.wait_ge(vec_done, V.done("am", hp))
            tt(k_t[:], k_t[:], a_t[:], ALU.mult).then_inc(vec_done, V.one("kp"))
            vec.wait_ge(vec_done, V.done("kp", hp))
            tt(BK[:, :, C:P], by_chunk(k_t[:]), by_chunk(Linv), ALU.mult).then_inc(vec_done, V.one("kt"))
            vec.wait_ge(vec_done, V.done("kt", hp))
            vec.wait_ge(act_done, A.done("Lamx", hp))
            tt(QR[:, :, 0:C], by_chunk(kk_t[:]), by_chunk(Lamx), ALU.mult).then_inc(vec_done, V.one("kq"))
            vec.wait_ge(vec_done, V.done("kq", hp))
            tt(QR[:, :, C:P], by_chunk(r_t[:]), by_chunk(Lam), ALU.mult).then_inc(vec_done, V.one("rt"))
            vec.wait_ge(vec_done, V.done("rt", hp))
            stt(out=r_t[:], in0=r_t[:], scalar=param(BON), in1=k_t[:], op0=ALU.mult, op1=ALU.mult).then_inc(vec_done, V.one("rk"))
            vec.wait_ge(vec_done, V.done("rk", hp))
            mask4 = bc(mask2, 4)
            xb = {0: (0, 1, 2, 3, 4), 1: (5, 6, 7, 0, 1)}
            quad = lambda b: bank[b].rearrange("p (c t) -> p c t", t=2 * C)
            octo = lambda b: bank[b].rearrange("p (c t) -> p c t", t=C)
            for g in range(G):
                gs = slice(g * GC, (g + 1) * GC)
                for q in range(2):
                    vec.wait_ge(pe_done, PE.done(("X1", g, q), hp))
                    tt(M1[:, g * GC + 4 * q:g * GC + 4 * q + 4, :], quad(xb[g][q]), mask4, ALU.mult).then_inc(vec_done, V.one(("X1", g, q)))
                    vec.wait_ge(vec_done, V.done(("X1", g, q), hp))
                for q in range(2):
                    vec.wait_ge(pe_done, PE.done(("X2", g, q), hp))
                    tt(M2[:, g * GC + 4 * q:g * GC + 4 * q + 4, :], quad(xb[g][2 + q]), mask4, ALU.mult).then_inc(vec_done, V.one(("X2", g, q)))
                    vec.wait_ge(vec_done, V.done(("X2", g, q), hp))
                vec.wait_ge(pe_done, PE.done(("A", g), hp))
                tt(T[:, gs, :], octo(xb[g][4]), bc(e.consts[:, C_NL1:C_NL1 + C], GC), ALU.mult).then_inc(vec_done, V.one(("A", g)))
                vec.wait_ge(vec_done, V.done(("A", g), hp))
                tt(T[:, gs, :], T[:, gs, :], eye8, ALU.add).then_inc(vec_done, V.one(("T2", g)))
                vec.wait_ge(vec_done, V.done(("T2", g), hp))
                tt(TT[:, gs, :], M1[:, gs, 0:C], bc(e.consts[:, C_NL1T:C_NL1T + C], GC), ALU.mult).then_inc(vec_done, V.one(("T2T0", g)))
                vec.wait_ge(vec_done, V.done(("T2T0", g), hp))
                tt(TT[:, gs, :], TT[:, gs, :], eye8, ALU.add).then_inc(vec_done, V.one(("T2T", g)))
                vec.wait_ge(vec_done, V.done(("T2T", g), hp))
                tt(M1[:, gs, 0:C], M1[:, gs, 0:C], eye8, ALU.add).then_inc(vec_done, V.one(("ATI", g)))
                vec.wait_ge(vec_done, V.done(("ATI", g), hp))
            for m in LEVELS:
                for g in range(G):
                    vec.wait_ge(pe_done, PE.done(("X", m, g), hp))
                    tt(X[:, g * GC:(g + 1) * GC, :], octo(3 * g), level[m], ALU.mult).then_inc(vec_done, V.one(("X", m, g)))
                    vec.wait_ge(vec_done, V.done(("X", m, g), hp))
            for c in range(NC_ + 1):
                if c < NC_:
                    vec.wait_ge(pe_done, PE.done(("W", c), hp))
                    nc.vector.tensor_copy(Wt[:], bank[4][:, 0:C]).then_inc(vec_done, V.one(("W", c)))
                    vec.wait_ge(vec_done, V.done(("W", c), hp))
                    j, i, nk = unit(c)
                    vec.wait_ge(pe_done, PE.done(("sc", c), hp))
                    if c >= 2:
                        vec.wait_ge(pe_done, PE.done(("pT", c - 2), hp))
                    settle(vec, vec_passed)
                    nc.vector.tensor_tensor_reduce(out=pe_s[:, c % 2, 0:nk * P], in0=e.banks[:, 0:nk * P], in1=bias[:, j, BAND - nk * P:],
                                                       scale=1.0, scalar=-3e38, op0=ALU.add, op1=ALU.max, accum_out=small[:, 6 + c % 2:7 + c % 2]).then_inc(vec_done, V.one(("ttr", c)))
                    vec.wait_ge(vec_done, V.done(("ttr", c), hp))
                    ts(small[:, 2 + c % 2:3 + c % 2], small[:, 6 + c % 2:7 + c % 2], -1.0, None, ALU.mult).then_inc(vec_done, V.one(("nmx", c)))
                    vec.wait_ge(vec_done, V.done(("nmx", c), hp))
                    vec.wait_ge(pe_done, PE.done(("U", c), hp))
                    ts(Ut[:], bank[4][:, 0:C], -1.0, None, ALU.mult).then_inc(vec_done, V.one(("U", c)))
                    vec.wait_ge(vec_done, V.done(("U", c), hp))
                if c > 0:
                    u = c - 1
                    nk = unit(u)[2]
                    vec.wait_ge(act_done, A.done(("exp", u), hp))
                    nc.vector.reciprocal(small[:, u % 2:u % 2 + 1], small[:, 4 + u % 2:5 + u % 2]).then_inc(vec_done, V.one(("rin", u)))
                    vec.wait_ge(vec_done, V.done(("rin", u), hp))
                    ts(pe_s[:, u % 2, 0:nk * P], pe_s[:, u % 2, 0:nk * P], small[:, u % 2:u % 2 + 1], None, ALU.mult).then_inc(vec_done, V.one(("pn", u)))
                    vec.wait_ge(vec_done, V.done(("pn", u), hp))
                if c < NC_:
                    if c > 0:
                        ts(st_L[:], st_S[:, c % 2, :], lamC[:, c:c + 1], None, ALU.mult).then_inc(vec_done, V.one(("SL", c)))
                        vec.wait_ge(vec_done, V.done(("SL", c), hp))
                    vec.wait_ge(pe_done, PE.done(("S", c), hp))
                    if c == 0:
                        ts(st_S[:, 1, :], bank[5][:, 0:C], lamC[:, 0:1], None, ALU.mult).then_inc(vec_done, V.one(("S", 0)))
                        vec.wait_ge(vec_done, V.done(("S", 0), hp))
                    else:
                        stt(out=st_S[:, (c + 1) % 2, :], in0=bank[5][:, 0:C], scalar=lamC[:, c:c + 1], in1=st_L[:], op0=ALU.mult, op1=ALU.add).then_inc(vec_done, V.one(("S", c)))
                        vec.wait_ge(vec_done, V.done(("S", c), hp))
                h, s = e_stage(c)
                if h is not None:
                    gn_vec(vec, hp, h, s)
            for s in range(ELEN):
                gn_vec(vec, hp, 1, s)

        @block.tensor
        def _(pe):
            for n in range(3):
                pe.wait_ge(w_split, n + 1)
                for h in halves:
                    if n == 2:
                        pe.wait_ge(pro_act, LA.done(("pc", 0, h)))
                    last = gemm(nc, bank[(2 * n + h) % 4], e.whi[:, n % 2], e.wlo[:, n % 2], e.ahi, e.alo, range(KT), hs[h])
                    last.then_inc(pro_pe, LP.one(("l", n, h)))
            pe.sem_inc(pe_done, PE.n)
            pe.wait_ge(pro_act, LA.done(("sg", 1)))
            with pe.Fori(0, HP) as hp:
                mix_pe(pe, hp)
            LP.close()
            PE.close()

        @block.scalar
        def _(act):
            act.dma_start(rst[:], e.consts_d[:, C_RST:C_N]).then_inc(rst_in, 16)
            for n in range(3):
                for h in halves:
                    act.wait_ge(pro_pe, LP.done(("l", n, h)))
                    if h == 1:
                        act.sem_inc(w_used, 1)
                    if n == 0 and h == 0:
                        act.wait_ge(pro_vec, LV.done("zero1"))
                    if n == 2 and h == 0:
                        act.wait_ge(pro_vec, LV.done(("z", 0)))
                    nc.scalar.activation(Pb[n % 2][:, 1 + h * HALF:1 + (h + 1) * HALF], bank[(2 * n + h) % 4], ACT.Copy).then_inc(pro_act, LA.one(("pc", n, h)))
            act.wait_ge(pro_vec, LV.done(("z", 0)))
            nc.scalar.activation(lora[0:C, :], lora[0:C, :], ACT.Tanh).then_inc(pro_act, LA.one("tanh"))
            for n in range(2):
                act.wait_ge(pro_vec, LV.done(("z", n + 1)))
                nc.scalar.activation(sg[:, n, :], sg[:, n, :], ACT.Sigmoid).then_inc(pro_act, LA.one(("sg", n)))
            act.sem_inc(act_done, A.n)
            with act.Fori(0, HP) as hp:
                mix_act(act, hp)
            LA.close()
            A.close()

        @block.vector
        def _(vec):
            nc.vector.memset(Pb[0][:, 0:1], 0.0).then_inc(pro_vec, LV.one("zero0"))
            nc.vector.memset(Pb[1][:, 0:1], 0.0).then_inc(pro_vec, LV.one("zero1"))
            nc.vector.tensor_scalar(cur[:, 0:3], e.par[:, Q_LORA:Q_LORA + 3], -1.0, 1.0, ALU.mult, ALU.add).then_inc(pro_vec, LV.one("omm"))
            vec.wait_ge(pro_vec, LV.done("omm"))
            dst = [lora[:], sg[:, 0, :], sg[:, 1, :]]
            for n in range(3):
                vec.wait_ge(pro_act, LA.done(("pc", n, 1)))
                nc.vector.tensor_scalar(dst[n], Pb[n % 2][:, 1:1025], cur[:, n:n + 1], None, ALU.mult).then_inc(pro_vec, LV.one(("t", n)))
                vec.wait_ge(pro_vec, LV.done(("t", n)))
                nc.vector.scalar_tensor_tensor(out=dst[n], in0=Pb[n % 2][:, 0:1024], scalar=e.par[:, Q_LORA + n:Q_LORA + n + 1],
                                                   in1=dst[n], op0=ALU.mult, op1=ALU.add).then_inc(pro_vec, LV.one(("z", n)))
            vec.wait_ge(rst_in, 16)
            vec.wait_ge(pro_vec, LV.done(("z", 2)))
            vec.sem_inc(vec_done, V.n)
            with vec.Fori(0, HP) as hp:
                mix_vec(vec, hp)
            LV.close()
            V.close()


def merge_phase(e):
    nc = e.nc
    with ExitStack() as ctx:
        yhi = e.sb("y_hi", [P, KT, SEQ], F32R, ctx)
        ylo = e.sb("y_lo", [P, KT, SEQ], F32R, ctx)
        st = e.sb("y_stage", [P, 2, SEQ], ctx=ctx)
        sg = e.sb("gates", [P, 2, SEQ], ctx=ctx)
        w = weight_sems(e, e.ctx, "merge")
        w_split, w_used = w[1], w[2][0]
        y_in = sems(nc, e.ctx, "y_in0", "y_in1")
        (conv,) = sems(nc, e.ctx, "y_split")
        CV = Steps(conv, [(s, b, k) for b in range(2) for k in range(KT) for s in ("hi", "lo")])
        hs = [slice(0, HALF), slice(HALF, SEQ)]
        S = []
        for b in range(2):
            sa, sv, sp_ = sems(nc, e.ctx, f"merge_act{b}", f"merge_vec{b}", f"merge_pe{b}")
            S.append((Steps(sa, [("gate", k, h) for k in range(2) for h in range(2)], True),
                      Steps(sv, [(n, k, h) for k in range(2) for h in range(2) for n in (("m",) if b == 0 else ("m", "sum"))], True),
                      Steps(sp_, [(n, k, h) for k in range(2) for n in ("gate", "y") for h in range(2)], True)))
        rounds = KT // 2
        block = ctx.enter_context(nc.Block())
        start_weights(e, block, NB_GA, 4 * KT, w)

        @block.tensor
        def _(pe):
            for b in range(2):
                A, V, PE = S[b]
                pe.sem_inc(PE.sem, PE.n)
                with pe.Fori(0, rounds) as i:
                    for k in range(2):
                        pe.wait_ge(w_split, i * 4 + (4 * rounds * b + 2 * k + 1))
                        pe.wait_ge(A.sem, A.done(("gate", k, 1), i, 1))
                        for h in range(2):
                            gemm(nc, e.ps[4 * k + h], e.whi[:, 0], e.wlo[:, 0], e.ahi, e.alo, range(KT), hs[h]).then_inc(PE.sem, PE.one(("gate", k, h)))
                        pe.wait_ge(w_split, i * 4 + (4 * rounds * b + 2 * k + 2))
                        if k == 0:
                            pe.wait_ge(CV.sem, CV.done(("lo", b, KT - 1)))
                        pe.wait_ge(V.sem, V.done(("m", k, 1), i, 1))
                        for h in range(2):
                            gemm(nc, e.ps[4 * k + 2 + h], e.whi[:, 1], e.wlo[:, 1], yhi, ylo, range(KT), hs[h]).then_inc(PE.sem, PE.one(("y", k, h)))
                PE.close()
                if b == 0:
                    pe.wait_ge(V.sem, V.done(("m", 1, 1), rounds - 1))

        @block.scalar
        def _(act):
            for b in range(2):
                A, V, PE = S[b]
                act.sem_inc(A.sem, A.n)
                if b == 1:
                    act.wait_ge(S[0][2].sem, S[0][2].done(("y", 1, 1), rounds - 1))
                for k in range(KT):
                    if k >= 2 or b == 1:
                        act.wait_ge(CV.sem, CV.done(("lo", b if k >= 2 else 0, (k - 2) % KT)))
                    act.dma_start(st[:, k % 2], (e.ya_d, e.yb_d)[b][k]).then_inc(y_in[k % 2], 16)
                with act.Fori(0, rounds) as i:
                    for k in range(2):
                        act.wait_ge(V.sem, V.done(("m" if b == 0 else "sum", k, 1), i, 1))
                        for h in range(2):
                            act.wait_ge(PE.sem, PE.done(("gate", k, h), i))
                            if h == 1:
                                act.sem_inc(w_used, 1)
                            nc.scalar.activation(sg[:, k, hs[h]], e.ps[4 * k + h], ACT.Sigmoid).then_inc(A.sem, A.one(("gate", k, h)))
                        act.wait_ge(PE.sem, PE.done(("y", k, 1), i))
                        act.sem_inc(w_used, 1)
                A.close()

        @block.vector
        def _(vec):
            tt = nc.vector.tensor_tensor
            for b in range(2):
                A, V, PE = S[b]
                vec.sem_inc(V.sem, V.n)
                for k in range(KT):
                    vec.wait_ge(y_in[k % 2], 16 * (b * KT // 2 + k // 2 + 1))
                    nc.vector.tensor_copy(yhi[:, k], st[:, k % 2]).then_inc(conv, CV.one(("hi", b, k)))
                    vec.wait_ge(CV.sem, CV.done(("hi", b, k)))
                    tt(ylo[:, k], st[:, k % 2], yhi[:, k].bitcast(F32), ALU.subtract).then_inc(conv, CV.one(("lo", b, k)))
                with vec.Fori(0, rounds) as i:
                    for k in range(2):
                        for h in range(2):
                            m = e.mo[:, bass.ds(i * 2 + k, 1), hs[h]].rearrange("p a t -> p (a t)")
                            vec.wait_ge(A.sem, A.done(("gate", k, h), i))
                            vec.wait_ge(PE.sem, PE.done(("y", k, h), i))
                            if b == 0:
                                tt(m, e.ps[4 * k + 2 + h], sg[:, k, hs[h]], ALU.mult).then_inc(V.sem, V.one(("m", k, h)))
                            else:
                                tt(sg[:, k, hs[h]], e.ps[4 * k + 2 + h], sg[:, k, hs[h]], ALU.mult).then_inc(V.sem, V.one(("m", k, h)))
                                vec.wait_ge(V.sem, V.done(("m", k, h), i))
                                tt(m, m, sg[:, k, hs[h]], ALU.add).then_inc(V.sem, V.one(("sum", k, h)))
                V.close()


def project_phase(e, tag, first, per_block, split_first):
    nc = e.nc
    kts = KT // per_block
    nb = 2 * per_block
    rounds = KT // nb
    with ExitStack() as ctx:
        w = weight_sems(e, e.ctx, tag)
        w_split, w_used = w[1], w[2][0]
        sa, sv, sp_, hi_done, lo_done = sems(nc, e.ctx, f"{tag}_act", f"{tag}_vec", f"{tag}_pe", f"{tag}_hi", f"{tag}_lo")
        A = Steps(sa, [(n, h) for n in range(nb) for h in range(2)], True)
        PE = Steps(sp_, [(n, h) for n in range(nb) for h in range(2)], True)
        block = ctx.enter_context(nc.Block())
        start_weights(e, block, first, KT // per_block, w)
        hs = [slice(0, HALF), slice(HALF, SEQ)]

        @block.vector
        def _(vec):
            if split_first:
                for k in range(KT):
                    vec.wait_ge(hi_done, k + 1)
                    nc.vector.tensor_tensor(e.alo[:, k], e.mo[:, k], e.ahi[:, k].bitcast(F32), ALU.subtract).then_inc(lo_done, 1)

        @block.scalar
        def _(act):
            if split_first:
                for k in range(KT):
                    nc.scalar.activation(e.ahi[:, k], e.mo[:, k], ACT.Copy).then_inc(hi_done, 1)
                act.wait_ge(lo_done, KT)
            act.sem_inc(sa, A.n)
            with act.Fori(0, rounds) as i:
                for n in range(nb):
                    for h in range(2):
                        act.wait_ge(PE.sem, PE.done((n, h), i))
                        if h == 1 and n % per_block == per_block - 1:
                            act.sem_inc(w_used, 1)
                        dst = e.mo[:, bass.ds(i * nb + n, 1), hs[h]].rearrange("p a t -> p (a t)")
                        nc.scalar.activation(dst, e.ps[2 * n + h], ACT.Copy).then_inc(sa, A.one((n, h)))
            A.close()

        @block.tensor
        def _(pe):
            if split_first:
                pe.wait_ge(lo_done, KT)
            pe.sem_inc(sp_, PE.n)
            with pe.Fori(0, rounds) as i:
                for n in range(nb):
                    s, off = n // per_block, n % per_block * kts
                    pe.wait_ge(w_split, i * 2 + s + 1)
                    pe.wait_ge(A.sem, A.done((n, 1), i, 1))
                    for h in range(2):
                        gemm(nc, e.ps[2 * n + h], e.whi[:, s, off:off + kts], e.wlo[:, s, off:off + kts], e.ahi, e.alo, range(kts), hs[h]).then_inc(sp_, PE.one((n, h)))
            PE.close()


def finish_phase(e, tag, g_row, x_in, x_out, gain):
    nc = e.nc
    with ExitStack() as ctx:
        tok = e.sb(f"{tag}_tok", [P, NT, D], ctx=ctx)
        xr = e.sb(f"{tag}_x", [P, NT, D], ctx=ctx)
        junk = e.sb(f"{tag}_squares", [P, D], ctx=ctx)
        stage = e.sb(f"{tag}_stage", [P, 2, HALF], ctx=ctx)
        gpost = e.sb(f"{tag}_gain", [P, D], ctx=ctx)
        st = e.sb(f"{tag}_stats", [P, 32], ctx=ctx)
        sa, sv, sp_, g_in = sems(nc, e.ctx, f"{tag}_act", f"{tag}_vec", f"{tag}_pe", f"{tag}_g_in")
        x_ld, x_st = e.x_loaded, e.x_stored
        ld_value, st_value = 16 * (g_row + 2), 16 * (g_row + 1)
        na, nv, np_ = norm_steps("n", NT) if gain is not None else ([], [], [])
        A = Steps(sa, [(n, i) for i in range(NT) for n in ("cp0", "cp1", "psq")] + ["psd"] + na)
        V = Steps(sv, ["pms", "prs"] + [(n, i) for i in range(NT) for n in ("g", "res")] + nv)
        PE = Steps(sp_, [("tok", i) for i in range(NT)] + np_)
        block = ctx.enter_context(nc.Block())

        @block.sync
        def _(sp):
            sp.dma_start(gpost[:], bass.AP(tensor=e.g_rows.tensor, offset=g_row * D, ap=[[0, P], [1, D]])).then_inc(g_in, 16)
            for i in range(NT):
                sp.dma_start(xr[:, i], x_in[i * P:(i + 1) * P, :]).then_inc(x_ld[i], 16)
            for i in range(NT):
                sp.wait_ge(V.sem, V.done(("res", i)))
                sp.dma_start(x_out[i * P:(i + 1) * P, :], tok[:, i]).then_inc(x_st[i], 16)
            for i in range(NT):
                sp.wait_ge(x_st[i], st_value)

        @block.tensor
        def _(pe):
            for i in range(NT):
                if i >= 4:
                    pe.wait_ge(A.sem, A.done(("cp1", i - 4)))
                for kt in range(KT):
                    last = nc.tensor.transpose(e.ps[2 * (i % 4) + kt // 4][:, kt % 4 * P:(kt % 4 + 1) * P], e.mo[:, kt, i * P:(i + 1) * P], e.ident)
                last.then_inc(sp_, PE.one(("tok", i)))
            if gain is not None:
                pe.wait_ge(A.sem, A.done(("cp1", NT - 1)))
                norm_pe(e, pe, A, V, PE, "n", tok, NT)
            PE.close()

        @block.scalar
        def _(act):
            for i in range(NT):
                act.wait_ge(PE.sem, PE.done(("tok", i)))
                for h in range(2):
                    nc.scalar.activation(tok[:, i, h * HALF:(h + 1) * HALF], e.ps[2 * (i % 4) + h], ACT.Copy).then_inc(sa, A.one((f"cp{h}", i)))
                act.wait_ge(A.sem, A.done(("cp1", i)))
                nc.scalar.activation(junk[:], tok[:, i], ACT.Square, accum_out=st[:, 16 + i:17 + i]).then_inc(sa, A.one(("psq", i)))
            act.wait_ge(V.sem, V.done("pms"))
            nc.scalar.activation(st[:, 24:32], st[:, 16:24], ACT.Sqrt).then_inc(sa, A.one("psd"))
            if gain is not None:
                norm_act(e, act, A, V, PE, "n", tok, NT, st, junk[:], stage, gain, lambda eng, i: eng.wait_ge(V.sem, V.done(("res", i))))
            A.close()

        @block.vector
        def _(vec):
            vec.wait_ge(A.sem, A.done(("psq", NT - 1)))
            nc.vector.tensor_scalar(st[:, 16:24], st[:, 16:24], 1.0 / D, EPS, ALU.mult, ALU.add).then_inc(sv, V.one("pms"))
            vec.wait_ge(A.sem, A.done("psd"))
            nc.vector.reciprocal(st[:, 16:24], st[:, 24:32]).then_inc(sv, V.one("prs"))
            vec.wait_ge(g_in, 16)
            vec.wait_ge(V.sem, V.done("prs"))
            for i in range(NT):
                nc.vector.scalar_tensor_tensor(out=tok[:, i], in0=tok[:, i], scalar=st[:, 16 + i:17 + i], in1=gpost[:],
                                               op0=ALU.mult, op1=ALU.mult).then_inc(sv, V.one(("g", i)))
                vec.wait_ge(x_ld[i], ld_value)
                vec.wait_ge(V.sem, V.done(("g", i)))
                nc.vector.tensor_tensor(tok[:, i], tok[:, i], xr[:, i], ALU.add).then_inc(sv, V.one(("res", i)))
            if gain is not None:
                norm_vec(e, vec, A, V, "n", tok, NT, st, stage, e.ahi, e.alo, lambda eng, i: eng.wait_ge(x_st[i], st_value))
            V.close()


def cross_phase(e):
    nc = e.nc
    with ExitStack() as ctx:
        sb = lambda name, shape, dt=F32: e.sb(name, shape, dt, ctx)
        mt = sb("mem_tok", [P, 2, D])
        mhi = sb("mem_hi", [P, KT, MEM], F32R)
        mlo = sb("mem_lo", [P, KT, MEM], F32R)
        km = sb("mem_k", [P, MH, MEM])
        vmc = sb("mem_v_cm", [P, MH, MEM])
        vm = sb("mem_v_tok", [P, 2, MH * P])
        q = sb("cross_q", [P, MH, SEQ])
        o = sb("cross_o", [P, MH, SEQ])
        pr = sb("cross_probs", [P, 2, MEM])
        pT = sb("cross_probs_T", [P, 2, MEM])
        small = sb("cross_small", [P, 8])
        junk = sb("cross_squares", [P, D])
        stage = sb("cross_stage", [P, 2, HALF])
        st = sb("cross_stats", [P, 16])
        w = weight_sems(e, e.ctx, "cross")
        w_split, w_used = w[1], w[2][0]
        m_in = sems(nc, e.ctx, "mem_in0", "mem_in1")
        sa, sv, sp_ = sems(nc, e.ctx, "cross_act", "cross_vec", "cross_pe")
        na, nv, np_ = norm_steps("m", 2)
        NUC = MH * NT
        kv = [("kv", n) for n in range(8)]
        qs = [("q", n, h) for n in range(MH) for h in range(2)]
        a_names, v_names, p_names = na + kv + qs + ["vm0", "vm1"], list(nv), np_ + kv + qs + ["vm0", "vm1"]
        for u in range(NUC + 2):
            if u < NUC:
                p_names += [("s", u)]
                v_names += [("mx", u), ("nmx", u)]
                a_names += [("exp", u)]
            if 1 <= u <= NUC:
                v_names += [("rin", u - 1), ("pn", u - 1)]
                p_names += [("pT", u - 1)]
                a_names += [("pT", u - 1)]
            if u >= 2:
                p_names += [("out", u - 2)]
                a_names += [("out", u - 2)]
                if (u - 2) % NT == NT - 1:
                    v_names += [("hi", (u - 2) // NT), ("lo", (u - 2) // NT)]
        A, V, PE = Steps(sa, a_names), Steps(sv, v_names), Steps(sp_, p_names)
        hs = [slice(0, HALF), slice(HALF, SEQ)]
        block = ctx.enter_context(nc.Block())
        start_weights(e, block, NB_MEM, 8 + MH, w)

        @block.tensor
        def _(pe):
            norm_pe(e, pe, A, V, PE, "m", mt, 2)
            for n in range(8):
                pe.wait_ge(w_split, n + 1)
                if n == 0:
                    pe.wait_ge(V.sem, V.done(("m", "lo", KT - 1, 0)))
                if n >= 4:
                    pe.wait_ge(A.sem, A.done(("kv", n - 4)))
                gemm(nc, e.ps[4 + n % 4][:, 0:MEM], e.whi[:, n % 2], e.wlo[:, n % 2], mhi, mlo, range(KT), slice(0, MEM)).then_inc(sp_, PE.one(("kv", n)))
            for n in range(MH):
                pe.wait_ge(w_split, 8 + n + 1)
                pe.wait_ge(A.sem, A.done(("q", n - 2, 1))) if n >= 2 else pe.wait_ge(A.sem, A.done(("m", "scaled", KT - 1, 0)))
                for h in range(2):
                    gemm(nc, e.ps[2 * (n % 2) + h], e.whi[:, n % 2], e.wlo[:, n % 2], e.ahi, e.alo, range(KT), hs[h]).then_inc(sp_, PE.one(("q", n, h)))
            for g in range(2):
                pe.wait_ge(A.sem, A.done(("kv", 7)))
                for n in range(MH):
                    last = nc.tensor.transpose(e.ps[4 + g][:, n * P:(n + 1) * P], vmc[:, n, g * P:(g + 1) * P], e.ident)
                last.then_inc(sp_, PE.one(f"vm{g}"))
            for u in range(NUC + 2):
                if u < NUC:
                    hd, i = u // NT, u % NT
                    if u == 0:
                        pe.wait_ge(A.sem, A.done(("q", MH - 1, 1)))
                    if u >= 2:
                        pe.wait_ge(A.sem, A.done(("exp", u - 2)))
                    nc.tensor.matmul(e.ps[u % 2][:, 0:MEM], q[:, hd, i * P:(i + 1) * P], km[:, hd, :], start=True, stop=True).then_inc(sp_, PE.one(("s", u)))
                if 1 <= u <= NUC:
                    v = u - 1
                    pe.wait_ge(V.sem, V.done(("pn", v)))
                    if v >= 2:
                        pe.wait_ge(A.sem, A.done(("pT", v - 2)))
                    for t in range(2):
                        last = nc.tensor.transpose(e.ps[2 + v % 2][:, t * P:(t + 1) * P], pr[:, v % 2, t * P:(t + 1) * P], e.ident)
                    last.then_inc(sp_, PE.one(("pT", v)))
                if u >= 2:
                    v = u - 2
                    hd = v // NT
                    pe.wait_ge(A.sem, A.done(("pT", v)))
                    if v == 0:
                        pe.wait_ge(A.sem, A.done("vm1"))
                    if v >= 2:
                        pe.wait_ge(A.sem, A.done(("out", v - 2)))
                    for t in range(2):
                        last = nc.tensor.matmul(e.ps[4 + v % 2][:, 0:P], vm[:, t, hd * P:(hd + 1) * P], pT[:, v % 2, t * P:(t + 1) * P], start=t == 0, stop=t == 1)
                    last.then_inc(sp_, PE.one(("out", v)))
            PE.close()

        @block.scalar
        def _(act):
            for i in range(2):
                act.dma_start(mt[:, i], e.mem[i * P:(i + 1) * P, :]).then_inc(m_in[i], 16)
            norm_act(e, act, A, V, PE, "m", mt, 2, st, junk[:], stage, e.par[:, Q_MEM:Q_MEM + KT], lambda eng, i: eng.wait_ge(m_in[i], 16))
            for n in range(8):
                act.wait_ge(PE.sem, PE.done(("kv", n)))
                act.sem_inc(w_used, 1)
                dst = km[:, n] if n < 4 else vmc[:, n - 4]
                nc.scalar.activation(dst, e.ps[4 + n % 4][:, 0:MEM], ACT.Copy).then_inc(sa, A.one(("kv", n)))
            for n in range(MH):
                for h in range(2):
                    act.wait_ge(PE.sem, PE.done(("q", n, h)))
                    if h == 1:
                        act.sem_inc(w_used, 1)
                    nc.scalar.activation(q[:, n, hs[h]], e.ps[2 * (n % 2) + h], ACT.Copy, scale=float(P) ** -0.5).then_inc(sa, A.one(("q", n, h)))
            for g in range(2):
                act.wait_ge(PE.sem, PE.done(f"vm{g}"))
                nc.scalar.activation(vm[:, g], e.ps[4 + g], ACT.Copy).then_inc(sa, A.one(f"vm{g}"))
            for u in range(NUC + 2):
                if u < NUC:
                    act.wait_ge(V.sem, V.done(("nmx", u)))
                    if u >= 2:
                        act.wait_ge(PE.sem, PE.done(("pT", u - 2)))
                    nc.scalar.activation(pr[:, u % 2], e.ps[u % 2][:, 0:MEM], ACT.Exp, bias=small[:, u % 2:u % 2 + 1],
                                         accum_out=small[:, 2 + u % 2:3 + u % 2]).then_inc(sa, A.one(("exp", u)))
                if 1 <= u <= NUC:
                    v = u - 1
                    act.wait_ge(PE.sem, PE.done(("pT", v)))
                    if v >= 2:
                        act.wait_ge(PE.sem, PE.done(("out", v - 2)))
                    nc.scalar.activation(pT[:, v % 2], e.ps[2 + v % 2][:, 0:MEM], ACT.Copy).then_inc(sa, A.one(("pT", v)))
                if u >= 2:
                    v = u - 2
                    hd, i = v // NT, v % NT
                    act.wait_ge(PE.sem, PE.done(("out", v)))
                    nc.scalar.activation(o[:, hd, i * P:(i + 1) * P], e.ps[4 + v % 2][:, 0:P], ACT.Copy).then_inc(sa, A.one(("out", v)))
            A.close()

        @block.vector
        def _(vec):
            norm_vec(e, vec, A, V, "m", mt, 2, st, stage, mhi, mlo)
            for u in range(NUC + 2):
                if u < NUC:
                    vec.wait_ge(PE.sem, PE.done(("s", u)))
                    nc.vector.reduce_max(small[:, 4 + u % 2:5 + u % 2], e.ps[u % 2][:, 0:MEM], mybir.AxisListType.X).then_inc(sv, V.one(("mx", u)))
                    vec.wait_ge(V.sem, V.done(("mx", u)))
                    if u >= 2:
                        vec.wait_ge(A.sem, A.done(("exp", u - 2)))
                    nc.vector.tensor_scalar(small[:, u % 2:u % 2 + 1], small[:, 4 + u % 2:5 + u % 2], -1.0, None, ALU.mult).then_inc(sv, V.one(("nmx", u)))
                if 1 <= u <= NUC:
                    v = u - 1
                    vec.wait_ge(A.sem, A.done(("exp", v)))
                    nc.vector.reciprocal(small[:, 6 + v % 2:7 + v % 2], small[:, 2 + v % 2:3 + v % 2]).then_inc(sv, V.one(("rin", v)))
                    vec.wait_ge(V.sem, V.done(("rin", v)))
                    nc.vector.tensor_scalar(pr[:, v % 2], pr[:, v % 2], small[:, 6 + v % 2:7 + v % 2], None, ALU.mult).then_inc(sv, V.one(("pn", v)))
                if u >= 2 and (u - 2) % NT == NT - 1:
                    hd = (u - 2) // NT
                    vec.wait_ge(A.sem, A.done(("out", u - 2)))
                    nc.vector.tensor_copy(e.ahi[:, hd], o[:, hd]).then_inc(sv, V.one(("hi", hd)))
                    vec.wait_ge(V.sem, V.done(("hi", hd)))
                    nc.vector.tensor_tensor(e.alo[:, hd], o[:, hd], e.ahi[:, hd].bitcast(F32), ALU.subtract).then_inc(sv, V.one(("lo", hd)))
            V.close()


def ffn_phase(e):
    nc = e.nc
    with ExitStack() as ctx:
        ghi = e.sb("hidden_hi", [P, KT, SEQ], F32R, ctx)
        glo = e.sb("hidden_lo", [P, KT, SEQ], F32R, ctx)
        sg = e.sb("silu", [P, 2, SEQ], ctx=ctx)
        w = weight_sems(e, e.ctx, "ffn")
        w_split, w_used = w[1], w[2][0]
        hs = [slice(0, HALF), slice(HALF, SEQ)]
        S = []
        for n in range(len(FGROUPS)):
            s = sems(nc, e.ctx, *[f"ffn_{x}{n}" for x in ("in_act", "in_vec", "in_pe", "out_vec", "out_pe")])
            kh = [(k, h) for k in range(2) for h in range(2)]
            S.append((Steps(s[0], [("silu",) + x for x in kh], True),
                      Steps(s[1], [(m,) + x for x in kh for m in ("prod", "hi", "lo")], True),
                      Steps(s[2], [(m, k, h) for k in range(2) for m in ("gate", "up") for h in range(2)], True),
                      Steps(s[3], [("acc",) + x for x in kh], True),
                      Steps(s[4], [("out",) + x for x in kh], True)))
        block = ctx.enter_context(nc.Block())
        start_weights(e, block, NB_FFN, 2 * FT + KT * len(FGROUPS), w)

        @block.tensor
        def _(pe):
            at = 0
            for n, (f0, nf) in enumerate(FGROUPS):
                A, V, PE, OV, OPE = S[n]
                pe.sem_inc(PE.sem, PE.n)
                with pe.Fori(0, nf // 2) as i:
                    for k in range(2):
                        for m, name in enumerate(("gate", "up")):
                            pe.wait_ge(w_split, i * 4 + (at + 2 * k + m + 1))
                            pe.wait_ge(A.sem, A.done(("silu", k, 1), i, 1)) if m == 0 else pe.wait_ge(V.sem, V.done(("prod", k, 1), i, 1))
                            for h in range(2):
                                gemm(nc, e.ps[4 * k + 2 * m + h], e.whi[:, m], e.wlo[:, m], e.ahi, e.alo, range(KT), hs[h]).then_inc(PE.sem, PE.one((name, k, h)))
                PE.close()
                at += 2 * nf
                pe.wait_ge(V.sem, V.done(("lo", 1, 1), nf // 2 - 1))
                pe.sem_inc(OPE.sem, OPE.n)
                with pe.Fori(0, KT // 2) as i:
                    for k in range(2):
                        pe.wait_ge(w_split, i * 2 + (at + k + 1))
                        pe.wait_ge(OV.sem, OV.done(("acc", k, 1), i, 1))
                        for h in range(2):
                            gemm(nc, e.ps[2 * k + h], e.whi[:, k], e.wlo[:, k], ghi, glo, range(nf), hs[h]).then_inc(OPE.sem, OPE.one(("out", k, h)))
                OPE.close()
                at += KT
                pe.wait_ge(OV.sem, OV.done(("acc", 1, 1), KT // 2 - 1))

        @block.scalar
        def _(act):
            for n, (f0, nf) in enumerate(FGROUPS):
                A, V, PE, OV, OPE = S[n]
                act.sem_inc(A.sem, A.n)
                with act.Fori(0, nf // 2) as i:
                    for k in range(2):
                        act.wait_ge(V.sem, V.done(("lo", k, 1), i, 1))
                        for h in range(2):
                            act.wait_ge(PE.sem, PE.done(("gate", k, h), i))
                            if h == 1:
                                act.sem_inc(w_used, 1)
                            nc.scalar.activation(sg[:, k, hs[h]], e.ps[4 * k + h], ACT.Silu).then_inc(A.sem, A.one(("silu", k, h)))
                        act.wait_ge(PE.sem, PE.done(("up", k, 1), i))
                        act.sem_inc(w_used, 1)
                A.close()
                with act.Fori(0, KT // 2) as i:
                    for k in range(2):
                        act.wait_ge(OPE.sem, OPE.done(("out", k, 1), i))
                        act.sem_inc(w_used, 1)

        @block.vector
        def _(vec):
            tt = nc.vector.tensor_tensor
            for n, (f0, nf) in enumerate(FGROUPS):
                A, V, PE, OV, OPE = S[n]
                vec.sem_inc(V.sem, V.n)
                vec.sem_inc(OV.sem, OV.n)
                if n > 0:
                    vec.wait_ge(S[n - 1][4].sem, S[n - 1][4].done(("out", 1, 1), KT // 2 - 1))
                with vec.Fori(0, nf // 2) as i:
                    for k in range(2):
                        for h in range(2):
                            vec.wait_ge(A.sem, A.done(("silu", k, h), i))
                            vec.wait_ge(PE.sem, PE.done(("up", k, h), i))
                            g = sg[:, k, hs[h]]
                            hi, lo = (t[:, bass.ds(i * 2 + k, 1), hs[h]].rearrange("p a t -> p (a t)") for t in (ghi, glo))
                            tt(g, e.ps[4 * k + 2 + h], g, ALU.mult).then_inc(V.sem, V.one(("prod", k, h)))
                            vec.wait_ge(V.sem, V.done(("prod", k, h), i))
                            nc.vector.tensor_copy(hi, g).then_inc(V.sem, V.one(("hi", k, h)))
                            vec.wait_ge(V.sem, V.done(("hi", k, h), i))
                            tt(lo, g, hi.bitcast(F32), ALU.subtract).then_inc(V.sem, V.one(("lo", k, h)))
                V.close()
                with vec.Fori(0, KT // 2) as i:
                    for k in range(2):
                        for h in range(2):
                            m = e.mo[:, bass.ds(i * 2 + k, 1), hs[h]].rearrange("p a t -> p (a t)")
                            vec.wait_ge(OPE.sem, OPE.done(("out", k, h), i))
                            if n == 0:
                                nc.vector.tensor_copy(m, e.ps[2 * k + h]).then_inc(OV.sem, OV.one(("acc", k, h)))
                            else:
                                tt(m, e.ps[2 * k + h], m, ALU.add).then_inc(OV.sem, OV.one(("acc", k, h)))
                OV.close()


def blocks_of(np, w):
    k, n = w.shape
    return w.reshape(k // P, P, n // P, P).transpose(2, 1, 0, 3)


def lay_out(np, i):
    a = {k: np.ascontiguousarray(v[0]) if k not in ("x", "mem") else v[0] for k, v in i.items()}
    win = a["w_in"]
    w = RWKV = 1024
    col = lambda s, n: blocks_of(np, win[:, s:s + n])
    r, k, v = (col(w * n, w) for n in range(3))
    lora = np.zeros((D, 3 * P), win.dtype)
    lora[:, 0:288] = win[:, 3072:3360]
    aq, ak, av, ga, gb = (col(3360 + w * n, w) for n in range(5))
    heads = np.stack([aq, ak, av, r, k, v], 1).reshape(6 * HP, P, KT, P)
    pair = lambda g, y: np.stack([g, blocks_of(np, y)], 1).reshape(2 * KT, P, KT, P)
    wo = blocks_of(np, a["w_o_mem"])
    wo = wo.reshape(4, 2, P, MH, P).transpose(0, 2, 1, 3, 4).reshape(4, P, KT, P)
    gate = blocks_of(np, a["w_ffn_in"][:, :FFN])
    up = blocks_of(np, a["w_ffn_in"][:, FFN:])
    down = blocks_of(np, a["w_ffn_out"])
    ffn = []
    for f0, nf in FGROUPS:
        ffn.append(np.stack([gate[f0:f0 + nf], up[f0:f0 + nf]], 1).reshape(2 * nf, P, KT, P))
        d = np.zeros((KT, P, KT, P), win.dtype)
        d[:, :, :nf] = down[:, :, f0:f0 + nf]
        ffn.append(d)
    wblocks = np.concatenate([blocks_of(np, lora), heads, pair(ga, a["w_branch_a"]), pair(gb, a["w_branch_b"]),
                              blocks_of(np, a["w_out"]), blocks_of(np, a["w_kv_mem"]), blocks_of(np, a["w_q_mem"]), wo] + ffn)
    lora_up = np.concatenate([a["decay_up"], a["iclr_up"]]).reshape(P, HP, P).transpose(1, 0, 2)
    gu = np.zeros((2, P, w), win.dtype)
    gu[0], gu[1, :32] = a["gate_up"][:P], a["gate_up"][P:]
    gate_up2 = gu.reshape(2, P, HP, P).transpose(2, 1, 0, 3)
    sm = a["shift_mix"]
    rows = np.stack([sm[0:w], sm[w:2 * w], sm[2 * w:3 * w], a["decay_base"], a["iclr_base"], a["key_norm_scale"],
                     a["key_iclr_scale"], a["bonus_scale"].reshape(-1), a["lnx_w"], a["lnx_b"]])
    par = np.zeros((P, Q_N), win.dtype)
    par[:, :Q_PRE] = rows.reshape(PP, HP, P).transpose(2, 1, 0).reshape(P, HP * PP)
    for at, name in ((Q_PRE, "g_pre_mix"), (Q_CROSS, "g_pre_cross"), (Q_FFN, "g_pre_ffn"), (Q_MEM, "g_mem")):
        par[:, at:at + KT] = a[name].reshape(KT, P).T
    par[:, Q_LORA] = sm[3072:3200]
    par[:, Q_LORA + 1] = sm[3200:3328]
    par[:32, Q_LORA + 2] = sm[3328:3360]
    return {
        "x": a["x"], "mem": a["mem"], "wblocks": wblocks, "lora_up": lora_up, "gate_up2": gate_up2, "params": par,
        "consts": constants(np), "rel_rev": a["rel_bias"][:, ::-1],
        "g_rows": np.stack([a["g_post_mix"], a["g_post_cross"], a["g_post_ffn"]]),
    }


def constants(np):
    c = np.zeros((P, C_N), np.float32)
    s, t = np.arange(P)[:, None] % C, np.arange(C)[None, :]
    c[:, C_ID:C_ID + P] = np.eye(P)
    c[:, C_MASK:C_MASK + C] = s < t
    c[:, C_MASK + C:C_MASK + P] = s <= t
    c[:, C_EYE:C_EYE + C] = s == t
    lower = lambda row, colm, m: (row // (2 * m) == colm // (2 * m)) & (row // m % 2 == 1) & (colm // m % 2 == 0)
    c[:, C_NL1:C_NL1 + C] = -1.0 * lower(s, t, 1)
    c[:, C_NL1T:C_NL1T + C] = -1.0 * lower(t, s, 1)
    for n, m in enumerate(LEVELS):
        c[:, C_LV + C * n:C_LV + C * (n + 1)] = 1.0 * (s == t) - lower(s, t, m)
    c[:, C_ONES:C_ONES + P] = np.arange(P)[:, None] // C == np.arange(P)[None, :] // C
    c[:, C_RST:C_RST + SEQ] = np.arange(SEQ)[None, :] % C != 0
    return c


def kernel(**inputs):
    import numpy as np
    from concourse import bacc
    from concourse.bass_utils import run_bass_kernel_spmd

    laid = lay_out(np, {k: np.asarray(v) for k, v in inputs.items()})
    nc = bacc.Bacc("TRN2", target_bir_lowering=False, num_devices=1)
    arrays, args = {}, []
    for name, a in laid.items():
        arrays[f"in_{name}"] = np.ascontiguousarray(a)
        args.append(nc.dram_tensor(f"in_{name}", a.shape, mybir.dt.from_np(a.dtype), kind="ExternalInput").ap())
    out = nc.dram_tensor("out", (SEQ, D), F32, kind="ExternalOutput").ap()
    hybrid_block(nc, *args, out)
    r = run_bass_kernel_spmd(nc, [arrays], core_ids=[0])
    return r.results[0]["out"].reshape(1, SEQ, D)
```

```python
from contextlib import ExitStack

import concourse.bass as bass
from concourse import mybir

P = 128
D = 1024
SEQ = 1024
KT = D // P
NT = SEQ // P
HALF = 512
HP = 8
C = 64
NC_ = SEQ // C
G = 2
GC = NC_ // G
MEM = 256
MH = 4
FFN = 2816
FT = FFN // P
FGROUPS = [(0, 8), (8, 8), (16, 6)]
BANDT = 5
BAND = BANDT * P
EXT = 768
PP = 10
EXP_HALF = 0.6065306597126334
LEVELS = [2, 4, 8, 16, 32]
EPS = 1e-6
SCAN = 4 * C
GN_EPS = 64e-5
MASKED = -1e30

F32 = mybir.dt.float32
F32R = mybir.dt.float32r
ALU = mybir.AluOpType
ACT = mybir.ActivationFunctionType

C_ID = 0
C_MASK = C_ID + P
C_EYE = C_MASK + P
C_NL1 = C_EYE + C
C_NL1T = C_NL1 + C
C_LV = C_NL1T + C
C_ONES = C_LV + C * len(LEVELS)
C_RST = C_ONES + P
C_N = C_RST + SCAN

(MIX_R, MIX_K, MIX_V, DEC_B, ICL_B, KNS, KIS, BON, LNW, LNB) = range(PP)
Q_PRE = HP * PP
Q_CROSS = Q_PRE + KT
Q_FFN = Q_CROSS + KT
Q_MEM = Q_FFN + KT
Q_LORA = Q_MEM + KT
Q_N = Q_LORA + 3
OM_R, OM_K, OM_V, OM_KIS = PP, PP + 1, PP + 2, PP + 3

NB_LORA = 0
NB_HEAD = 3
NB_GA = NB_HEAD + 2 + 6 * HP
NB_GB = NB_GA + 2 * KT
NB_OUT = NB_GB + 2 * KT
NB_MEM = NB_OUT + KT
NB_Q = NB_MEM + 8
NB_O = NB_Q + MH
NB_FFN = NB_O + 4
NB_N = NB_FFN + 2 * FT + 8 * len(FGROUPS)


class Steps:

    def __init__(self, sem, names, looped=False):
        self.sem, self.n, self.looped = sem, len(names), looped
        self.index = {name: i + 1 for i, name in enumerate(names)}
        assert len(self.index) == self.n
        self.at = 0

    def done(self, name, rnd=0, back=0):
        return (rnd + 1 - back) * self.n + self.index[name] if self.looped else self.index[name]

    def one(self, name):
        self.at += 1
        assert self.index[name] == self.at, (name, self.at)
        return 1

    def close(self):
        assert self.at == self.n, (self.at, self.n)


def settle(eng, passed):
    eng.sem_inc(passed, 1)


def weight_stream(nc, block, wblocks, first, count, raw, whi, wlo, loaded, split, used):
    assert count >= 4

    @block.sync
    def _(sp):
        for s in range(2):
            sp.dma_start(raw[:, s], wblocks[first + s]).then_inc(loaded[s], 16)
        with sp.Fori(1, count // 2) as i:
            for s in range(2):
                sp.wait_ge(split, i * 2 + s - 1)
                sp.dma_start(raw[:, s], wblocks[bass.ds(i * 2 + (s + first), 1)].rearrange("a p k m -> p (a k) m")).then_inc(loaded[s], 16)
        if count % 2:
            sp.wait_ge(split, count - 2)
            sp.dma_start(raw[:, 0], wblocks[first + count - 1]).then_inc(loaded[0], 16)

    @block.gpsimd
    def _(pool):
        def one(s, i):
            pool.wait_ge(loaded[s], i * 16 + 16)
            settle(pool, passed)
            pool.tensor_copy(whi[:, s], raw[:, s]).then_inc(split_hi, 1)
            pool.wait_ge(split_hi, i * 2 + s + 1)
            pool.tensor_tensor(wlo[:, s], raw[:, s], whi[:, s].bitcast(F32), ALU.subtract).then_inc(split, 1)

        split_hi, passed = used[1:]
        for s in range(2):
            one(s, 0)
        with pool.Fori(1, count // 2) as i:
            for s in range(2):
                pool.wait_ge(used[0], i * 2 + s - 1)
                one(s, i)
        if count % 2:
            pool.wait_ge(used[0], count - 2)
            one(0, count // 2)


def mm3(nc, out, whi, wlo, ahi, alo, start, stop):
    nc.tensor.matmul(out, whi, ahi, start=start, stop=False)
    nc.tensor.matmul(out, whi, alo, start=False, stop=False)
    return nc.tensor.matmul(out, wlo, ahi, start=False, stop=stop)


def gemm(nc, out, whi, wlo, ahi, alo, kts, cols):
    last = None
    for n, kt in enumerate(kts):
        last = mm3(nc, out, whi[:, n], wlo[:, n], ahi[:, kt, cols], alo[:, kt, cols], n == 0, n == len(kts) - 1)
    return last


def hybrid_block(nc, x, mem, wblocks, lora_up, gate_up2, params, consts, rel_rev, g_rows, out):
    ctx = ExitStack()
    with ctx:
        env = Env(nc, ctx)
        e = env
        e.x, e.mem, e.wblocks, e.lora_up, e.gate_up2 = x, mem, wblocks, lora_up, gate_up2
        e.params_d, e.consts_d, e.rel_rev, e.g_rows, e.out = params, consts, rel_rev, g_rows, out
        dram = lambda name, shape: nc.dram_tensor(name, shape, F32, kind="Internal").ap()
        e.ya_d = dram("ya_scratch", (HP, P, SEQ))
        e.yb_d = dram("yb_scratch", (HP, P, SEQ))
        e.ext_d = dram("ext_scratch", (2 * HP, EXT))
        e.bias_d = dram("bias_scratch", (2 * HP, P, BAND))
        e.x1_d = dram("x1_scratch", (SEQ, D))
        e.x2_d = dram("x2_scratch", (SEQ, D))
        e.consts = e.sb("consts", [P, C_N])
        e.par = e.sb("par", [P, Q_N])
        e.ahi = e.sb("act_hi", [P, KT, SEQ], F32R)
        e.alo = e.sb("act_lo", [P, KT, SEQ], F32R)
        e.raw = e.sb("w_raw", [P, 2, KT, P])
        e.whi = e.sb("w_hi", [P, 2, KT, P], F32R)
        e.wlo = e.sb("w_lo", [P, 2, KT, P], F32R)
        psum = ctx.enter_context(nc.psum_tensor("banks", [P, 8 * HALF], F32))
        e.banks = psum
        e.ps = [psum[:, b * HALF:(b + 1) * HALF] for b in range(8)]
        e.x_loaded = sems(nc, ctx, *[f"x_loaded{i}" for i in range(NT)])
        e.x_stored = sems(nc, ctx, *[f"x_stored{i}" for i in range(NT)])
        e.ident = e.consts[:, C_ID:C_ID + P]
        norm_phase(e)
        mix_phase(e)
        e.mo = e.sb("mixed", [P, KT, SEQ])
        merge_phase(e)
        project_phase(e, "out", NB_OUT, 1, True)
        finish_phase(e, "mixfin", 0, e.x, e.x1_d, e.par[:, Q_CROSS:Q_CROSS + KT])
        cross_phase(e)
        project_phase(e, "cross_o", NB_O, 2, False)
        finish_phase(e, "crossfin", 1, e.x1_d, e.x2_d, e.par[:, Q_FFN:Q_FFN + KT])
        ffn_phase(e)
        finish_phase(e, "ffnfin", 2, e.x2_d, e.out, None)


class Env:

    def __init__(self, nc, ctx):
        self.nc, self.ctx = nc, ctx

    def sb(self, name, shape, dt=F32, ctx=None):
        return (ctx or self.ctx).enter_context(self.nc.sbuf_tensor(name, shape, dt))


def sems(nc, ctx, *names):
    return [ctx.enter_context(nc.semaphore(n)) for n in names]


def weight_sems(e, ctx, tag):
    nc = e.nc
    loaded = sems(nc, ctx, f"{tag}_w_loaded0", f"{tag}_w_loaded1")
    split, used, split_hi, passed = sems(nc, ctx, f"{tag}_w_split", f"{tag}_w_used", f"{tag}_w_split_hi", f"{tag}_pool_passed")
    return loaded, split, (used, split_hi, passed)


def start_weights(e, block, first, count, w):
    weight_stream(e.nc, block, e.wblocks, first, count, e.raw, e.whi, e.wlo, w[0], w[1], w[2])


def norm_steps(tag, tiles):
    halves = range(max(1, tiles // 4))
    act = [(tag, "sq", i) for i in range(tiles)] + [(tag, "sd")]
    act += [(tag, "scaled", kt, h) for kt in range(KT) for h in halves]
    vec = [(tag, "ms"), (tag, "rs")] + [(tag, "xn", i) for i in range(tiles)]
    vec += [(tag, s, kt, h) for kt in range(KT) for h in halves for s in ("hi", "lo")]
    pe = [(tag, "T", kt, h) for kt in range(KT) for h in halves]
    return act, vec, pe


def norm_act(e, act, A, V, PE, tag, xb, tiles, st, junk, stage, gain, loaded, first=True):
    nc, width = e.nc, min(4, tiles) * P
    if first:
        for i in range(tiles):
            loaded(act, i)
            if i:
                act.wait_ge(A.sem, A.done((tag, "sq", i - 1)))
            nc.scalar.activation(junk, xb[:, i], ACT.Square, accum_out=st[:, i:i + 1]).then_inc(A.sem, A.one((tag, "sq", i)))
    act.wait_ge(V.sem, V.done((tag, "ms")))
    nc.scalar.activation(st[:, 8:8 + tiles], st[:, 0:tiles], ACT.Sqrt).then_inc(A.sem, A.one((tag, "sd")))
    halves = max(1, tiles // 4)
    for kt in range(KT):
        for h in range(halves):
            n = kt * halves + h
            act.wait_ge(PE.sem, PE.done((tag, "T", kt, h)))
            if n >= 2:
                act.wait_ge(V.sem, V.done((tag, "lo", (n - 2) // halves, (n - 2) % halves)))
            nc.scalar.activation(stage[:, n % 2, 0:width], e.ps[n % 4][:, 0:width], ACT.Copy,
                                 scale=gain[:, kt:kt + 1]).then_inc(A.sem, A.one((tag, "scaled", kt, h)))


def norm_vec(e, vec, A, V, tag, xb, tiles, st, stage, hi, lo, stored=None):
    nc, width = e.nc, min(4, tiles) * P
    vec.wait_ge(A.sem, A.done((tag, "sq", tiles - 1)))
    nc.vector.tensor_scalar(st[:, 0:tiles], st[:, 0:tiles], 1.0 / D, EPS, ALU.mult, ALU.add).then_inc(V.sem, V.one((tag, "ms")))
    vec.wait_ge(A.sem, A.done((tag, "sd")))
    nc.vector.reciprocal(st[:, 0:tiles], st[:, 8:8 + tiles]).then_inc(V.sem, V.one((tag, "rs")))
    vec.wait_ge(V.sem, V.done((tag, "rs")))
    for i in range(tiles):
        if stored:
            stored(vec, i)
        nc.vector.tensor_scalar(xb[:, i], xb[:, i], st[:, i:i + 1], None, ALU.mult).then_inc(V.sem, V.one((tag, "xn", i)))
    halves = max(1, tiles // 4)
    for kt in range(KT):
        for h in range(halves):
            n = kt * halves + h
            cols = slice(h * HALF, h * HALF + width)
            vec.wait_ge(A.sem, A.done((tag, "scaled", kt, h)))
            nc.vector.tensor_copy(hi[:, kt, cols], stage[:, n % 2, 0:width]).then_inc(V.sem, V.one((tag, "hi", kt, h)))
            vec.wait_ge(V.sem, V.done((tag, "hi", kt, h)))
            nc.vector.tensor_tensor(lo[:, kt, cols], stage[:, n % 2, 0:width], hi[:, kt, cols].bitcast(F32),
                                    ALU.subtract).then_inc(V.sem, V.one((tag, "lo", kt, h)))


def norm_pe(e, pe, A, V, PE, tag, xb, tiles):
    nc = e.nc
    halves = max(1, tiles // 4)
    for kt in range(KT):
        for h in range(halves):
            n = kt * halves + h
            if kt == 0:
                pe.wait_ge(V.sem, V.done((tag, "xn", min(4 * h + 3, tiles - 1))))
            if n >= 4:
                pe.wait_ge(A.sem, A.done((tag, "scaled", (n - 4) // halves, (n - 4) % halves)))
            for i in range(min(4, tiles)):
                last = nc.tensor.transpose(e.ps[n % 4][:, i * P:(i + 1) * P], xb[:, 4 * h + i, kt * P:(kt + 1) * P], e.ident)
            last.then_inc(PE.sem, PE.one((tag, "T", kt, h)))


def norm_phase(e):
    nc = e.nc
    with ExitStack() as ctx:
        xb = e.sb("x_tok", [P, NT, D], ctx=ctx)
        junk = e.sb("squares", [P, D], ctx=ctx)
        stage = e.sb("stage", [P, 2, HALF], ctx=ctx)
        st = e.sb("stats", [P, 16], ctx=ctx)
        ext = e.sb("ext", [2 * HP, EXT], ctx=ctx)
        x_in = e.x_loaded
        const_in, par_in, rel_in, ext_out, bias_out = sems(nc, e.ctx, "const_in", "par_in", "rel_in", "ext_out", "bias_out")
        a_s, v_s, p_s = sems(nc, e.ctx, "norm_act", "norm_vec", "norm_pe")
        na, nv, np_ = norm_steps("x", NT)
        A, V, PE = Steps(a_s, na), Steps(v_s, [("ext", 0), ("ext", 1)] + nv), Steps(p_s, np_)
        block = ctx.enter_context(nc.Block())

        @block.sync
        def _(sp):
            for i in range(NT):
                sp.dma_start(xb[:, i], e.x[i * P:(i + 1) * P, :]).then_inc(x_in[i], 16)
            sp.dma_start(e.consts[:], e.consts_d).then_inc(const_in, 16)
            sp.dma_start(e.par[:], e.params_d).then_inc(par_in, 16)
            sp.dma_start(ext[:, 511:703], e.rel_rev).then_inc(rel_in, 16)
            sp.wait_ge(V.sem, V.done(("ext", 1)))
            sp.dma_start(e.ext_d, ext[:]).then_inc(ext_out, 16)
            sp.wait_ge(ext_out, 16)
            sp.dma_start(e.bias_d, bass.AP(tensor=e.ext_d.tensor, offset=P - 1, ap=[[EXT, 2 * HP], [-1, P], [1, BAND]])).then_inc(bias_out, 16)
            sp.wait_ge(bias_out, 16)

        @block.scalar
        def _(act):
            act.wait_ge(par_in, 16)
            norm_act(e, act, A, V, PE, "x", xb, NT, st, junk[:], stage, e.par[:, Q_PRE:Q_PRE + KT],
                     lambda eng, i: eng.wait_ge(x_in[i], 16))
            A.close()

        @block.vector
        def _(vec):
            vec.wait_ge(rel_in, 16)
            nc.vector.tensor_copy(ext[:, 0:511], ext[:, 511:512].broadcast_to([2 * HP, 511])).then_inc(v_s, V.one(("ext", 0)))
            nc.vector.memset(ext[:, 703:EXT], 0.0).then_inc(v_s, V.one(("ext", 1)))
            norm_vec(e, vec, A, V, "x", xb, NT, st, stage, e.ahi, e.alo)
            V.close()

        @block.tensor
        def _(pe):
            pe.wait_ge(const_in, 16)
            norm_pe(e, pe, A, V, PE, "x", xb, NT)
            PE.close()


def mix_phase(e):
    nc = e.nc
    with ExitStack() as ctx:
        sb = lambda name, shape, dt=F32: e.sb(name, shape, dt, ctx)
        lora = sb("lora", [P, SEQ])
        sg = sb("sig_gate", [P, 2, SEQ])
        lup = sb("lora_up", [P, P])
        gup = sb("gate_up", [P, 2, P])
        bias = sb("bias", [P, 2, BAND])
        cur = sb("cur", [P, PP + 4])
        Z = sb("work", [P, 7 * SEQ])
        r_t, k_t, a_t, kk_t = (sb(n, [P, SEQ]) for n in ("r_cm", "k_cm", "a_cm", "kk_cm"))
        v_t = sb("v_cm", [P, SEQ])
        QR = sb("kq_rt", [P, NC_, 2 * C])
        BK = sb("bt_kt", [P, NC_, 2 * C])
        qz = sb("att_q", [P, 2, SEQ])
        kT = sb("att_k", [P, SEQ])
        vtm = sb("att_v_tok", [P, NT, P])
        yb = sb("att_out", [P, SEQ])
        vT = yb
        pe_s = sb("probs", [P, 2, BAND])
        pT = sb("probs_T", [P, BANDT, 2, P])
        small = sb("small", [P, 8])
        st_S = sb("state", [P, 2, C])
        st_L = sb("state_decayed", [P, C])
        Wt = sb("w_tok", [P, C])
        Ut = sb("u_tok", [P, C])
        lamC = sb("chunk_decay", [P, NC_])

        rs_kk, sq, sig, Ls, Linv, Lam, Lamx = (Z[:, 1024 * i:1024 * (i + 1)] for i in range(7))
        Pr, Pk = (QR[:].rearrange("p c t -> p (c t)")[:, SEQ * i:SEQ * (i + 1)] for i in range(2))
        Pb = {"r": Pr, "k": Pk, "v": yb[:]}
        Zb = {"r": r_t[:], "k": k_t[:], "v": v_t[:]}
        M1 = Z[:, 0:2048].rearrange("p (c t) -> p c t", t=2 * C)
        M2 = Z[:, 2048:4096].rearrange("p (c t) -> p c t", t=2 * C)
        T, TT, X = (Z[:, 4096 + 1024 * i:5120 + 1024 * i].rearrange("p (c t) -> p c t", t=C) for i in range(3))
        Vm, Bm, Km = (t[:].rearrange("p (c t) -> p c t", t=C) for t in (k_t, kk_t, a_t))
        yT = Z[:, 4096:5120]
        gsq, grs = Z[:, 6144:6656], Z[:, 6656:7168]

        mask2 = e.consts[:, C_MASK:C_MASK + P]
        bc = lambda ap, n: ap.rearrange("p (a t) -> p a t", a=1).broadcast_to([P, n, ap.shape[1]])
        eye8 = bc(e.consts[:, C_EYE:C_EYE + C], GC)
        level = {m: bc(e.consts[:, C_LV + C * n:C_LV + C * (n + 1)], GC) for n, m in enumerate(LEVELS)}
        ones = e.consts[:, C_ONES:C_ONES + P]
        param = lambda i: cur[:, i:i + 1]

        w = weight_sems(e, e.ctx, "mix")
        loaded, w_split, (w_used, _, _) = w
        pro_act, pro_vec, pro_pe = sems(nc, e.ctx, "lora_act", "lora_vec", "lora_pe")
        act_done, vec_done, pe_done = sems(nc, e.ctx, "act_done", "vec_done", "pe_done")
        pe_passed, vec_passed = sems(nc, e.ctx, "pe_passed", "vec_passed")
        lup_in, gup_in, ya_out, yb_out = sems(nc, e.ctx, "lup_in", "gup_in", "ya_out", "yb_out")
        bias_in = sems(nc, e.ctx, "bias_in0", "bias_in1")

        def unit(u):
            j, i = u % 2, u // 2
            return j, i, min(i + 1, BANDT)

        NU = 16
        halves = (0, 1)
        a_names = [("T", name, h) for name in "kr" for h in halves]
        a_names += [("kksq", h) for h in halves] + [("sig", h) for h in halves]
        a_names += [("P", "v", 0), ("T", "v", 0)] + [("a", h) for h in halves] + [("kksd", h) for h in halves]
        a_names += ["Linv", "Lam", "Lamx", ("P", "v", 1), ("T", "v", 1)]
        a_names += [("aq", h, j) for h in halves for j in range(2)]
        a_names += [(n, g) for g in range(G) for n in ("Vm", "Bm", "Km")] + [("av", 0)]
        for m in LEVELS:
            for g in range(G):
                if m == 4 and g == 0:
                    a_names += [("av", 1)]
                a_names += [("T", m, g)] * (m != LEVELS[-1])
                if m == 4 and g == 0:
                    a_names += [("vtm", 0), ("vtm", 1)]
                if m == 8 and g == 1:
                    a_names += [("ak", 0)]
                a_names += [("TT", m, g)]
                if m == 16 and g == 1:
                    a_names += [("ak", 1)]
                if m == 32 and g == 0:
                    a_names += [("exp", 0), ("exp", 1)]
        v_names = ["cur", "om", "omk", ("z", "k"), ("z", "r")] + [("scan", n) for n in range(SEQ // SCAN)] + [("kkmax", 0), ("kkmax", 1), "Lx"]
        for h in halves:
            v_names += [(n, h) for n in ("kkrs", "kk", "b", "bt", "kq", "rt", "am", "kp", "kt")]
        v_names += ["lamC"]
        for g in range(G):
            if g == 1:
                v_names += [("z", "v"), "rk", ("bmask", 0), ("bmask", 1)]
            v_names += [("X1", g, 0), ("X1", g, 1), ("X2", g, 0), ("X2", g, 1), ("A", g)]
            v_names += [("T2", g), ("T2T0", g), ("T2T", g), ("ATI", g)]
        for m in LEVELS:
            v_names += [("X", m, g) for g in range(G)]
            if m == 32:
                v_names += [("ttr", 0), ("nmx", 0), ("ttr", 1), ("nmx", 1), ("rin", 0), ("pn", 0)]
        p_names = [("dec", h) for h in halves] + [("v", 0)] + [("icl", h) for h in halves]
        p_names += [("kkss", h) for h in halves] + [("v", 1), ("aq", 0)]
        order = []
        for g in range(G):
            order += [("X1", g, 0), ("X1", g, 1), ("X2", g, 0), ("X2", g, 1), ("A", g)]
        order += [(n, g) for g in range(G) for n in ("Vm", "Bm", "Km")]
        for m in LEVELS:
            order += [("X", m, g) for g in range(G)]
            for g in range(G):
                order += [("T", m, g)] * (m != LEVELS[-1]) + [("TT", m, g)]
        STEPS_AT = {item: [] for item in order}
        for first, apart, name, h in ((1, 0, "aq", 1), (2, 2, "av", 0), (16, 1, "av", 1), (25, 1, "ak", 0), (33, 1, "ak", 1)):
            for kt in range(KT):
                STEPS_AT[order[first + apart * kt]] += [(name, h, kt)]
        for item in order:
            p_names += [item]
            p_names += [(name, h) for name, h, kt in STEPS_AT[item] if kt == KT - 1]
            if item == ("T", 4, 0):
                p_names += [("avT", 0), ("avT", 1)]
            if item == ("X", 32, 1):
                p_names += [("sc", 0), ("sc", 1)]

        ELEN = 8

        def e_stage(c):
            return (0, c - 8) if c >= 8 else (None, None)

        def five(u):
            return unit(u)[2] == BANDT

        def slots_act(c):
            out = [("SL", c)] * (c > 0) + [("pT", c)] + [("pT5", c)] * five(c) + [("Y", c)]
            return out + [("exp", c + 2)] * (c + 2 < NU) + [("out", c, 0), ("out", c, 1)] * (c % 2)

        def slots_vec(c):
            return [("W", c)] + [("rin", c + 1), ("pn", c + 1)] * (c + 1 < NU) + [("U", c), ("S", c)] + [("ttr", c + 2), ("nmx", c + 2)] * (c + 2 < NU)

        def slots_pe(c):
            return [("W", c), ("pT", c), ("U", c)] + [("sc", c + 2)] * (c + 2 < NU) + [("S", c), ("Y", c)] + [("out", c)] * (c % 2)

        E_ACT = [["gsq"], ["gsd"], [], [], [], [], [], []]
        E_VEC = [["yc"], ["gms"], ["grs0"], ["bov", "grs1"], ["grs2"], ["grs3"], ["yn", "yw"], ["yb", "yg"]]
        E_PE = [["mu"], ["var"], ["bo"], [], [], [], [], ["gt"]]
        for c in range(NC_):
            a_names += slots_act(c)
            v_names += slots_vec(c)
            p_names += slots_pe(c) + [("r", 0)] * (c == KT - 1)
            h, s = e_stage(c)
            if h is not None:
                a_names += [(n, h) for n in E_ACT[s]]
                v_names += [(n, h) for n in E_VEC[s]]
                p_names += [(n, h) for n in E_PE[s]]
        for s in range(ELEN):
            a_names += [(n, 1) for n in E_ACT[s]] + {1: [("P", "r", 0), ("P", "r", 1)], 2: [("P", "k", 0), ("P", "k", 1)]}.get(s, [])
            v_names += [(n, 1) for n in E_VEC[s]]
            p_names += [(n, 1) for n in E_PE[s]]
            p_names += {0: [("r", 1)], 1: [("k", 0)], 2: [("k", 1)]}.get(s, [])
        A = Steps(act_done, a_names, True)
        V = Steps(vec_done, v_names, True)
        PE = Steps(pe_done, p_names, True)
        LA = Steps(pro_act, [("pc", n, h) for n in range(3) for h in halves] + ["tanh", ("sg", 0), ("sg", 1)] + [("P", n, h) for n in "rk" for h in halves])
        LV = Steps(pro_vec, ["qzero0", "qzero1", "omm", ("t", 0), ("z", 0), ("t", 1), ("z", 1), ("t", 2), ("z", 2)])
        LP = Steps(pro_pe, [("l", n, h) for n in range(3) for h in halves] + [(n, h) for n in "rk" for h in halves])

        bank = e.ps
        block = ctx.enter_context(nc.Block())
        start_weights(e, block, NB_LORA, NB_GA, w)

        hs = [slice(0, HALF), slice(HALF, SEQ)]
        rows = [slice(0, C), slice(C, P)]

        def gn_pe(pe, hp, h, s):
            if s == 0:
                pe.wait_ge(act_done, A.done(("Y", NC_ // 2 * (h + 1) - 1), hp))
                if h == 1:
                    pe.wait_ge(vec_done, V.done(("yg", 0), hp))
                nc.tensor.matmul(bank[3], ones, yT[:, hs[h]], start=True, stop=True).then_inc(pe_done, PE.one(("mu", h)))
            elif s == 1:
                pe.wait_ge(act_done, A.done(("gsq", h), hp))
                nc.tensor.matmul(bank[3], ones, gsq, start=True, stop=True).then_inc(pe_done, PE.one(("var", h)))
            elif s == 2:
                pe.wait_ge(vec_done, V.done(("gms", h), hp))
                nc.tensor.matmul(bank[3], ones, r_t[:, hs[h]], start=True, stop=True).then_inc(pe_done, PE.one(("bo", h)))
            elif s == 7:
                pe.wait_ge(vec_done, V.done(("bov", h), hp))
                pe.wait_ge(gup_in, hp * 16 + 16)
                nc.tensor.matmul(bank[3], gup[:, 0, :], sg[:, 0, hs[h]], start=True, stop=False)
                nc.tensor.matmul(bank[3], gup[0:32, 1, :], sg[0:32, 1, hs[h]], start=False, stop=True).then_inc(pe_done, PE.one(("gt", h)))

        def gn_act(act, hp, h, s):
            if s == 0:
                act.wait_ge(vec_done, V.done(("yc", h), hp))
                nc.scalar.activation(gsq, yT[:, hs[h]], ACT.Square).then_inc(act_done, A.one(("gsq", h)))
            elif s == 1:
                act.wait_ge(vec_done, V.done(("gms", h), hp))
                nc.scalar.activation(grs, grs, ACT.Sqrt).then_inc(act_done, A.one(("gsd", h)))
            elif s == 7:
                act.wait_ge(vec_done, V.done(("yg", h), hp))
                act.dma_start(e.ya_d[bass.ds(hp, 1), :, hs[h]].rearrange("a p t -> p (a t)"), yT[:, hs[h]]).then_inc(ya_out, 16)

        def gn_vec(vec, hp, h, s):
            tt, ts, stt = nc.vector.tensor_tensor, nc.vector.tensor_scalar, nc.vector.scalar_tensor_tensor
            y = yT[:, hs[h]]
            if s == 0:
                vec.wait_ge(pe_done, PE.done(("mu", h), hp))
                stt(out=y, in0=bank[3], scalar=-1.0 / C, in1=y, op0=ALU.mult, op1=ALU.add).then_inc(vec_done, V.one(("yc", h)))
            elif s == 1:
                vec.wait_ge(pe_done, PE.done(("var", h), hp))
                ts(grs, bank[3], 1.0 / C, GN_EPS, ALU.mult, ALU.add).then_inc(vec_done, V.one(("gms", h)))
            elif 2 <= s < 6:
                if s == 2:
                    vec.wait_ge(act_done, A.done(("gsd", h), hp))
                if s == 3:
                    vec.wait_ge(pe_done, PE.done(("bo", h), hp))
                    tt(gsq, bank[3], v_t[:, hs[h]], ALU.mult).then_inc(vec_done, V.one(("bov", h)))
                part = grs[:, (s - 2) * P:(s - 1) * P]
                nc.vector.reciprocal(part, part).then_inc(vec_done, V.one((f"grs{s - 2}", h)))
            elif s == 6:
                vec.wait_ge(vec_done, V.done(("grs3", h), hp))
                tt(y, y, grs, ALU.mult).then_inc(vec_done, V.one(("yn", h)))
                vec.wait_ge(vec_done, V.done(("yn", h), hp))
                ts(y, y, param(LNW), param(LNB), ALU.mult, ALU.add).then_inc(vec_done, V.one(("yw", h)))
            else:
                vec.wait_ge(vec_done, V.done(("yw", h), hp))
                tt(y, y, gsq, ALU.add).then_inc(vec_done, V.one(("yb", h)))
                vec.wait_ge(vec_done, V.done(("yb", h), hp))
                vec.wait_ge(pe_done, PE.done(("gt", h), hp))
                tt(y, bank[3], y, ALU.mult).then_inc(vec_done, V.one(("yg", h)))

        BANKS = {"r": (5, 0), "k": (1, 4), "dec": (2, 6), "icl": (5, 0), "kkss": (1, 4), "v": (7, 3), "aq": (6, 7), "av": (6, 7), "ak": (6, 7)}

        def project(pe, blk, name, h, kts=range(KT)):
            s = blk % 2
            for kt in kts:
                last = mm3(nc, bank[BANKS[name][h]], e.whi[:, s, kt], e.wlo[:, s, kt], e.ahi[:, kt, hs[h]], e.alo[:, kt, hs[h]], kt == 0, kt == KT - 1)
            return last

        def project_step(pe, hp, item):
            for name, h, kt in STEPS_AT[item]:
                blk = NB_HEAD + 3 + ("aq", "av", "ak").index(name)
                if kt == 0:
                    if h == 0:
                        pe.wait_ge(w_split, hp * 6 + blk + 1)
                    pe.wait_ge(act_done, A.done({("aq", 1): ("T", "v", 0), ("av", 0): ("aq", 0, 1), ("av", 1): ("aq", 1, 1),
                                                 ("ak", 0): ("vtm", 0), ("ak", 1): ("vtm", 1)}[name, h], hp))
                last = project(pe, blk, name, h, [kt])
                if kt == KT - 1:
                    last.then_inc(pe_done, PE.one((name, h)))

        def mix_pe(pe, hp):
            blk = NB_HEAD + 2
            pe.wait_ge(lup_in, hp * 16 + 16)
            pe.wait_ge(act_done, A.done(("out", NU - 1, 1), hp, 1))
            for h in halves:
                nc.tensor.matmul(bank[BANKS["dec"][h]], lup[0:C, :], lora[0:C, hs[h]], start=True, stop=True).then_inc(pe_done, PE.one(("dec", h)))
            pe.wait_ge(w_split, hp * 6 + blk + 1)
            project(pe, blk, "v", 0).then_inc(pe_done, PE.one(("v", 0)))
            pe.wait_ge(act_done, A.done(("T", "r", 1), hp))
            for h in halves:
                nc.tensor.matmul(bank[BANKS["icl"][h]], lup[C:P, :], lora[C:P, hs[h]], start=True, stop=True).then_inc(pe_done, PE.one(("icl", h)))
            pe.wait_ge(vec_done, V.done(("yg", 1), hp, 1))
            project(pe, blk, "v", 1, range(KT // 2))
            for h in halves:
                pe.wait_ge(act_done, A.done(("kksq", h), hp))
                nc.tensor.matmul(bank[BANKS["kkss"][h]], ones, sq[:, hs[h]], start=True, stop=True).then_inc(pe_done, PE.one(("kkss", h)))
            project(pe, blk, "v", 1, range(KT // 2, KT)).then_inc(pe_done, PE.one(("v", 1)))
            pe.wait_ge(w_split, hp * 6 + blk + 2)
            pe.wait_ge(act_done, A.done(("sig", 1), hp))
            project(pe, blk + 1, "aq", 0).then_inc(pe_done, PE.one(("aq", 0)))
            xb = {0: (0, 1, 2, 3, 4), 1: (5, 0, 1, 2, 3)}
            for g in range(G):
                for q in range(2):
                    b = bank[xb[g][q]]
                    if q == 0:
                        pe.wait_ge(vec_done, V.done(("rt", g), hp))
                    elif g == 1:
                        pe.wait_ge(vec_done, V.done(("X1", 0, 0), hp))
                    settle(pe, pe_passed)
                    for cc in range(4):
                        c = g * GC + q * 4 + cc
                        for j in range(2):
                            last = nc.tensor.matmul(b[rows[j], cc * P:(cc + 1) * P], BK[rows[j], c, 0:C], QR[rows[j], c, :], start=True, stop=True, skip_group_check=True)
                    last.then_inc(pe_done, PE.one(("X1", g, q)))
                    project_step(pe, hp, ("X1", g, q))
                for q in range(2):
                    b = bank[xb[g][2 + q]]
                    if g == 1:
                        pe.wait_ge(vec_done, V.done(("X1", 0, 1) if q == 0 else ("X2", 0, 0), hp))
                    elif q == 1:
                        pe.wait_ge(act_done, A.done(("T", "v", 1), hp))
                    if q == 0:
                        pe.wait_ge(vec_done, V.done(("kt", g), hp))
                    settle(pe, pe_passed)
                    for cc in range(4):
                        c = g * GC + q * 4 + cc
                        for j in range(2):
                            last = nc.tensor.matmul(b[rows[j], cc * P:(cc + 1) * P], BK[rows[j], c, C:P], QR[rows[j], c, :], start=True, stop=True, skip_group_check=True)
                    last.then_inc(pe_done, PE.one(("X2", g, q)))
                    project_step(pe, hp, ("X2", g, q))
                b = bank[xb[g][4]]
                if g == 1:
                    pe.wait_ge(vec_done, V.done(("X2", 0, 1), hp))
                settle(pe, pe_passed)
                for cc in range(GC):
                    c = g * GC + cc
                    for j in range(2):
                        last = nc.tensor.matmul(b[rows[j], cc * C:(cc + 1) * C], QR[rows[j], c, 0:C], BK[rows[j], c, 0:C], start=True, stop=True, skip_group_check=True)
                last.then_inc(pe_done, PE.one(("A", g)))
                project_step(pe, hp, ("A", g))
            tm_bank = {("Vm", 0): 4, ("Bm", 0): 5, ("Km", 0): 0, ("Vm", 1): 1, ("Bm", 1): 2, ("Km", 1): 3}
            prev = {("Vm", 0): ("z", "v"), ("Bm", 0): ("X1", 1, 0), ("Km", 0): ("X1", 1, 1),
                    ("Vm", 1): ("X2", 1, 0), ("Bm", 1): ("X2", 1, 1), ("Km", 1): ("A", 1)}
            for g in range(G):
                for n, name in enumerate(("Vm", "Bm", "Km")):
                    b = bank[tm_bank[name, g]]
                    pe.wait_ge(vec_done, V.done(prev[name, g], hp))
                    settle(pe, pe_passed)
                    for cc in range(GC):
                        c = g * GC + cc
                        for j in range(2):
                            src = {"Vm": v_t[rows[j], c * C:(c + 1) * C], "Bm": BK[rows[j], c, 0:C], "Km": BK[rows[j], c, C:P]}[name]
                            last = nc.tensor.matmul(b[rows[j], cc * C:(cc + 1) * C], src, e.consts[rows[j], C_EYE:C_EYE + C], start=True, stop=True, skip_group_check=True)
                    last.then_inc(pe_done, PE.one((name, g)))
                    project_step(pe, hp, (name, g))
            for m in LEVELS:
                for g in range(G):
                    if m == 2:
                        pe.wait_ge(vec_done, V.done(("ATI", g), hp))
                        pe.wait_ge(act_done, A.done(("Km", g), hp))
                    else:
                        pe.wait_ge(act_done, A.done(("T", m // 2, g), hp))
                        pe.wait_ge(vec_done, V.done(("X", m // 2, g), hp))
                    settle(pe, pe_passed)
                    for cc in range(GC):
                        c = g * GC + cc
                        for j in range(2):
                            last = nc.tensor.matmul(bank[3 * g][rows[j], cc * C:(cc + 1) * C], M1[rows[j], c, 0:C], T[rows[j], c, :], start=True, stop=True, skip_group_check=True)
                    last.then_inc(pe_done, PE.one(("X", m, g)))
                    project_step(pe, hp, ("X", m, g))
                if m == 32:
                    for u in range(2):
                        pe.wait_ge(act_done, A.done(("ak", 1), hp))
                        scores(u).then_inc(pe_done, PE.one(("sc", u)))
                for g in range(G):
                    pe.wait_ge(vec_done, V.done(("X", m, g), hp))
                    if m == 2:
                        pe.wait_ge(act_done, A.done(("Bm", 1), hp))
                    else:
                        pe.wait_ge(act_done, A.done(("TT", m // 2, g), hp))
                    if m != LEVELS[-1]:
                        settle(pe, pe_passed)
                        for cc in range(GC):
                            c = g * GC + cc
                            for j in range(2):
                                last = nc.tensor.matmul(bank[3 * g + 1][rows[j], cc * C:(cc + 1) * C], TT[rows[j], c, :], X[rows[j], c, :], start=True, stop=True, skip_group_check=True)
                        last.then_inc(pe_done, PE.one(("T", m, g)))
                        project_step(pe, hp, ("T", m, g))
                    if m == 4 and g == 0:
                        for n in range(2):
                            pe.wait_ge(act_done, A.done(("av", n), hp))
                            for i in range(4):
                                last = nc.tensor.transpose(bank[6 + n][:, i * P:(i + 1) * P], vT[:, (4 * n + i) * P:(4 * n + i + 1) * P], e.ident)
                            last.then_inc(pe_done, PE.one(("avT", n)))
                    settle(pe, pe_passed)
                    for cc in range(GC):
                        c = g * GC + cc
                        for j in range(2):
                            last = nc.tensor.matmul(bank[3 * g + 2][rows[j], cc * C:(cc + 1) * C], X[rows[j], c, :], TT[rows[j], c, :], start=True, stop=True, skip_group_check=True)
                    last.then_inc(pe_done, PE.one(("TT", m, g)))
                    project_step(pe, hp, ("TT", m, g))
            for c in range(NC_):
                if c == 0:
                    pe.wait_ge(act_done, A.done(("TT", 32, 1), hp))
                else:
                    pe.wait_ge(vec_done, V.done(("S", c - 1), hp))
                settle(pe, pe_passed)
                for j in range(2):
                    last = nc.tensor.matmul(bank[4][rows[j], 0:C], M2[rows[j], c, 0:C], Vm[rows[j], c, :], start=True, stop=c == 0)
                if c > 0:
                    for j in range(2):
                        last = nc.tensor.matmul(bank[4][rows[j], 0:C], QR[rows[j], c, 0:C], st_S[rows[j], c % 2, :], start=False, stop=True)
                last.then_inc(pe_done, PE.one(("W", c)))
                nk = unit(c)[2]
                pe.wait_ge(vec_done, V.done(("pn", c), hp))
                if c > 0:
                    pe.wait_ge(act_done, A.done(("out", c - 1, 1) if c % 2 == 0 else ("pT5" if five(c - 1) else "pT", c - 1), hp))
                for t in range(nk):
                    dst = bank[2][:, t * P:(t + 1) * P] if t < 4 else bank[7][:, 2 * P:3 * P]
                    last = nc.tensor.transpose(dst, pe_s[:, c % 2, t * P:(t + 1) * P], e.ident)
                last.then_inc(pe_done, PE.one(("pT", c)))
                pe.wait_ge(vec_done, V.done(("W", c), hp))
                settle(pe, pe_passed)
                for j in range(2):
                    last = nc.tensor.matmul(bank[4][rows[j], 0:C], TT[rows[j], c, :], Wt[rows[j], :], start=True, stop=True)
                last.then_inc(pe_done, PE.one(("U", c)))
                if c + 2 < NU:
                    if c > 0:
                        pe.wait_ge(vec_done, V.done(("ttr", c + 1), hp))
                    scores(c + 2).then_inc(pe_done, PE.one(("sc", c + 2)))
                pe.wait_ge(vec_done, V.done(("U", c), hp))
                settle(pe, pe_passed)
                for j in range(2):
                    nc.tensor.matmul(bank[4][rows[j], 0:C], Km[rows[j], c, :], Vm[rows[j], c, :], start=True, stop=False)
                for j in range(2):
                    last = nc.tensor.matmul(bank[4][rows[j], 0:C], Bm[rows[j], c, :], Ut[rows[j], :], start=False, stop=True)
                last.then_inc(pe_done, PE.one(("S", c)))
                if c > 0:
                    pe.wait_ge(act_done, A.done(("Y", c - 1), hp))
                settle(pe, pe_passed)
                for j in range(2):
                    nc.tensor.matmul(bank[6][rows[j], 0:C], Vm[rows[j], c, :], M2[rows[j], c, C:P], start=True, stop=False)
                for j in range(2):
                    last = nc.tensor.matmul(bank[6][rows[j], 0:C], Ut[rows[j], :], M1[rows[j], c, C:P], start=False, stop=c == 0)
                if c > 0:
                    for j in range(2):
                        last = nc.tensor.matmul(bank[6][rows[j], 0:C], st_S[rows[j], c % 2, :], QR[rows[j], c, C:P], start=False, stop=True)
                last.then_inc(pe_done, PE.one(("Y", c)))
                if c % 2:
                    j, i, nk = unit(c)
                    pe.wait_ge(act_done, A.done(("pT5" if five(c) else "pT", c), hp))
                    for t in range(nk):
                        last = nc.tensor.matmul(bank[7][:, 0:2 * P], vtm[:, i + 1 - nk + t, :], pT[:, t, :, :].rearrange("p j q -> p (j q)"), start=t == 0, stop=t == nk - 1)
                    last.then_inc(pe_done, PE.one(("out", c)))
                if c < KT:
                    if c == 0:
                        pe.wait_ge(w_split, hp * 6 + (NB_HEAD + 7))
                    last = project(pe, NB_HEAD, "r", 0, [c])
                    if c == KT - 1:
                        last.then_inc(pe_done, PE.one(("r", 0)))
                h, s = e_stage(c)
                if h is not None:
                    gn_pe(pe, hp, h, s)
            for s in range(ELEN):
                gn_pe(pe, hp, 1, s)
                if s == 0:
                    project(pe, NB_HEAD, "r", 1).then_inc(pe_done, PE.one(("r", 1)))
                if s == 1:
                    pe.wait_ge(w_split, hp * 6 + (NB_HEAD + 8))
                    project(pe, NB_HEAD + 1, "k", 0).then_inc(pe_done, PE.one(("k", 0)))
                if s == 2:
                    project(pe, NB_HEAD + 1, "k", 1).then_inc(pe_done, PE.one(("k", 1)))

        def scores(u):
            j, i, nk = unit(u)
            k0, n0 = (i + 1 - nk) * P, min(nk, 4) * P
            b0 = 6 + u if u < 2 else 0
            last = nc.tensor.matmul(bank[b0][:, 0:n0], qz[:, j, i * P:(i + 1) * P], kT[:, k0:k0 + n0], start=True, stop=True)
            if nk == BANDT:
                last = nc.tensor.matmul(bank[1][:, 0:P], qz[:, j, i * P:(i + 1) * P], kT[:, k0 + n0:k0 + n0 + P], start=True, stop=True)
            return last

        def mix_act(act, hp):
            act.wait_ge(vec_done, V.done("omk", hp))
            for name in "kr":
                for h in halves:
                    nc.scalar.activation(Zb[name][:, hs[h]], bank[BANKS[name][h]], ACT.Copy, scale=param(OM_K if name == "k" else OM_R)).then_inc(act_done, A.one(("T", name, h)))
            act.wait_ge(vec_done, V.done(("z", "k"), hp))
            for h in halves:
                nc.scalar.activation(sq[:, hs[h]], k_t[:, hs[h]], ACT.Square, scale=param(KNS)).then_inc(act_done, A.one(("kksq", h)))
            for h in halves:
                act.wait_ge(pe_done, PE.done(("dec", h), hp))
                nc.scalar.activation(sig[:, hs[h]], bank[BANKS["dec"][h]], ACT.Sigmoid, bias=param(DEC_B)).then_inc(act_done, A.one(("sig", h)))
            act.wait_ge(yb_out, hp * 16 + 1)
            v_act(act, hp, 0)
            for h in halves:
                act.wait_ge(pe_done, PE.done(("icl", h), hp))
                nc.scalar.activation(a_t[:, hs[h]], bank[BANKS["icl"][h]], ACT.Sigmoid, bias=param(ICL_B)).then_inc(act_done, A.one(("a", h)))
            act.dma_start(lup[:], e.lora_up[bass.ds(hp + 1, 1)].rearrange("a p m -> p (a m)")).then_inc(lup_in, 16)
            for h in halves:
                act.wait_ge(vec_done, V.done(("kkmax", h), hp))
                nc.scalar.activation(rs_kk[:, hs[h]], rs_kk[:, hs[h]], ACT.Sqrt).then_inc(act_done, A.one(("kksd", h)))
            nc.scalar.activation(Linv, Ls, ACT.Exp, scale=EXP_HALF).then_inc(act_done, A.one("Linv"))
            nc.scalar.activation(Lam, Ls, ACT.Exp, scale=-EXP_HALF).then_inc(act_done, A.one("Lam"))
            act.wait_ge(vec_done, V.done("Lx", hp))
            nc.scalar.activation(Lamx, sig, ACT.Exp, scale=-EXP_HALF).then_inc(act_done, A.one("Lamx"))
            v_act(act, hp, 1)
            act.sem_inc(w_used, 1)
            act.dma_start(gup[:], e.gate_up2[bass.ds(hp, 1)].rearrange("a p g m -> p (a g) m")).then_inc(gup_in, 16)
            for j in range(2):
                act.dma_start(bias[:, j], e.bias_d[bass.ds(hp * 2 + j, 1)].rearrange("a p c -> p (a c)")).then_inc(bias_in[j], 16)
            for h in halves:
                act.wait_ge(pe_done, PE.done(("aq", h), hp))
                if h == 1:
                    act.sem_inc(w_used, 1)
                for j in range(2):
                    nc.scalar.activation(qz[rows[j], j, hs[h]], bank[6 + h][rows[j], :], ACT.Copy, scale=0.125).then_inc(act_done, A.one(("aq", h, j)))
            act.wait_ge(vec_done, V.done("rk", hp))
            tm_bank = {("Vm", 0): 4, ("Bm", 0): 5, ("Km", 0): 0, ("Vm", 1): 1, ("Bm", 1): 2, ("Km", 1): 3}
            for g in range(G):
                for name, dst in (("Vm", Vm), ("Bm", Bm), ("Km", Km)):
                    act.wait_ge(pe_done, PE.done((name, g), hp))
                    nc.scalar.activation(dst[:, g * GC:(g + 1) * GC, :].rearrange("p c t -> p (c t)"), bank[tm_bank[name, g]], ACT.Copy).then_inc(act_done, A.one((name, g)))
            kv_act(act, hp, "av", 0)
            for m in LEVELS:
                for g in range(G):
                    gs = slice(g * GC, (g + 1) * GC)
                    if m == 4 and g == 0:
                        kv_act(act, hp, "av", 1)
                    if m != LEVELS[-1]:
                        act.wait_ge(pe_done, PE.done(("T", m, g), hp))
                        nc.scalar.activation(T[:, gs, :].rearrange("p c t -> p (c t)"), bank[3 * g + 1], ACT.Copy).then_inc(act_done, A.one(("T", m, g)))
                    if m == 4 and g == 0:
                        for n in range(2):
                            act.wait_ge(pe_done, PE.done(("avT", n), hp))
                            nc.scalar.activation(vtm[:, 4 * n:4 * n + 4, :].rearrange("p i m -> p (i m)"), bank[6 + n], ACT.Copy).then_inc(act_done, A.one(("vtm", n)))
                    if m == 8 and g == 1:
                        kv_act(act, hp, "ak", 0)
                    act.wait_ge(pe_done, PE.done(("TT", m, g), hp))
                    nc.scalar.activation(TT[:, gs, :].rearrange("p c t -> p (c t)"), bank[3 * g + 2], ACT.Copy).then_inc(act_done, A.one(("TT", m, g)))
                    if m == 16 and g == 1:
                        kv_act(act, hp, "ak", 1)
                    if m == 32 and g == 0:
                        for u in range(2):
                            exp_act(act, hp, u)
            for c in range(NC_):
                if c > 0:
                    act.wait_ge(vec_done, V.done(("S", c - 1), hp))
                    nc.scalar.activation(st_L[:], st_S[:, c % 2, :], ACT.Copy, scale=lamC[:, c:c + 1]).then_inc(act_done, A.one(("SL", c)))
                j, i, nk = unit(c)
                act.wait_ge(pe_done, PE.done(("pT", c), hp))
                n0 = min(nk, 4)
                nc.scalar.activation(pT[:, 0:n0, j, :], bank[2][:, 0:n0 * P].rearrange("p (t q) -> p t q", q=P), ACT.Copy).then_inc(act_done, A.one(("pT", c)))
                if nk == BANDT:
                    nc.scalar.activation(pT[:, 4, j, :], bank[7][:, 2 * P:3 * P], ACT.Copy).then_inc(act_done, A.one(("pT5", c)))
                act.wait_ge(pe_done, PE.done(("Y", c), hp))
                nc.scalar.activation(yT[:, c * C:(c + 1) * C], bank[6][:, 0:C], ACT.Copy).then_inc(act_done, A.one(("Y", c)))
                if c + 2 < NU:
                    exp_act(act, hp, c + 2)
                if c % 2:
                    act.wait_ge(pe_done, PE.done(("out", c), hp))
                    for j in range(2):
                        nc.scalar.activation(yb[rows[j], i * P:(i + 1) * P], bank[7][rows[j], j * P:(j + 1) * P], ACT.Copy).then_inc(act_done, A.one(("out", c, j)))
                h, s = e_stage(c)
                if h is not None:
                    gn_act(act, hp, h, s)
            act.wait_ge(act_done, A.done(("out", NU - 1, 1), hp))
            act.dma_start(e.yb_d[bass.ds(hp, 1)].rearrange("a p t -> p (a t)"), yb[:]).then_inc(yb_out, 16)
            for s in range(ELEN):
                gn_act(act, hp, 1, s)
                if s in (1, 2):
                    name = "rk"[s - 1]
                    act.wait_ge(pe_done, PE.done((name, 1), hp))
                    act.sem_inc(w_used, 1)
                    for h in halves:
                        nc.scalar.activation(Pb[name][:, hs[h]], bank[BANKS[name][h]], ACT.Copy).then_inc(act_done, A.one(("P", name, h)))

        def v_act(act, hp, h):
            act.wait_ge(pe_done, PE.done(("v", h), hp))
            nc.scalar.activation(Pb["v"][:, hs[h]], bank[BANKS["v"][h]], ACT.Copy).then_inc(act_done, A.one(("P", "v", h)))
            nc.scalar.activation(Zb["v"][:, hs[h]], bank[BANKS["v"][h]], ACT.Copy, scale=param(OM_V)).then_inc(act_done, A.one(("T", "v", h)))

        def kv_act(act, hp, name, h):
            act.wait_ge(pe_done, PE.done((name, h), hp))
            if h == 1:
                act.sem_inc(w_used, 1)
            nc.scalar.activation({"ak": kT, "av": vT}[name][:, hs[h]], bank[6 + h], ACT.Copy).then_inc(act_done, A.one((name, h)))

        def exp_act(act, hp, u):
            nk = unit(u)[2]
            act.wait_ge(vec_done, V.done(("nmx", u), hp))
            nc.scalar.activation(pe_s[:, u % 2, 0:nk * P], pe_s[:, u % 2, 0:nk * P], ACT.Exp,
                                 bias=small[:, 2 + u % 2:3 + u % 2], accum_out=small[:, 4 + u % 2:5 + u % 2]).then_inc(act_done, A.one(("exp", u)))

        def mix_vec(vec, hp):

            tt = nc.vector.tensor_tensor
            ts = nc.vector.tensor_scalar
            stt = nc.vector.scalar_tensor_tensor
            nc.vector.tensor_copy(cur[:, 0:PP], e.par[:, bass.ds(hp * PP, PP)]).then_inc(vec_done, V.one("cur"))
            vec.wait_ge(vec_done, V.done("cur", hp))
            ts(cur[:, OM_R:OM_R + 3], cur[:, MIX_R:MIX_R + 3], -1.0, 1.0, ALU.mult, ALU.add).then_inc(vec_done, V.one("om"))
            vec.wait_ge(vec_done, V.done("om", hp))
            ts(cur[:, OM_KIS:OM_KIS + 1], param(KIS), -1.0, 1.0, ALU.mult, ALU.add).then_inc(vec_done, V.one("omk"))
            vec.wait_ge(vec_done, V.done("omk", hp))
            for name in "kr":
                vec.wait_ge(act_done, A.done(("T", name, 1), hp))
                stt(out=Zb[name][:, 1:], in0=Pb[name][:, 0:SEQ - 1], scalar=param(MIX_K if name == "k" else MIX_R), in1=Zb[name][:, 1:], op0=ALU.mult, op1=ALU.add).then_inc(vec_done, V.one(("z", name)))
            vec.wait_ge(act_done, A.done(("sig", 1), hp))
            vec.wait_ge(ya_out, hp * 32 + 1)
            for n in range(SEQ // SCAN):
                part = slice(n * SCAN, (n + 1) * SCAN)
                nc.vector.tensor_tensor_scan(Ls[:, part], e.consts[:, C_RST:C_N], sig[:, part], 0.0, ALU.mult, ALU.add).then_inc(vec_done, V.one(("scan", n)))
            for h in halves:
                vec.wait_ge(pe_done, PE.done(("kkss", h), hp))
                ts(rs_kk[:, hs[h]], bank[BANKS["kkss"][h]], 1e-24, None, ALU.max).then_inc(vec_done, V.one(("kkmax", h)))
            vec.wait_ge(vec_done, V.done(("scan", SEQ // SCAN - 1), hp))
            tt(sig, Ls, sig, ALU.subtract).then_inc(vec_done, V.one("Lx"))
            b_t = sq
            for h in halves:
                cols = hs[h]
                by_chunk = lambda ap: ap[:, cols].rearrange("p (c t) -> p c t", t=C)
                cs = slice(h * GC, (h + 1) * GC)
                vec.wait_ge(act_done, A.done(("kksd", h), hp))
                nc.vector.reciprocal(rs_kk[:, cols], rs_kk[:, cols]).then_inc(vec_done, V.one(("kkrs", h)))
                vec.wait_ge(vec_done, V.done(("kkrs", h), hp))
                stt(out=kk_t[:, cols], in0=k_t[:, cols], scalar=param(KNS), in1=rs_kk[:, cols], op0=ALU.mult, op1=ALU.mult).then_inc(vec_done, V.one(("kk", h)))
                vec.wait_ge(vec_done, V.done(("kk", h), hp))
                vec.wait_ge(act_done, A.done(("a", h), hp))
                tt(b_t[:, cols], kk_t[:, cols], a_t[:, cols], ALU.mult).then_inc(vec_done, V.one(("b", h)))
                vec.wait_ge(vec_done, V.done(("b", h), hp))
                vec.wait_ge(act_done, A.done("Linv", hp))
                tt(BK[:, cs, 0:C], by_chunk(b_t), by_chunk(Linv), ALU.mult).then_inc(vec_done, V.one(("bt", h)))
                vec.wait_ge(act_done, A.done("Lamx", hp))
                tt(QR[:, cs, 0:C], by_chunk(kk_t), by_chunk(Lamx), ALU.mult).then_inc(vec_done, V.one(("kq", h)))
                tt(QR[:, cs, C:P], by_chunk(r_t), by_chunk(Lam), ALU.mult).then_inc(vec_done, V.one(("rt", h)))
                ts(a_t[:, cols], a_t[:, cols], param(KIS), param(OM_KIS), ALU.mult, ALU.add).then_inc(vec_done, V.one(("am", h)))
                vec.wait_ge(vec_done, V.done(("am", h), hp))
                tt(k_t[:, cols], k_t[:, cols], a_t[:, cols], ALU.mult).then_inc(vec_done, V.one(("kp", h)))
                vec.wait_ge(vec_done, V.done(("kp", h), hp))
                tt(BK[:, cs, C:P], by_chunk(k_t), by_chunk(Linv), ALU.mult).then_inc(vec_done, V.one(("kt", h)))
            nc.vector.tensor_copy(lamC[:], Lam.rearrange("p (c t) -> p c t", t=C)[:, :, C - 1]).then_inc(vec_done, V.one("lamC"))
            mask4 = bc(mask2, 4)
            xb = {0: (0, 1, 2, 3, 4), 1: (5, 0, 1, 2, 3)}
            quad = lambda b: bank[b].rearrange("p (c t) -> p c t", t=2 * C)
            octo = lambda b: bank[b].rearrange("p (c t) -> p c t", t=C)
            for g in range(G):
                gs = slice(g * GC, (g + 1) * GC)
                if g == 1:
                    vec.wait_ge(act_done, A.done(("T", "v", 1), hp))
                    stt(out=v_t[:, 1:], in0=Pb["v"][:, 0:SEQ - 1], scalar=param(MIX_V), in1=v_t[:, 1:], op0=ALU.mult, op1=ALU.add).then_inc(vec_done, V.one(("z", "v")))
                    vec.wait_ge(vec_done, V.done(("rt", 1), hp))
                    stt(out=r_t[:], in0=r_t[:], scalar=param(BON), in1=k_t[:], op0=ALU.mult, op1=ALU.mult).then_inc(vec_done, V.one("rk"))
                    for j in range(2):
                        vec.wait_ge(bias_in[j], hp * 16 + 16)
                    nc.vector.memset(bias[0:C, :, BAND - C:], MASKED).then_inc(vec_done, V.one(("bmask", 0)))
                    vec.wait_ge(vec_done, V.done(("bmask", 0), hp))
                    nc.vector.memset(bias[C:P, :, 0:C], MASKED).then_inc(vec_done, V.one(("bmask", 1)))
                    vec.wait_ge(vec_done, V.done(("bmask", 1), hp))
                for q in range(2):
                    vec.wait_ge(pe_done, PE.done(("X1", g, q), hp))
                    tt(M1[:, g * GC + 4 * q:g * GC + 4 * q + 4, :], quad(xb[g][q]), mask4, ALU.mult).then_inc(vec_done, V.one(("X1", g, q)))
                    vec.wait_ge(vec_done, V.done(("X1", g, q), hp))
                for q in range(2):
                    vec.wait_ge(pe_done, PE.done(("X2", g, q), hp))
                    tt(M2[:, g * GC + 4 * q:g * GC + 4 * q + 4, :], quad(xb[g][2 + q]), mask4, ALU.mult).then_inc(vec_done, V.one(("X2", g, q)))
                    vec.wait_ge(vec_done, V.done(("X2", g, q), hp))
                vec.wait_ge(pe_done, PE.done(("A", g), hp))
                tt(T[:, gs, :], octo(xb[g][4]), bc(e.consts[:, C_NL1:C_NL1 + C], GC), ALU.mult).then_inc(vec_done, V.one(("A", g)))
                vec.wait_ge(vec_done, V.done(("A", g), hp))
                tt(T[:, gs, :], T[:, gs, :], eye8, ALU.add).then_inc(vec_done, V.one(("T2", g)))
                vec.wait_ge(vec_done, V.done(("T2", g), hp))
                tt(TT[:, gs, :], M1[:, gs, 0:C], bc(e.consts[:, C_NL1T:C_NL1T + C], GC), ALU.mult).then_inc(vec_done, V.one(("T2T0", g)))
                vec.wait_ge(vec_done, V.done(("T2T0", g), hp))
                tt(TT[:, gs, :], TT[:, gs, :], eye8, ALU.add).then_inc(vec_done, V.one(("T2T", g)))
                vec.wait_ge(vec_done, V.done(("T2T", g), hp))
                tt(M1[:, gs, 0:C], M1[:, gs, 0:C], eye8, ALU.add).then_inc(vec_done, V.one(("ATI", g)))
                vec.wait_ge(vec_done, V.done(("ATI", g), hp))
            for m in LEVELS:
                for g in range(G):
                    vec.wait_ge(pe_done, PE.done(("X", m, g), hp))
                    tt(X[:, g * GC:(g + 1) * GC, :], octo(3 * g), level[m], ALU.mult).then_inc(vec_done, V.one(("X", m, g)))
                    vec.wait_ge(vec_done, V.done(("X", m, g), hp))
                if m == 32:
                    for u in range(2):
                        max_vec(vec, hp, u)
                    prob_vec(vec, hp, 0)
            for c in range(NC_):
                vec.wait_ge(pe_done, PE.done(("W", c), hp))
                nc.vector.tensor_copy(Wt[:], bank[4][:, 0:C]).then_inc(vec_done, V.one(("W", c)))
                if c + 1 < NU:
                    prob_vec(vec, hp, c + 1)
                vec.wait_ge(pe_done, PE.done(("U", c), hp))
                ts(Ut[:], bank[4][:, 0:C], -1.0, None, ALU.mult).then_inc(vec_done, V.one(("U", c)))
                vec.wait_ge(pe_done, PE.done(("S", c), hp))
                if c == 0:
                    ts(st_S[:, 1, :], bank[4][:, 0:C], lamC[:, 0:1], None, ALU.mult).then_inc(vec_done, V.one(("S", 0)))
                else:
                    vec.wait_ge(act_done, A.done(("SL", c), hp))
                    stt(out=st_S[:, (c + 1) % 2, :], in0=bank[4][:, 0:C], scalar=lamC[:, c:c + 1], in1=st_L[:], op0=ALU.mult, op1=ALU.add).then_inc(vec_done, V.one(("S", c)))
                if c + 2 < NU:
                    max_vec(vec, hp, c + 2)
                h, s = e_stage(c)
                if h is not None:
                    gn_vec(vec, hp, h, s)
            for s in range(ELEN):
                gn_vec(vec, hp, 1, s)

        def max_vec(vec, hp, u):
            j, i, nk = unit(u)
            b0 = (6 + u) * HALF if u < 2 else 0
            vec.wait_ge(pe_done, PE.done(("sc", u), hp))
            settle(vec, vec_passed)
            nc.vector.tensor_tensor_reduce(out=pe_s[:, u % 2, 0:nk * P], in0=e.banks[:, b0:b0 + nk * P], in1=bias[:, j, BAND - nk * P:],
                                           scale=1.0, scalar=-3e38, op0=ALU.add, op1=ALU.max, accum_out=small[:, 6 + u % 2:7 + u % 2]).then_inc(vec_done, V.one(("ttr", u)))
            vec.wait_ge(vec_done, V.done(("ttr", u), hp))
            nc.vector.tensor_scalar(small[:, 2 + u % 2:3 + u % 2], small[:, 6 + u % 2:7 + u % 2], -1.0, None, ALU.mult).then_inc(vec_done, V.one(("nmx", u)))

        def prob_vec(vec, hp, u):
            nk = unit(u)[2]
            vec.wait_ge(act_done, A.done(("exp", u), hp))
            nc.vector.reciprocal(small[:, u % 2:u % 2 + 1], small[:, 4 + u % 2:5 + u % 2]).then_inc(vec_done, V.one(("rin", u)))
            vec.wait_ge(vec_done, V.done(("rin", u), hp))
            nc.vector.tensor_scalar(pe_s[:, u % 2, 0:nk * P], pe_s[:, u % 2, 0:nk * P], small[:, u % 2:u % 2 + 1], None, ALU.mult).then_inc(vec_done, V.one(("pn", u)))

        Plora = [rs_kk, sq, sig]

        @block.tensor
        def _(pe):
            for n in range(3):
                pe.wait_ge(w_split, n + 1)
                for h in halves:
                    if n == 2:
                        pe.wait_ge(pro_act, LA.done(("pc", 0, h)))
                    last = gemm(nc, bank[(2 * n + h) % 4], e.whi[:, n % 2], e.wlo[:, n % 2], e.ahi, e.alo, range(KT), hs[h])
                    last.then_inc(pro_pe, LP.one(("l", n, h)))
            pe.wait_ge(pro_act, LA.done(("pc", 2, 1)))
            for name, blk in (("r", NB_HEAD), ("k", NB_HEAD + 1)):
                pe.wait_ge(w_split, blk + 1)
                for h in halves:
                    project(pe, blk, name, h).then_inc(pro_pe, LP.one((name, h)))
            pe.sem_inc(pe_done, PE.n)
            pe.wait_ge(pro_act, LA.done(("sg", 1)))
            with pe.Fori(0, HP) as hp:
                mix_pe(pe, hp)
            LP.close()
            PE.close()

        @block.scalar
        def _(act):
            for n in range(3):
                for h in halves:
                    act.wait_ge(pro_pe, LP.done(("l", n, h)))
                    if h == 1:
                        act.sem_inc(w_used, 1)
                    nc.scalar.activation(Plora[n][:, hs[h]], bank[(2 * n + h) % 4], ACT.Copy).then_inc(pro_act, LA.one(("pc", n, h)))
            act.wait_ge(pro_vec, LV.done(("z", 0)))
            nc.scalar.activation(lora[0:C, :], lora[0:C, :], ACT.Tanh).then_inc(pro_act, LA.one("tanh"))
            for n in range(2):
                act.wait_ge(pro_vec, LV.done(("z", n + 1)))
                nc.scalar.activation(sg[:, n, :], sg[:, n, :], ACT.Sigmoid).then_inc(pro_act, LA.one(("sg", n)))
            act.dma_start(lup[:], e.lora_up[0]).then_inc(lup_in, 16)
            for name in "rk":
                act.wait_ge(pro_pe, LP.done((name, 1)))
                act.sem_inc(w_used, 1)
                for h in halves:
                    nc.scalar.activation(Pb[name][:, hs[h]], bank[BANKS[name][h]], ACT.Copy).then_inc(pro_act, LA.one(("P", name, h)))
            act.wait_ge(pro_act, LA.done(("P", "k", 1)))
            act.sem_inc(ya_out, 1)
            act.sem_inc(yb_out, 1)
            act.sem_inc(act_done, A.n)
            with act.Fori(0, HP) as hp:
                mix_act(act, hp)
            act.wait_ge(yb_out, HP * 16 + 1)
            act.wait_ge(ya_out, HP * 32 + 1)
            LA.close()
            A.close()

        @block.vector
        def _(vec):
            for j in range(2):
                nc.vector.memset(qz[rows[1 - j], j, :], 0.0).then_inc(pro_vec, LV.one(f"qzero{j}"))
            nc.vector.tensor_scalar(cur[:, 0:3], e.par[:, Q_LORA:Q_LORA + 3], -1.0, 1.0, ALU.mult, ALU.add).then_inc(pro_vec, LV.one("omm"))
            vec.wait_ge(pro_vec, LV.done("omm"))
            dst = [lora[:], sg[:, 0, :], sg[:, 1, :]]
            for n in range(3):
                vec.wait_ge(pro_act, LA.done(("pc", n, 1)))
                nc.vector.tensor_scalar(dst[n], Plora[n], cur[:, n:n + 1], None, ALU.mult).then_inc(pro_vec, LV.one(("t", n)))
                vec.wait_ge(pro_vec, LV.done(("t", n)))
                nc.vector.scalar_tensor_tensor(out=dst[n][:, 1:], in0=Plora[n][:, 0:SEQ - 1], scalar=e.par[:, Q_LORA + n:Q_LORA + n + 1],
                                                   in1=dst[n][:, 1:], op0=ALU.mult, op1=ALU.add).then_inc(pro_vec, LV.one(("z", n)))
            vec.wait_ge(pro_vec, LV.done(("z", 2)))
            vec.sem_inc(vec_done, V.n)
            with vec.Fori(0, HP) as hp:
                mix_vec(vec, hp)
            LV.close()
            V.close()


def merge_phase(e):
    nc = e.nc
    with ExitStack() as ctx:
        yhi = e.sb("y_hi", [P, KT, SEQ], F32R, ctx)
        ylo = e.sb("y_lo", [P, KT, SEQ], F32R, ctx)
        st = e.sb("y_stage", [P, 2, SEQ], ctx=ctx)
        sg = e.sb("gates", [P, 2, SEQ], ctx=ctx)
        w = weight_sems(e, e.ctx, "merge")
        w_split, w_used = w[1], w[2][0]
        y_in = sems(nc, e.ctx, "y_in0", "y_in1")
        (conv,) = sems(nc, e.ctx, "y_split")
        CV = Steps(conv, [(s, b, k) for b in range(2) for k in range(KT) for s in ("hi", "lo")])
        hs = [slice(0, HALF), slice(HALF, SEQ)]
        S = []
        for b in range(2):
            sa, sv, sp_ = sems(nc, e.ctx, f"merge_act{b}", f"merge_vec{b}", f"merge_pe{b}")
            S.append((Steps(sa, [("gate", k, h) for k in range(2) for h in range(2)], True),
                      Steps(sv, [(n, k, h) for k in range(2) for h in range(2) for n in (("m",) if b == 0 else ("m", "sum"))], True),
                      Steps(sp_, [(n, k, h) for k in range(2) for n in ("gate", "y") for h in range(2)], True)))
        rounds = KT // 2
        block = ctx.enter_context(nc.Block())
        start_weights(e, block, NB_GA, 4 * KT, w)

        @block.tensor
        def _(pe):
            for b in range(2):
                A, V, PE = S[b]
                pe.sem_inc(PE.sem, PE.n)
                with pe.Fori(0, rounds) as i:
                    for k in range(2):
                        pe.wait_ge(w_split, i * 4 + (4 * rounds * b + 2 * k + 1))
                        pe.wait_ge(A.sem, A.done(("gate", k, 1), i, 1))
                        for h in range(2):
                            gemm(nc, e.ps[4 * k + h], e.whi[:, 0], e.wlo[:, 0], e.ahi, e.alo, range(KT), hs[h]).then_inc(PE.sem, PE.one(("gate", k, h)))
                        pe.wait_ge(w_split, i * 4 + (4 * rounds * b + 2 * k + 2))
                        if k == 0:
                            pe.wait_ge(CV.sem, CV.done(("lo", b, KT - 1)))
                        pe.wait_ge(V.sem, V.done(("m", k, 1), i, 1))
                        for h in range(2):
                            gemm(nc, e.ps[4 * k + 2 + h], e.whi[:, 1], e.wlo[:, 1], yhi, ylo, range(KT), hs[h]).then_inc(PE.sem, PE.one(("y", k, h)))
                PE.close()
                if b == 0:
                    pe.wait_ge(V.sem, V.done(("m", 1, 1), rounds - 1))

        @block.scalar
        def _(act):
            for b in range(2):
                A, V, PE = S[b]
                act.sem_inc(A.sem, A.n)
                if b == 1:
                    act.wait_ge(S[0][2].sem, S[0][2].done(("y", 1, 1), rounds - 1))
                for k in range(KT):
                    if k >= 2 or b == 1:
                        act.wait_ge(CV.sem, CV.done(("lo", b if k >= 2 else 0, (k - 2) % KT)))
                    act.dma_start(st[:, k % 2], (e.ya_d, e.yb_d)[b][k]).then_inc(y_in[k % 2], 16)
                with act.Fori(0, rounds) as i:
                    for k in range(2):
                        act.wait_ge(V.sem, V.done(("m" if b == 0 else "sum", k, 1), i, 1))
                        for h in range(2):
                            act.wait_ge(PE.sem, PE.done(("gate", k, h), i))
                            if h == 1:
                                act.sem_inc(w_used, 1)
                            nc.scalar.activation(sg[:, k, hs[h]], e.ps[4 * k + h], ACT.Sigmoid).then_inc(A.sem, A.one(("gate", k, h)))
                        act.wait_ge(PE.sem, PE.done(("y", k, 1), i))
                        act.sem_inc(w_used, 1)
                A.close()

        @block.vector
        def _(vec):
            tt = nc.vector.tensor_tensor
            for b in range(2):
                A, V, PE = S[b]
                vec.sem_inc(V.sem, V.n)
                for k in range(KT):
                    vec.wait_ge(y_in[k % 2], 16 * (b * KT // 2 + k // 2 + 1))
                    nc.vector.tensor_copy(yhi[:, k], st[:, k % 2]).then_inc(conv, CV.one(("hi", b, k)))
                    vec.wait_ge(CV.sem, CV.done(("hi", b, k)))
                    tt(ylo[:, k], st[:, k % 2], yhi[:, k].bitcast(F32), ALU.subtract).then_inc(conv, CV.one(("lo", b, k)))
                with vec.Fori(0, rounds) as i:
                    for k in range(2):
                        for h in range(2):
                            m = e.mo[:, bass.ds(i * 2 + k, 1), hs[h]].rearrange("p a t -> p (a t)")
                            vec.wait_ge(A.sem, A.done(("gate", k, h), i))
                            vec.wait_ge(PE.sem, PE.done(("y", k, h), i))
                            if b == 0:
                                tt(m, e.ps[4 * k + 2 + h], sg[:, k, hs[h]], ALU.mult).then_inc(V.sem, V.one(("m", k, h)))
                            else:
                                tt(sg[:, k, hs[h]], e.ps[4 * k + 2 + h], sg[:, k, hs[h]], ALU.mult).then_inc(V.sem, V.one(("m", k, h)))
                                vec.wait_ge(V.sem, V.done(("m", k, h), i))
                                tt(m, m, sg[:, k, hs[h]], ALU.add).then_inc(V.sem, V.one(("sum", k, h)))
                V.close()


def project_phase(e, tag, first, per_block, split_first):
    nc = e.nc
    kts = KT // per_block
    nb = 2 * per_block
    rounds = KT // nb
    with ExitStack() as ctx:
        w = weight_sems(e, e.ctx, tag)
        w_split, w_used = w[1], w[2][0]
        sa, sv, sp_, hi_done, lo_done = sems(nc, e.ctx, f"{tag}_act", f"{tag}_vec", f"{tag}_pe", f"{tag}_hi", f"{tag}_lo")
        A = Steps(sa, [(n, h) for n in range(nb) for h in range(2)], True)
        PE = Steps(sp_, [(n, h) for n in range(nb) for h in range(2)], True)
        block = ctx.enter_context(nc.Block())
        start_weights(e, block, first, KT // per_block, w)
        hs = [slice(0, HALF), slice(HALF, SEQ)]

        @block.vector
        def _(vec):
            if split_first:
                for k in range(KT):
                    vec.wait_ge(hi_done, k + 1)
                    nc.vector.tensor_tensor(e.alo[:, k], e.mo[:, k], e.ahi[:, k].bitcast(F32), ALU.subtract).then_inc(lo_done, 1)

        @block.scalar
        def _(act):
            if split_first:
                for k in range(KT):
                    nc.scalar.activation(e.ahi[:, k], e.mo[:, k], ACT.Copy).then_inc(hi_done, 1)
                act.wait_ge(lo_done, KT)
            act.sem_inc(sa, A.n)
            with act.Fori(0, rounds) as i:
                for n in range(nb):
                    for h in range(2):
                        act.wait_ge(PE.sem, PE.done((n, h), i))
                        if h == 1 and n % per_block == per_block - 1:
                            act.sem_inc(w_used, 1)
                        dst = e.mo[:, bass.ds(i * nb + n, 1), hs[h]].rearrange("p a t -> p (a t)")
                        nc.scalar.activation(dst, e.ps[2 * n + h], ACT.Copy).then_inc(sa, A.one((n, h)))
            A.close()

        @block.tensor
        def _(pe):
            if split_first:
                pe.wait_ge(lo_done, KT)
            pe.sem_inc(sp_, PE.n)
            with pe.Fori(0, rounds) as i:
                for n in range(nb):
                    s, off = n // per_block, n % per_block * kts
                    pe.wait_ge(w_split, i * 2 + s + 1)
                    pe.wait_ge(A.sem, A.done((n, 1), i, 1))
                    for h in range(2):
                        gemm(nc, e.ps[2 * n + h], e.whi[:, s, off:off + kts], e.wlo[:, s, off:off + kts], e.ahi, e.alo, range(kts), hs[h]).then_inc(sp_, PE.one((n, h)))
            PE.close()


def finish_phase(e, tag, g_row, x_in, x_out, gain):
    nc = e.nc
    with ExitStack() as ctx:
        tok = e.sb(f"{tag}_tok", [P, NT, D], ctx=ctx)
        xr = e.sb(f"{tag}_x", [P, NT, D], ctx=ctx)
        junk = e.sb(f"{tag}_squares", [P, D], ctx=ctx)
        stage = e.sb(f"{tag}_stage", [P, 2, HALF], ctx=ctx)
        gpost = e.sb(f"{tag}_gain", [P, D], ctx=ctx)
        st = e.sb(f"{tag}_stats", [P, 32], ctx=ctx)
        sa, sv, sp_, g_in = sems(nc, e.ctx, f"{tag}_act", f"{tag}_vec", f"{tag}_pe", f"{tag}_g_in")
        x_ld, x_st = e.x_loaded, e.x_stored
        ld_value, st_value = 16 * (g_row + 2), 16 * (g_row + 1)
        na, nv, np_ = norm_steps("n", NT) if gain is not None else ([], [], [])
        A = Steps(sa, [(n, i) for i in range(NT) for n in ("cp0", "cp1", "psq")] + ["psd"] + na)
        V = Steps(sv, ["pms", "prs"] + [(n, i) for i in range(NT) for n in ("g", "res")] + nv)
        PE = Steps(sp_, [("tok", i) for i in range(NT)] + np_)
        block = ctx.enter_context(nc.Block())

        @block.sync
        def _(sp):
            sp.dma_start(gpost[:], bass.AP(tensor=e.g_rows.tensor, offset=g_row * D, ap=[[0, P], [1, D]])).then_inc(g_in, 16)
            for i in range(NT):
                sp.dma_start(xr[:, i], x_in[i * P:(i + 1) * P, :]).then_inc(x_ld[i], 16)
            for i in range(NT):
                sp.wait_ge(V.sem, V.done(("res", i)))
                sp.dma_start(x_out[i * P:(i + 1) * P, :], tok[:, i]).then_inc(x_st[i], 16)
            for i in range(NT):
                sp.wait_ge(x_st[i], st_value)

        @block.tensor
        def _(pe):
            for i in range(NT):
                if i >= 4:
                    pe.wait_ge(A.sem, A.done(("cp1", i - 4)))
                for kt in range(KT):
                    last = nc.tensor.transpose(e.ps[2 * (i % 4) + kt // 4][:, kt % 4 * P:(kt % 4 + 1) * P], e.mo[:, kt, i * P:(i + 1) * P], e.ident)
                last.then_inc(sp_, PE.one(("tok", i)))
            if gain is not None:
                pe.wait_ge(A.sem, A.done(("cp1", NT - 1)))
                norm_pe(e, pe, A, V, PE, "n", tok, NT)
            PE.close()

        @block.scalar
        def _(act):
            for i in range(NT):
                act.wait_ge(PE.sem, PE.done(("tok", i)))
                for h in range(2):
                    nc.scalar.activation(tok[:, i, h * HALF:(h + 1) * HALF], e.ps[2 * (i % 4) + h], ACT.Copy).then_inc(sa, A.one((f"cp{h}", i)))
                act.wait_ge(A.sem, A.done(("cp1", i)))
                nc.scalar.activation(junk[:], tok[:, i], ACT.Square, accum_out=st[:, 16 + i:17 + i]).then_inc(sa, A.one(("psq", i)))
            act.wait_ge(V.sem, V.done("pms"))
            nc.scalar.activation(st[:, 24:32], st[:, 16:24], ACT.Sqrt).then_inc(sa, A.one("psd"))
            if gain is not None:
                norm_act(e, act, A, V, PE, "n", tok, NT, st, junk[:], stage, gain, lambda eng, i: eng.wait_ge(V.sem, V.done(("res", i))))
            A.close()

        @block.vector
        def _(vec):
            vec.wait_ge(A.sem, A.done(("psq", NT - 1)))
            nc.vector.tensor_scalar(st[:, 16:24], st[:, 16:24], 1.0 / D, EPS, ALU.mult, ALU.add).then_inc(sv, V.one("pms"))
            vec.wait_ge(A.sem, A.done("psd"))
            nc.vector.reciprocal(st[:, 16:24], st[:, 24:32]).then_inc(sv, V.one("prs"))
            vec.wait_ge(g_in, 16)
            vec.wait_ge(V.sem, V.done("prs"))
            for i in range(NT):
                nc.vector.scalar_tensor_tensor(out=tok[:, i], in0=tok[:, i], scalar=st[:, 16 + i:17 + i], in1=gpost[:],
                                               op0=ALU.mult, op1=ALU.mult).then_inc(sv, V.one(("g", i)))
                vec.wait_ge(x_ld[i], ld_value)
                vec.wait_ge(V.sem, V.done(("g", i)))
                nc.vector.tensor_tensor(tok[:, i], tok[:, i], xr[:, i], ALU.add).then_inc(sv, V.one(("res", i)))
            if gain is not None:
                norm_vec(e, vec, A, V, "n", tok, NT, st, stage, e.ahi, e.alo, lambda eng, i: eng.wait_ge(x_st[i], st_value))
            V.close()


def cross_phase(e):
    nc = e.nc
    with ExitStack() as ctx:
        sb = lambda name, shape, dt=F32: e.sb(name, shape, dt, ctx)
        mt = sb("mem_tok", [P, 2, D])
        mhi = sb("mem_hi", [P, KT, MEM], F32R)
        mlo = sb("mem_lo", [P, KT, MEM], F32R)
        km = sb("mem_k", [P, MH, MEM])
        vmc = sb("mem_v_cm", [P, MH, MEM])
        vm = sb("mem_v_tok", [P, 2, MH * P])
        q = sb("cross_q", [P, MH, SEQ])
        o = sb("cross_o", [P, MH, SEQ])
        pr = sb("cross_probs", [P, 2, MEM])
        pT = sb("cross_probs_T", [P, 2, MEM])
        small = sb("cross_small", [P, 8])
        junk = sb("cross_squares", [P, D])
        stage = sb("cross_stage", [P, 2, HALF])
        st = sb("cross_stats", [P, 16])
        w = weight_sems(e, e.ctx, "cross")
        w_split, w_used = w[1], w[2][0]
        m_in = sems(nc, e.ctx, "mem_in0", "mem_in1")
        sa, sv, sp_ = sems(nc, e.ctx, "cross_act", "cross_vec", "cross_pe")
        na, nv, np_ = norm_steps("m", 2)
        NUC = MH * NT
        kv = [("kv", n) for n in range(8)]
        qs = [("q", n, h) for n in range(MH) for h in range(2)]
        a_names, v_names, p_names = na + kv + qs + ["vm0", "vm1"], list(nv), np_ + kv + qs + ["vm0", "vm1"]
        for u in range(NUC + 2):
            if u < NUC:
                p_names += [("s", u)]
                v_names += [("mx", u), ("nmx", u)]
                a_names += [("exp", u)]
            if 1 <= u <= NUC:
                v_names += [("rin", u - 1), ("pn", u - 1)]
                p_names += [("pT", u - 1)]
                a_names += [("pT", u - 1)]
            if u >= 2:
                p_names += [("out", u - 2)]
                a_names += [("out", u - 2)]
                if (u - 2) % NT == NT - 1:
                    v_names += [("hi", (u - 2) // NT), ("lo", (u - 2) // NT)]
        A, V, PE = Steps(sa, a_names), Steps(sv, v_names), Steps(sp_, p_names)
        hs = [slice(0, HALF), slice(HALF, SEQ)]
        block = ctx.enter_context(nc.Block())
        start_weights(e, block, NB_MEM, 8 + MH, w)

        @block.tensor
        def _(pe):
            norm_pe(e, pe, A, V, PE, "m", mt, 2)
            for n in range(8):
                pe.wait_ge(w_split, n + 1)
                if n == 0:
                    pe.wait_ge(V.sem, V.done(("m", "lo", KT - 1, 0)))
                if n >= 4:
                    pe.wait_ge(A.sem, A.done(("kv", n - 4)))
                gemm(nc, e.ps[4 + n % 4][:, 0:MEM], e.whi[:, n % 2], e.wlo[:, n % 2], mhi, mlo, range(KT), slice(0, MEM)).then_inc(sp_, PE.one(("kv", n)))
            for n in range(MH):
                pe.wait_ge(w_split, 8 + n + 1)
                pe.wait_ge(A.sem, A.done(("q", n - 2, 1))) if n >= 2 else pe.wait_ge(A.sem, A.done(("m", "scaled", KT - 1, 0)))
                for h in range(2):
                    gemm(nc, e.ps[2 * (n % 2) + h], e.whi[:, n % 2], e.wlo[:, n % 2], e.ahi, e.alo, range(KT), hs[h]).then_inc(sp_, PE.one(("q", n, h)))
            for g in range(2):
                pe.wait_ge(A.sem, A.done(("kv", 7)))
                for n in range(MH):
                    last = nc.tensor.transpose(e.ps[4 + g][:, n * P:(n + 1) * P], vmc[:, n, g * P:(g + 1) * P], e.ident)
                last.then_inc(sp_, PE.one(f"vm{g}"))
            for u in range(NUC + 2):
                if u < NUC:
                    hd, i = u // NT, u % NT
                    if u == 0:
                        pe.wait_ge(A.sem, A.done(("q", MH - 1, 1)))
                    if u >= 2:
                        pe.wait_ge(A.sem, A.done(("exp", u - 2)))
                    nc.tensor.matmul(e.ps[u % 2][:, 0:MEM], q[:, hd, i * P:(i + 1) * P], km[:, hd, :], start=True, stop=True).then_inc(sp_, PE.one(("s", u)))
                if 1 <= u <= NUC:
                    v = u - 1
                    pe.wait_ge(V.sem, V.done(("pn", v)))
                    if v >= 2:
                        pe.wait_ge(A.sem, A.done(("pT", v - 2)))
                    for t in range(2):
                        last = nc.tensor.transpose(e.ps[2 + v % 2][:, t * P:(t + 1) * P], pr[:, v % 2, t * P:(t + 1) * P], e.ident)
                    last.then_inc(sp_, PE.one(("pT", v)))
                if u >= 2:
                    v = u - 2
                    hd = v // NT
                    pe.wait_ge(A.sem, A.done(("pT", v)))
                    if v == 0:
                        pe.wait_ge(A.sem, A.done("vm1"))
                    if v >= 2:
                        pe.wait_ge(A.sem, A.done(("out", v - 2)))
                    for t in range(2):
                        last = nc.tensor.matmul(e.ps[4 + v % 2][:, 0:P], vm[:, t, hd * P:(hd + 1) * P], pT[:, v % 2, t * P:(t + 1) * P], start=t == 0, stop=t == 1)
                    last.then_inc(sp_, PE.one(("out", v)))
            PE.close()

        @block.scalar
        def _(act):
            for i in range(2):
                act.dma_start(mt[:, i], e.mem[i * P:(i + 1) * P, :]).then_inc(m_in[i], 16)
            norm_act(e, act, A, V, PE, "m", mt, 2, st, junk[:], stage, e.par[:, Q_MEM:Q_MEM + KT], lambda eng, i: eng.wait_ge(m_in[i], 16))
            for n in range(8):
                act.wait_ge(PE.sem, PE.done(("kv", n)))
                act.sem_inc(w_used, 1)
                dst = km[:, n] if n < 4 else vmc[:, n - 4]
                nc.scalar.activation(dst, e.ps[4 + n % 4][:, 0:MEM], ACT.Copy).then_inc(sa, A.one(("kv", n)))
            for n in range(MH):
                for h in range(2):
                    act.wait_ge(PE.sem, PE.done(("q", n, h)))
                    if h == 1:
                        act.sem_inc(w_used, 1)
                    nc.scalar.activation(q[:, n, hs[h]], e.ps[2 * (n % 2) + h], ACT.Copy, scale=float(P) ** -0.5).then_inc(sa, A.one(("q", n, h)))
            for g in range(2):
                act.wait_ge(PE.sem, PE.done(f"vm{g}"))
                nc.scalar.activation(vm[:, g], e.ps[4 + g], ACT.Copy).then_inc(sa, A.one(f"vm{g}"))
            for u in range(NUC + 2):
                if u < NUC:
                    act.wait_ge(V.sem, V.done(("nmx", u)))
                    if u >= 2:
                        act.wait_ge(PE.sem, PE.done(("pT", u - 2)))
                    nc.scalar.activation(pr[:, u % 2], e.ps[u % 2][:, 0:MEM], ACT.Exp, bias=small[:, u % 2:u % 2 + 1],
                                         accum_out=small[:, 2 + u % 2:3 + u % 2]).then_inc(sa, A.one(("exp", u)))
                if 1 <= u <= NUC:
                    v = u - 1
                    act.wait_ge(PE.sem, PE.done(("pT", v)))
                    if v >= 2:
                        act.wait_ge(PE.sem, PE.done(("out", v - 2)))
                    nc.scalar.activation(pT[:, v % 2], e.ps[2 + v % 2][:, 0:MEM], ACT.Copy).then_inc(sa, A.one(("pT", v)))
                if u >= 2:
                    v = u - 2
                    hd, i = v // NT, v % NT
                    act.wait_ge(PE.sem, PE.done(("out", v)))
                    nc.scalar.activation(o[:, hd, i * P:(i + 1) * P], e.ps[4 + v % 2][:, 0:P], ACT.Copy).then_inc(sa, A.one(("out", v)))
            A.close()

        @block.vector
        def _(vec):
            norm_vec(e, vec, A, V, "m", mt, 2, st, stage, mhi, mlo)
            for u in range(NUC + 2):
                if u < NUC:
                    vec.wait_ge(PE.sem, PE.done(("s", u)))
                    nc.vector.reduce_max(small[:, 4 + u % 2:5 + u % 2], e.ps[u % 2][:, 0:MEM], mybir.AxisListType.X).then_inc(sv, V.one(("mx", u)))
                    vec.wait_ge(V.sem, V.done(("mx", u)))
                    if u >= 2:
                        vec.wait_ge(A.sem, A.done(("exp", u - 2)))
                    nc.vector.tensor_scalar(small[:, u % 2:u % 2 + 1], small[:, 4 + u % 2:5 + u % 2], -1.0, None, ALU.mult).then_inc(sv, V.one(("nmx", u)))
                if 1 <= u <= NUC:
                    v = u - 1
                    vec.wait_ge(A.sem, A.done(("exp", v)))
                    nc.vector.reciprocal(small[:, 6 + v % 2:7 + v % 2], small[:, 2 + v % 2:3 + v % 2]).then_inc(sv, V.one(("rin", v)))
                    vec.wait_ge(V.sem, V.done(("rin", v)))
                    nc.vector.tensor_scalar(pr[:, v % 2], pr[:, v % 2], small[:, 6 + v % 2:7 + v % 2], None, ALU.mult).then_inc(sv, V.one(("pn", v)))
                if u >= 2 and (u - 2) % NT == NT - 1:
                    hd = (u - 2) // NT
                    vec.wait_ge(A.sem, A.done(("out", u - 2)))
                    nc.vector.tensor_copy(e.ahi[:, hd], o[:, hd]).then_inc(sv, V.one(("hi", hd)))
                    vec.wait_ge(V.sem, V.done(("hi", hd)))
                    nc.vector.tensor_tensor(e.alo[:, hd], o[:, hd], e.ahi[:, hd].bitcast(F32), ALU.subtract).then_inc(sv, V.one(("lo", hd)))
            V.close()


def ffn_phase(e):
    nc = e.nc
    with ExitStack() as ctx:
        ghi = e.sb("hidden_hi", [P, KT, SEQ], F32R, ctx)
        glo = e.sb("hidden_lo", [P, KT, SEQ], F32R, ctx)
        sg = e.sb("silu", [P, 2, SEQ], ctx=ctx)
        w = weight_sems(e, e.ctx, "ffn")
        w_split, w_used = w[1], w[2][0]
        hs = [slice(0, HALF), slice(HALF, SEQ)]
        S = []
        for n in range(len(FGROUPS)):
            s = sems(nc, e.ctx, *[f"ffn_{x}{n}" for x in ("in_act", "in_vec", "in_pe", "out_vec", "out_pe")])
            kh = [(k, h) for k in range(2) for h in range(2)]
            S.append((Steps(s[0], [("silu",) + x for x in kh], True),
                      Steps(s[1], [(m,) + x for x in kh for m in ("prod", "hi", "lo")], True),
                      Steps(s[2], [(m, k, h) for k in range(2) for m in ("gate", "up") for h in range(2)], True),
                      Steps(s[3], [("acc",) + x for x in kh], True),
                      Steps(s[4], [("out",) + x for x in kh], True)))
        block = ctx.enter_context(nc.Block())
        start_weights(e, block, NB_FFN, 2 * FT + KT * len(FGROUPS), w)

        @block.tensor
        def _(pe):
            at = 0
            for n, (f0, nf) in enumerate(FGROUPS):
                A, V, PE, OV, OPE = S[n]
                pe.sem_inc(PE.sem, PE.n)
                with pe.Fori(0, nf // 2) as i:
                    for k in range(2):
                        for m, name in enumerate(("gate", "up")):
                            pe.wait_ge(w_split, i * 4 + (at + 2 * k + m + 1))
                            pe.wait_ge(A.sem, A.done(("silu", k, 1), i, 1)) if m == 0 else pe.wait_ge(V.sem, V.done(("prod", k, 1), i, 1))
                            for h in range(2):
                                gemm(nc, e.ps[4 * k + 2 * m + h], e.whi[:, m], e.wlo[:, m], e.ahi, e.alo, range(KT), hs[h]).then_inc(PE.sem, PE.one((name, k, h)))
                PE.close()
                at += 2 * nf
                pe.wait_ge(V.sem, V.done(("lo", 1, 1), nf // 2 - 1))
                pe.sem_inc(OPE.sem, OPE.n)
                with pe.Fori(0, KT // 2) as i:
                    for k in range(2):
                        pe.wait_ge(w_split, i * 2 + (at + k + 1))
                        pe.wait_ge(OV.sem, OV.done(("acc", k, 1), i, 1))
                        for h in range(2):
                            gemm(nc, e.ps[2 * k + h], e.whi[:, k], e.wlo[:, k], ghi, glo, range(nf), hs[h]).then_inc(OPE.sem, OPE.one(("out", k, h)))
                OPE.close()
                at += KT
                pe.wait_ge(OV.sem, OV.done(("acc", 1, 1), KT // 2 - 1))

        @block.scalar
        def _(act):
            for n, (f0, nf) in enumerate(FGROUPS):
                A, V, PE, OV, OPE = S[n]
                act.sem_inc(A.sem, A.n)
                with act.Fori(0, nf // 2) as i:
                    for k in range(2):
                        act.wait_ge(V.sem, V.done(("lo", k, 1), i, 1))
                        for h in range(2):
                            act.wait_ge(PE.sem, PE.done(("gate", k, h), i))
                            if h == 1:
                                act.sem_inc(w_used, 1)
                            nc.scalar.activation(sg[:, k, hs[h]], e.ps[4 * k + h], ACT.Silu).then_inc(A.sem, A.one(("silu", k, h)))
                        act.wait_ge(PE.sem, PE.done(("up", k, 1), i))
                        act.sem_inc(w_used, 1)
                A.close()
                with act.Fori(0, KT // 2) as i:
                    for k in range(2):
                        act.wait_ge(OPE.sem, OPE.done(("out", k, 1), i))
                        act.sem_inc(w_used, 1)

        @block.vector
        def _(vec):
            tt = nc.vector.tensor_tensor
            for n, (f0, nf) in enumerate(FGROUPS):
                A, V, PE, OV, OPE = S[n]
                vec.sem_inc(V.sem, V.n)
                vec.sem_inc(OV.sem, OV.n)
                if n > 0:
                    vec.wait_ge(S[n - 1][4].sem, S[n - 1][4].done(("out", 1, 1), KT // 2 - 1))
                with vec.Fori(0, nf // 2) as i:
                    for k in range(2):
                        for h in range(2):
                            vec.wait_ge(A.sem, A.done(("silu", k, h), i))
                            vec.wait_ge(PE.sem, PE.done(("up", k, h), i))
                            g = sg[:, k, hs[h]]
                            hi, lo = (t[:, bass.ds(i * 2 + k, 1), hs[h]].rearrange("p a t -> p (a t)") for t in (ghi, glo))
                            tt(g, e.ps[4 * k + 2 + h], g, ALU.mult).then_inc(V.sem, V.one(("prod", k, h)))
                            vec.wait_ge(V.sem, V.done(("prod", k, h), i))
                            nc.vector.tensor_copy(hi, g).then_inc(V.sem, V.one(("hi", k, h)))
                            vec.wait_ge(V.sem, V.done(("hi", k, h), i))
                            tt(lo, g, hi.bitcast(F32), ALU.subtract).then_inc(V.sem, V.one(("lo", k, h)))
                V.close()
                with vec.Fori(0, KT // 2) as i:
                    for k in range(2):
                        for h in range(2):
                            m = e.mo[:, bass.ds(i * 2 + k, 1), hs[h]].rearrange("p a t -> p (a t)")
                            vec.wait_ge(OPE.sem, OPE.done(("out", k, h), i))
                            if n == 0:
                                nc.vector.tensor_copy(m, e.ps[2 * k + h]).then_inc(OV.sem, OV.one(("acc", k, h)))
                            else:
                                tt(m, e.ps[2 * k + h], m, ALU.add).then_inc(OV.sem, OV.one(("acc", k, h)))
                OV.close()


def blocks_of(np, w):
    k, n = w.shape
    return w.reshape(k // P, P, n // P, P).transpose(2, 1, 0, 3)


def lay_out(np, i):
    a = {k: np.ascontiguousarray(v[0]) if k not in ("x", "mem") else v[0] for k, v in i.items()}
    win = a["w_in"]
    w = RWKV = 1024
    col = lambda s, n: blocks_of(np, win[:, s:s + n])
    r, k, v = (col(w * n, w) for n in range(3))
    lora = np.zeros((D, 3 * P), win.dtype)
    lora[:, 0:288] = win[:, 3072:3360]
    aq, ak, av, ga, gb = (col(3360 + w * n, w) for n in range(5))
    heads = np.stack([v, aq, av, ak, np.roll(r, -1, 0), np.roll(k, -1, 0)], 1).reshape(6 * HP, P, KT, P)
    pair = lambda g, y: np.stack([g, blocks_of(np, y)], 1).reshape(2 * KT, P, KT, P)
    wo = blocks_of(np, a["w_o_mem"])
    wo = wo.reshape(4, 2, P, MH, P).transpose(0, 2, 1, 3, 4).reshape(4, P, KT, P)
    gate = blocks_of(np, a["w_ffn_in"][:, :FFN])
    up = blocks_of(np, a["w_ffn_in"][:, FFN:])
    down = blocks_of(np, a["w_ffn_out"])
    ffn = []
    for f0, nf in FGROUPS:
        ffn.append(np.stack([gate[f0:f0 + nf], up[f0:f0 + nf]], 1).reshape(2 * nf, P, KT, P))
        d = np.zeros((KT, P, KT, P), win.dtype)
        d[:, :, :nf] = down[:, :, f0:f0 + nf]
        ffn.append(d)
    wblocks = np.concatenate([blocks_of(np, lora), r[0:1], k[0:1], heads, pair(ga, a["w_branch_a"]), pair(gb, a["w_branch_b"]),
                              blocks_of(np, a["w_out"]), blocks_of(np, a["w_kv_mem"]), blocks_of(np, a["w_q_mem"]), wo] + ffn)
    lora_up = np.zeros((HP + 1, P, P), win.dtype)
    lora_up[:HP] = np.concatenate([a["decay_up"], a["iclr_up"]]).reshape(P, HP, P).transpose(1, 0, 2)
    gu = np.zeros((2, P, w), win.dtype)
    gu[0], gu[1, :32] = a["gate_up"][:P], a["gate_up"][P:]
    gate_up2 = gu.reshape(2, P, HP, P).transpose(2, 1, 0, 3)
    sm = a["shift_mix"]
    rows = np.stack([sm[0:w], sm[w:2 * w], sm[2 * w:3 * w], a["decay_base"], a["iclr_base"], a["key_norm_scale"],
                     a["key_iclr_scale"], a["bonus_scale"].reshape(-1), a["lnx_w"], a["lnx_b"]])
    par = np.zeros((P, Q_N), win.dtype)
    par[:, :Q_PRE] = rows.reshape(PP, HP, P).transpose(2, 1, 0).reshape(P, HP * PP)
    for at, name in ((Q_PRE, "g_pre_mix"), (Q_CROSS, "g_pre_cross"), (Q_FFN, "g_pre_ffn"), (Q_MEM, "g_mem")):
        par[:, at:at + KT] = a[name].reshape(KT, P).T
    par[:, Q_LORA] = sm[3072:3200]
    par[:, Q_LORA + 1] = sm[3200:3328]
    par[:32, Q_LORA + 2] = sm[3328:3360]
    return {
        "x": a["x"], "mem": a["mem"], "wblocks": wblocks, "lora_up": lora_up, "gate_up2": gate_up2, "params": par,
        "consts": constants(np), "rel_rev": a["rel_bias"][:, ::-1],
        "g_rows": np.stack([a["g_post_mix"], a["g_post_cross"], a["g_post_ffn"]]),
    }


def constants(np):
    c = np.zeros((P, C_N), np.float32)
    s, t = np.arange(P)[:, None] % C, np.arange(C)[None, :]
    c[:, C_ID:C_ID + P] = np.eye(P)
    c[:, C_MASK:C_MASK + C] = s < t
    c[:, C_MASK + C:C_MASK + P] = s <= t
    c[:, C_EYE:C_EYE + C] = s == t
    lower = lambda row, colm, m: (row // (2 * m) == colm // (2 * m)) & (row // m % 2 == 1) & (colm // m % 2 == 0)
    c[:, C_NL1:C_NL1 + C] = -1.0 * lower(s, t, 1)
    c[:, C_NL1T:C_NL1T + C] = -1.0 * lower(t, s, 1)
    for n, m in enumerate(LEVELS):
        c[:, C_LV + C * n:C_LV + C * (n + 1)] = 1.0 * (s == t) - lower(s, t, m)
    c[:, C_ONES:C_ONES + P] = np.arange(P)[:, None] // C == np.arange(P)[None, :] // C
    c[:, C_RST:C_RST + SCAN] = np.arange(SCAN)[None, :] % C != 0
    return c


def kernel(**inputs):
    import numpy as np
    from concourse import bacc
    from concourse.bass_utils import run_bass_kernel_spmd

    laid = lay_out(np, {k: np.asarray(v) for k, v in inputs.items()})
    nc = bacc.Bacc("TRN2", target_bir_lowering=False, num_devices=1)
    arrays, args = {}, []
    for name, a in laid.items():
        arrays[f"in_{name}"] = np.ascontiguousarray(a)
        args.append(nc.dram_tensor(f"in_{name}", a.shape, mybir.dt.from_np(a.dtype), kind="ExternalInput").ap())
    out = nc.dram_tensor("out", (SEQ, D), F32, kind="ExternalOutput").ap()
    hybrid_block(nc, *args, out)
    r = run_bass_kernel_spmd(nc, [arrays], core_ids=[0])
    return r.results[0]["out"].reshape(1, SEQ, D)
```

```python
from contextlib import ExitStack

import concourse.bass as bass
from concourse import mybir

P = 128
D = 1024
SEQ = 1024
KT = D // P
NT = SEQ // P
HALF = 512
HP = 8
C = 64
NC_ = SEQ // C
G = 2
GC = NC_ // G
MEM = 256
MH = 4
FFN = 2816
FT = FFN // P
FGROUPS = [(0, 8), (8, 8), (16, 6)]
BANDT = 5
BAND = BANDT * P
EXT = 768
PP = 10
EXP_HALF = 0.6065306597126334
LEVELS = [2, 4, 8, 16, 32]
EPS = 1e-6
SCAN = 4 * C
GN_EPS = 64e-5
MASKED = -1e30

F32 = mybir.dt.float32
F32R = mybir.dt.float32r
ALU = mybir.AluOpType
ACT = mybir.ActivationFunctionType

C_ID = 0
C_MASK = C_ID + P
C_EYE = C_MASK + P
C_NL1 = C_EYE + C
C_NL1T = C_NL1 + C
C_LV = C_NL1T + C
C_ONES = C_LV + C * len(LEVELS)
C_RST = C_ONES + P
C_CEN = C_RST + SCAN
C_N = C_CEN + C

(MIX_R, MIX_K, MIX_V, DEC_B, ICL_B, KNS, KIS, BON, LNW, LNB) = range(PP)
Q_PRE = HP * PP
Q_CROSS = Q_PRE + KT
Q_FFN = Q_CROSS + KT
Q_MEM = Q_FFN + KT
Q_LORA = Q_MEM + KT
Q_N = Q_LORA + 3
OM_R, OM_K, OM_V, OM_KIS = PP, PP + 1, PP + 2, PP + 3

NB_LORA = 0
NB_HEAD = 3
NB_GA = NB_HEAD + 2 + 6 * HP
NB_OUT = NB_GA + 4 * KT - 2
NB_MEM = NB_OUT + KT
NB_O = NB_MEM + 3 * MH
NB_FFN = NB_O + 4
NB_N = NB_FFN + 2 * FT + 8 * len(FGROUPS)


class Steps:

    def __init__(self, sem, names, looped=False):
        self.sem, self.n, self.looped = sem, len(names), looped
        self.index = {name: i + 1 for i, name in enumerate(names)}
        assert len(self.index) == self.n
        self.at = 0

    def done(self, name, rnd=0, back=0):
        return (rnd + 1 - back) * self.n + self.index[name] if self.looped else self.index[name]

    def one(self, name):
        self.at += 1
        assert self.index[name] == self.at, (name, self.at)
        return 1

    def close(self):
        assert self.at == self.n, (self.at, self.n)


def settle(eng, passed):
    eng.sem_inc(passed, 1)


def load_block(sp, e, block, slot, index=None):
    src = e.wblocks[block] if index is None else e.wblocks[bass.ds(index, 1)].rearrange("a p k m -> p (a k) m")
    sp.dma_start(e.raw[:, slot], src).then_inc(e.w_loaded[slot], 16)


def split_block(pool, e, slot, loaded, split_hi, both=True):
    pool.wait_ge(e.w_loaded[slot], loaded)
    settle(pool, e.pool_passed)
    pool.tensor_copy(e.whi[:, slot], e.raw[:, slot]).then_inc(e.w_split_hi, 1)
    if not both:
        return
    pool.wait_ge(e.w_split_hi, split_hi)
    pool.tensor_tensor(e.wlo[:, slot], e.raw[:, slot], e.whi[:, slot].bitcast(F32), ALU.subtract).then_inc(e.w_split, 1)


def low_block(vec, e, slot, split_hi):
    vec.wait_ge(e.w_split_hi, split_hi)
    vec.tensor_tensor(e.wlo[:, slot], e.raw[:, slot], e.whi[:, slot].bitcast(F32), ALU.subtract).then_inc(e.w_split, 1)


def start_weights(e, block, first, count, both=True):
    load_to = min(first + count + 2, NB_N)
    split_from, split_to = max(first + 1, 2), min(first + count + 1, NB_N)

    @block.sync
    def _(sp):
        b = first + 2
        with sp.Fori(0, (load_to - b) // 2) as i:
            for s in range(2):
                sp.wait_ge(e.w_split, i * 2 + (b + s - 1))
                load_block(sp, e, b + s, (b + s) % 2, i * 2 + (b + s))
        if (load_to - b) % 2:
            sp.wait_ge(e.w_split, load_to - 2)
            load_block(sp, e, load_to - 1, (load_to - 1) % 2)

    @block.gpsimd
    def _(pool):
        b = split_from
        with pool.Fori(0, (split_to - b) // 2) as i:
            for s in range(2):
                pool.wait_ge(e.w_used, i * 2 + (b + s - 1))
                split_block(pool, e, (b + s) % 2, i * 16 + 16 * ((b + s) // 2 + 1), i * 2 + (b + s + 1), both)
        if (split_to - b) % 2:
            pool.wait_ge(e.w_used, split_to - 2)
            split_block(pool, e, (split_to - 1) % 2, 16 * ((split_to - 1) // 2 + 1), split_to, both)


def mm3(nc, out, whi, wlo, ahi, alo, start, stop):
    nc.tensor.matmul(out, whi, ahi, start=start, stop=False)
    nc.tensor.matmul(out, whi, alo, start=False, stop=False)
    return nc.tensor.matmul(out, wlo, ahi, start=False, stop=stop)


def gemm(nc, out, whi, wlo, ahi, alo, kts, cols):
    last = None
    for n, kt in enumerate(kts):
        last = mm3(nc, out, whi[:, n], wlo[:, n], ahi[:, kt, cols], alo[:, kt, cols], n == 0, n == len(kts) - 1)
    return last


def hybrid_block(nc, x, mem, wblocks, lora_up, gate_up2, params, consts, rel_rev, g_rows, out):
    ctx = ExitStack()
    with ctx:
        env = Env(nc, ctx)
        e = env
        e.x, e.mem, e.wblocks, e.lora_up, e.gate_up2 = x, mem, wblocks, lora_up, gate_up2
        e.params_d, e.consts_d, e.rel_rev, e.g_rows, e.out = params, consts, rel_rev, g_rows, out
        dram = lambda name, shape: nc.dram_tensor(name, shape, F32, kind="Internal").ap()
        e.ya_d = dram("ya_scratch", (HP, P, SEQ))
        e.yb_d = dram("yb_scratch", (HP, P, SEQ))
        e.ext_d = dram("ext_scratch", (2 * HP, EXT))
        e.bias_d = dram("bias_scratch", (2 * HP, P, BAND))
        e.x1_d = dram("x1_scratch", (SEQ, D))
        e.x2_d = dram("x2_scratch", (SEQ, D))
        e.consts = e.sb("consts", [P, C_N])
        e.par = e.sb("par", [P, Q_N])
        e.ahi = e.sb("act_hi", [P, KT, SEQ], F32R)
        e.alo = e.sb("act_lo", [P, KT, SEQ], F32R)
        e.raw = e.sb("w_raw", [P, 2, KT, P])
        e.whi = e.sb("w_hi", [P, 2, KT, P], F32R)
        e.wlo = e.sb("w_lo", [P, 2, KT, P], F32R)
        psum = ctx.enter_context(nc.psum_tensor("banks", [P, 8 * HALF], F32))
        e.banks = psum
        e.ps = [psum[:, b * HALF:(b + 1) * HALF] for b in range(8)]
        e.x_loaded = sems(nc, ctx, *[f"x_loaded{i}" for i in range(NT)])
        e.x_stored = sems(nc, ctx, *[f"x_stored{i}" for i in range(NT)])
        e.w_loaded = sems(nc, ctx, "w_loaded0", "w_loaded1")
        e.w_split, e.w_split_hi, e.w_used, e.pool_passed = sems(nc, ctx, "w_split", "w_split_hi", "w_used", "pool_passed")
        e.ident = e.consts[:, C_ID:C_ID + P]
        norm_phase(e)
        mix_phase(e)
        e.mo = e.sb("mixed", [P, KT, SEQ])
        merge_phase(e)
        project_phase(e, "out", NB_OUT, 1, True)
        finish_phase(e, "mixfin", 0, e.x, e.x1_d, e.par[:, Q_CROSS:Q_CROSS + KT])
        cross_phase(e)
        project_phase(e, "cross_o", NB_O, 2, False)
        finish_phase(e, "crossfin", 1, e.x1_d, e.x2_d, e.par[:, Q_FFN:Q_FFN + KT])
        ffn_phase(e)
        finish_phase(e, "ffnfin", 2, e.x2_d, e.out, None)


class Env:

    def __init__(self, nc, ctx):
        self.nc, self.ctx = nc, ctx

    def sb(self, name, shape, dt=F32, ctx=None):
        return (ctx or self.ctx).enter_context(self.nc.sbuf_tensor(name, shape, dt))


def sems(nc, ctx, *names):
    return [ctx.enter_context(nc.semaphore(n)) for n in names]


class Norm:

    def __init__(self, e, tag, x, tiles, st, junk, gain, hi, lo, A, V, PE, bank0=0, banks=8, xn=None):
        self.e, self.tag, self.x, self.tiles, self.st, self.junk, self.gain = e, tag, x, tiles, st, junk, gain
        self.hi, self.lo, self.A, self.V, self.PE, self.bank0, self.banks = hi, lo, A, V, PE, bank0, banks
        self.xn = x if xn is None else xn

    @staticmethod
    def steps(tag, part, g, tiles):
        of = range(4 * g, min(4 * g + 4, tiles))
        return {"sq": [(tag, "sq", i) for i in of], "sd": [(tag, "sd", g)], "rs": [(tag, "ms", g), (tag, "rs", g)],
                "xn": [(tag, "xn", i) for i in of]}.get(part) or [(tag, part, kt, g) for kt in range(KT)]

    def group(self, g):
        return range(4 * g, min(4 * g + 4, self.tiles))

    def bank(self, kt, g):
        width = len(self.group(g)) * P
        return self.e.ps[self.bank0 + (g * KT + kt) % self.banks][:, 0:width]

    def cols(self, g):
        return slice(4 * g * P, (4 * g + len(self.group(g))) * P)

    def squares(self, act, g, loaded):
        for i in self.group(g):
            loaded(act, i)
            if i:
                act.wait_ge(self.A.sem, self.A.done((self.tag, "sq", i - 1)))
            self.e.nc.scalar.activation(self.junk, self.x[:, i], ACT.Square, accum_out=self.st[:, i:i + 1]).then_inc(self.A.sem, self.A.one((self.tag, "sq", i)))

    def roots(self, act, g):
        of = self.group(g)
        act.wait_ge(self.V.sem, self.V.done((self.tag, "ms", g)))
        self.e.nc.scalar.activation(self.st[:, 8 + of[0]:9 + of[-1]], self.st[:, of[0]:of[-1] + 1], ACT.Sqrt).then_inc(self.A.sem, self.A.one((self.tag, "sd", g)))

    def high(self, act, g):
        for kt in range(KT):
            act.wait_ge(self.PE.sem, self.PE.done((self.tag, "T", kt, g)))
            self.e.nc.scalar.activation(self.hi[:, kt, self.cols(g)], self.bank(kt, g), ACT.Copy, scale=self.gain[:, kt:kt + 1]).then_inc(self.A.sem, self.A.one((self.tag, "hi", kt, g)))

    def scales(self, vec, g):
        of = self.group(g)
        part = self.st[:, of[0]:of[-1] + 1]
        vec.wait_ge(self.A.sem, self.A.done((self.tag, "sq", of[-1])))
        self.e.nc.vector.tensor_scalar(part, part, 1.0 / D, EPS, ALU.mult, ALU.add).then_inc(self.V.sem, self.V.one((self.tag, "ms", g)))
        vec.wait_ge(self.A.sem, self.A.done((self.tag, "sd", g)))
        self.e.nc.vector.reciprocal(part, self.st[:, 8 + of[0]:9 + of[-1]]).then_inc(self.V.sem, self.V.one((self.tag, "rs", g)))

    def normalise(self, vec, g):
        vec.wait_ge(self.V.sem, self.V.done((self.tag, "rs", g)))
        for i in self.group(g):
            self.e.nc.vector.tensor_scalar(self.xn[:, i], self.x[:, i], self.st[:, i:i + 1], None, ALU.mult).then_inc(self.V.sem, self.V.one((self.tag, "xn", i)))

    def low(self, vec, g):
        for kt in range(KT):
            vec.wait_ge(self.A.sem, self.A.done((self.tag, "hi", kt, g)))
            self.e.nc.vector.scalar_tensor_tensor(out=self.lo[:, kt, self.cols(g)], in0=self.bank(kt, g), scalar=self.gain[:, kt:kt + 1], in1=self.hi[:, kt, self.cols(g)].bitcast(F32),
                                                  op0=ALU.mult, op1=ALU.subtract).then_inc(self.V.sem, self.V.one((self.tag, "lo", kt, g)))

    def transposes(self, pe, g):
        of = self.group(g)
        pe.wait_ge(self.V.sem, self.V.done((self.tag, "xn", of[-1])))
        for kt in range(KT):
            n = g * KT + kt
            if n >= self.banks:
                b = n - self.banks
                pe.wait_ge(self.V.sem, self.V.done((self.tag, "lo", b % KT, b // KT)))
            for t, i in enumerate(of):
                last = self.e.nc.tensor.transpose(self.bank(kt, g)[:, t * P:(t + 1) * P], self.xn[:, i, kt * P:(kt + 1) * P], self.e.ident)
            last.then_inc(self.PE.sem, self.PE.one((self.tag, "T", kt, g)))


def norm_phase(e):
    nc = e.nc
    with ExitStack() as ctx:
        xb = e.sb("x_tok", [P, NT, D], ctx=ctx)
        junk = e.sb("squares", [P, D], ctx=ctx)
        st = e.sb("stats", [P, 16], ctx=ctx)
        ext = e.sb("ext", [2 * HP, EXT], ctx=ctx)
        x_in = e.x_loaded
        const_in, par_in, rel_in, ext_out, bias_out = sems(nc, e.ctx, "const_in", "par_in", "rel_in", "ext_out", "bias_out")
        a_s, v_s, p_s = sems(nc, e.ctx, "norm_act", "norm_vec", "norm_pe")
        names = lambda *parts: sum((Norm.steps("x", part, g, NT) for part, g in parts), [])
        A = Steps(a_s, names(("sq", 0), ("sd", 0), ("sq", 1), ("sd", 1), ("hi", 0), ("hi", 1)))
        V = Steps(v_s, names(("rs", 0), ("xn", 0)) + [("ext", 0), ("ext", 1)] + names(("rs", 1), ("xn", 1), ("lo", 0), ("lo", 1)))
        PE = Steps(p_s, names(("T", 0), ("T", 1)))
        norm = Norm(e, "x", xb, NT, st, junk[:], e.par[:, Q_PRE:Q_PRE + KT], e.ahi, e.alo, A, V, PE)
        block = ctx.enter_context(nc.Block())

        @block.sync
        def _(sp):
            for i in range(NT):
                sp.dma_start(xb[:, i], e.x[i * P:(i + 1) * P, :]).then_inc(x_in[i], 16)
            for b in range(2):
                load_block(sp, e, b, b)
            sp.dma_start(ext[:, 511:703], e.rel_rev).then_inc(rel_in, 16)
            sp.wait_ge(V.sem, V.done(("ext", 1)))
            sp.dma_start(e.ext_d, ext[:]).then_inc(ext_out, 16)
            sp.wait_ge(ext_out, 16)
            sp.dma_start(e.bias_d, bass.AP(tensor=e.ext_d.tensor, offset=P - 1, ap=[[EXT, 2 * HP], [-1, P], [1, BAND]])).then_inc(bias_out, 16)
            sp.wait_ge(bias_out, 16)

        @block.gpsimd
        def _(pool):
            for b in range(2):
                split_block(pool, e, b, 16, b + 1)

        @block.scalar
        def _(act):
            act.dma_start(e.par[:], e.params_d).then_inc(par_in, 16)
            act.dma_start(e.consts[:], e.consts_d).then_inc(const_in, 16)
            for g in range(2):
                norm.squares(act, g, lambda eng, i: eng.wait_ge(x_in[i], 16))
                norm.roots(act, g)
            act.wait_ge(par_in, 16)
            for g in range(2):
                norm.high(act, g)
            A.close()

        @block.vector
        def _(vec):
            norm.scales(vec, 0)
            norm.normalise(vec, 0)
            vec.wait_ge(rel_in, 16)
            nc.vector.tensor_copy(ext[:, 0:511], ext[:, 511:512].broadcast_to([2 * HP, 511])).then_inc(v_s, V.one(("ext", 0)))
            nc.vector.memset(ext[:, 703:EXT], 0.0).then_inc(v_s, V.one(("ext", 1)))
            norm.scales(vec, 1)
            norm.normalise(vec, 1)
            vec.wait_ge(par_in, 16)
            for g in range(2):
                norm.low(vec, g)
            V.close()

        @block.tensor
        def _(pe):
            pe.wait_ge(const_in, 16)
            for g in range(2):
                norm.transposes(pe, g)
            PE.close()


def mix_phase(e):
    nc = e.nc
    with ExitStack() as ctx:
        sb = lambda name, shape, dt=F32: e.sb(name, shape, dt, ctx)
        lora = sb("lora", [P, SEQ])
        sg = sb("sig_gate", [P, 2, SEQ])
        lup = sb("lora_up", [P, P])
        gup = sb("gate_up", [P, 2, P])
        bias = sb("bias", [P, 2, BAND])
        cur = sb("cur", [P, PP + 4])
        Z = sb("work", [P, 7 * SEQ])
        r_t, k_t, a_t, kk_t = (sb(n, [P, SEQ]) for n in ("r_cm", "k_cm", "a_cm", "kk_cm"))
        v_t = sb("v_cm", [P, SEQ])
        QR = sb("kq_rt", [P, NC_, 2 * C])
        BK = sb("bt_kt", [P, NC_, 2 * C])
        qz = sb("att_q", [P, 2, SEQ])
        kT = sb("att_k", [P, SEQ])
        vtm = sb("att_v_tok", [P, NT, P])
        yb = sb("att_out", [P, SEQ])
        vT = yb
        pe_s = sb("probs", [P, 2, BAND])
        pT = sb("probs_T", [P, BANDT, 2, P])
        small = sb("small", [P, 8])
        st_S = sb("state", [P, 2, C])
        st_L = sb("state_decayed", [P, C])
        Wt = sb("w_tok", [P, C])
        Ut = sb("u_tok", [P, C])
        lamC = sb("chunk_decay", [P, NC_])

        rs_kk, sq, sig, Ls, Linv, Lam, Lamx = (Z[:, 1024 * i:1024 * (i + 1)] for i in range(7))
        Pr, Pk = (QR[:].rearrange("p c t -> p (c t)")[:, SEQ * i:SEQ * (i + 1)] for i in range(2))
        Pb = {"r": Pr, "k": Pk, "v": yb[:]}
        Zb = {"r": r_t[:], "k": k_t[:], "v": v_t[:]}
        M1 = Z[:, 0:2048].rearrange("p (c t) -> p c t", t=2 * C)
        M2 = Z[:, 2048:4096].rearrange("p (c t) -> p c t", t=2 * C)
        T, TT, X = (Z[:, 4096 + 1024 * i:5120 + 1024 * i].rearrange("p (c t) -> p c t", t=C) for i in range(3))
        Vm, Bm, Km = (t[:].rearrange("p (c t) -> p c t", t=C) for t in (k_t, kk_t, a_t))
        yT = Z[:, 4096:5120]
        gsq, grs = Z[:, 6144:6656], Z[:, 6656:7168]

        mask2 = e.consts[:, C_MASK:C_MASK + P]
        bc = lambda ap, n: ap.rearrange("p (a t) -> p a t", a=1).broadcast_to([P, n, ap.shape[1]])
        eye8 = bc(e.consts[:, C_EYE:C_EYE + C], GC)
        level = {m: bc(e.consts[:, C_LV + C * n:C_LV + C * (n + 1)], GC) for n, m in enumerate(LEVELS)}
        ones = e.consts[:, C_ONES:C_ONES + P]
        param = lambda i: cur[:, i:i + 1]

        w_split, w_used = e.w_split, e.w_used
        pro_act, pro_vec, pro_pe = sems(nc, e.ctx, "lora_act", "lora_vec", "lora_pe")
        act_done, vec_done, pe_done = sems(nc, e.ctx, "act_done", "vec_done", "pe_done")
        pe_passed, vec_passed = sems(nc, e.ctx, "pe_passed", "vec_passed")
        lup_in, gup_in, ya_out, yb_out = sems(nc, e.ctx, "lup_in", "gup_in", "ya_out", "yb_out")
        bias_in = sems(nc, e.ctx, "bias_in0", "bias_in1")

        def unit(u):
            j, i = u % 2, u // 2
            return j, i, min(i + 1, BANDT)

        NU = 16
        halves = (0, 1)
        a_names = [("T", name, h) for name in "kr" for h in halves]
        a_names += [("kksq", h) for h in halves] + [("sig", h) for h in halves]
        a_names += [("P", "v", 0), ("T", "v", 0)] + [("a", h) for h in halves] + [("kksd", h) for h in halves]
        a_names += ["Linv", "Lam", "Lamx", ("P", "v", 1), ("T", "v", 1)]
        a_names += [("aq", h, j) for h in halves for j in range(2)]
        a_names += [(n, g) for g in range(G) for n in ("Vm", "Bm", "Km")] + [("av", 0)]
        for m in LEVELS:
            for g in range(G):
                if m == 4 and g == 0:
                    a_names += [("av", 1)]
                a_names += [("T", m, g)] * (m != LEVELS[-1])
                if m == 4 and g == 0:
                    a_names += [("vtm", 0), ("vtm", 1)]
                if m == 8 and g == 1:
                    a_names += [("ak", 0)]
                a_names += [("TT", m, g)]
                if m == 16 and g == 1:
                    a_names += [("ak", 1)]
                if m == 32 and g == 0:
                    a_names += [("exp", 0), ("exp", 1)]
        v_names = ["cur", "om", "omk", ("z", "k"), ("z", "r")] + [("scan", n) for n in range(SEQ // SCAN)] + [("kkmax", 0), ("kkmax", 1), "Lx"]
        for h in halves:
            v_names += [(n, h) for n in ("kkrs", "kk", "b", "bt", "kq", "rt", "am", "kp", "kt")]
        v_names += ["lamC"]
        for g in range(G):
            if g == 1:
                v_names += [("z", "v"), "rk", ("bmask", 0), ("bmask", 1)]
            v_names += [("X1", g, 0), ("X1", g, 1), ("X2", g, 0), ("X2", g, 1), ("A", g)]
            v_names += [("T2", g), ("T2T0", g), ("T2T", g), ("ATI", g)]
        for m in LEVELS:
            v_names += [("X", m, g) for g in range(G)]
            if m == 32:
                v_names += [("ttr", 0), ("nmx", 0), ("ttr", 1), ("nmx", 1), ("rin", 0), ("pn", 0)]
        p_names = [("dec", h) for h in halves] + [("v", 0)] + [("icl", h) for h in halves]
        p_names += [("kkss", h) for h in halves] + [("v", 1), ("aq", 0)]
        order = []
        for g in range(G):
            order += [("X1", g, 0), ("X1", g, 1), ("X2", g, 0), ("X2", g, 1), ("A", g)]
        order += [(n, g) for g in range(G) for n in ("Vm", "Bm", "Km")]
        for m in LEVELS:
            order += [("X", m, g) for g in range(G)]
            for g in range(G):
                order += [("T", m, g)] * (m != LEVELS[-1]) + [("TT", m, g)]
        STEPS_AT = {item: [] for item in order}
        for first, apart, name, h in ((1, 0, "aq", 1), (2, 2, "av", 0), (16, 1, "av", 1), (25, 1, "ak", 0), (33, 1, "ak", 1)):
            for kt in range(KT):
                STEPS_AT[order[first + apart * kt]] += [(name, h, kt)]
        for item in order:
            p_names += [item]
            p_names += [(name, h) for name, h, kt in STEPS_AT[item] if kt == KT - 1]
            if item == ("T", 4, 0):
                p_names += [("avT", 0), ("avT", 1)]
            if item == ("X", 32, 1):
                p_names += [("sc", 0), ("sc", 1)]

        ELEN = 8

        def e_stage(c):
            return (0, c - 8) if 8 <= c < 8 + ELEN else (None, None)

        R_AT = {0: (0, 1), 1: (2, 3), 2: (4,), 4: (5,), 12: (6,), 14: (7,)}

        def five(u):
            return unit(u)[2] == BANDT

        def slots_act(c):
            out = [("SL", c)] * (c > 0) + [("pT", c)] + [("pT5", c)] * five(c) + [("Y", c)]
            return out + [("exp", c + 2)] * (c + 2 < NU) + [("out", c, 0), ("out", c, 1)] * (c % 2)

        def slots_vec(c):
            return [("W", c)] + [("rin", c + 1), ("pn", c + 1)] * (c + 1 < NU) + [("U", c), ("S", c)] + [("ttr", c + 2), ("nmx", c + 2)] * (c + 2 < NU)

        def slots_pe(c):
            return [("W", c), ("pT", c), ("U", c)] + [("sc", c + 2)] * (c + 2 < NU) + [("S", c), ("Y", c)] + [("out", c)] * (c % 2)

        E_ACT = [["gsq"], [], ["gsd"], [], [], [], [], []]
        E_VEC = [[], [], ["gms"], ["grs0", "grs1"], ["bov"], ["grs2", "grs3"], ["yn"], ["yw", "yb", "yg"]]
        E_PE = [[], ["var"], [], ["bo"], [], [], [], ["gt"]]
        for c in range(NC_):
            a_names += slots_act(c)
            v_names += slots_vec(c)
            p_names += slots_pe(c) + [("r", 0)] * (KT - 1 in R_AT.get(c, ()))
            h, s = e_stage(c)
            if h is not None:
                a_names += [(n, h) for n in E_ACT[s]]
                v_names += [(n, h) for n in E_VEC[s]]
                p_names += [(n, h) for n in E_PE[s]]
        for s in range(ELEN):
            a_names += [(n, 1) for n in E_ACT[s]] + {1: [("P", "r", 0), ("P", "r", 1)], 2: [("P", "k", 0), ("P", "k", 1)]}.get(s, [])
            v_names += [(n, 1) for n in E_VEC[s]]
            p_names += {1: [("r", 1)], 3: [("k", 0)]}.get(s, []) + [(n, 1) for n in E_PE[s]] + {3: [("k", 1)]}.get(s, [])
        A = Steps(act_done, a_names, True)
        V = Steps(vec_done, v_names, True)
        PE = Steps(pe_done, p_names, True)
        LA = Steps(pro_act, [("pc", n, h) for n in range(3) for h in halves] + ["tanh", ("sg", 0), ("sg", 1)] + [("P", n, h) for n in "rk" for h in halves])
        LV = Steps(pro_vec, ["qzero0", "qzero1", "omm", ("t", 0), ("z", 0), ("t", 1), ("z", 1), ("t", 2), ("z", 2)])
        LP = Steps(pro_pe, [("l", n, h) for n in range(3) for h in halves] + [(n, h) for n in "rk" for h in halves])

        bank = e.ps
        block = ctx.enter_context(nc.Block())
        start_weights(e, block, NB_LORA, NB_GA)

        hs = [slice(0, HALF), slice(HALF, SEQ)]
        rows = [slice(0, C), slice(C, P)]

        def gn_pe(pe, hp, h, s):
            if s == 1:
                pe.wait_ge(act_done, A.done(("gsq", h), hp))
                if h == 1:
                    pe.wait_ge(vec_done, V.done(("yg", 0), hp))
                nc.tensor.matmul(bank[3], ones, gsq, start=True, stop=True).then_inc(pe_done, PE.one(("var", h)))
            elif s == 3:
                pe.wait_ge(vec_done, V.done(("gms", h), hp))
                nc.tensor.matmul(bank[3], ones, r_t[:, hs[h]], start=True, stop=True).then_inc(pe_done, PE.one(("bo", h)))
            elif s == 7:
                pe.wait_ge(vec_done, V.done(("bov", h), hp))
                pe.wait_ge(gup_in, hp * 16 + 16)
                nc.tensor.matmul(bank[3], gup[:, 0, :], sg[:, 0, hs[h]], start=True, stop=False)
                nc.tensor.matmul(bank[3], gup[0:32, 1, :], sg[0:32, 1, hs[h]], start=False, stop=True).then_inc(pe_done, PE.one(("gt", h)))

        def gn_act(act, hp, h, s):
            if s == 0:
                if h == 1:
                    act.wait_ge(vec_done, V.done(("yb", 0), hp))
                act.wait_ge(act_done, A.done(("Y", NC_ // 2 * (h + 1) - 1), hp))
                nc.scalar.activation(gsq, yT[:, hs[h]], ACT.Square).then_inc(act_done, A.one(("gsq", h)))
            elif s == 2:
                act.wait_ge(vec_done, V.done(("gms", h), hp))
                nc.scalar.activation(grs, grs, ACT.Sqrt).then_inc(act_done, A.one(("gsd", h)))
            elif s == 7:
                act.wait_ge(vec_done, V.done(("yg", h), hp))
                act.dma_start(e.ya_d[bass.ds(hp, 1), :, hs[h]].rearrange("a p t -> p (a t)"), yT[:, hs[h]]).then_inc(ya_out, 16)

        def gn_vec(vec, hp, h, s):
            tt, ts = nc.vector.tensor_tensor, nc.vector.tensor_scalar
            y = yT[:, hs[h]]
            if s == 2:
                vec.wait_ge(pe_done, PE.done(("var", h), hp))
                if h == 1:
                    vec.wait_ge(vec_done, V.done(("yn", 0), hp))
                ts(grs, bank[3], 1.0 / C, GN_EPS, ALU.mult, ALU.add).then_inc(vec_done, V.one(("gms", h)))
            elif 3 <= s < 6:
                if s == 3:
                    vec.wait_ge(act_done, A.done(("gsd", h), hp))
                if s == 4:
                    vec.wait_ge(pe_done, PE.done(("bo", h), hp))
                    tt(gsq, bank[3], v_t[:, hs[h]], ALU.mult).then_inc(vec_done, V.one(("bov", h)))
                for n in {3: (0, 1), 4: (), 5: (2, 3)}[s]:
                    part = grs[:, n * P:(n + 1) * P]
                    nc.vector.reciprocal(part, part).then_inc(vec_done, V.one((f"grs{n}", h)))
            elif s == 6:
                vec.wait_ge(vec_done, V.done(("grs3", h), hp))
                tt(y, y, grs, ALU.mult).then_inc(vec_done, V.one(("yn", h)))
            elif s == 7:
                vec.wait_ge(vec_done, V.done(("yn", h), hp))
                ts(y, y, param(LNW), param(LNB), ALU.mult, ALU.add).then_inc(vec_done, V.one(("yw", h)))
                vec.wait_ge(vec_done, V.done(("yw", h), hp))
                tt(y, y, gsq, ALU.add).then_inc(vec_done, V.one(("yb", h)))
                vec.wait_ge(vec_done, V.done(("yb", h), hp))
                vec.wait_ge(pe_done, PE.done(("gt", h), hp))
                tt(y, bank[3], y, ALU.mult).then_inc(vec_done, V.one(("yg", h)))

        BANKS = {"r": (5, 0), "k": (1, 4), "dec": (2, 6), "icl": (5, 0), "kkss": (1, 4), "v": (7, 3), "aq": (6, 7), "av": (6, 7), "ak": (6, 7)}

        def project(pe, blk, name, h, kts=range(KT)):
            s = blk % 2
            for kt in kts:
                last = mm3(nc, bank[BANKS[name][h]], e.whi[:, s, kt], e.wlo[:, s, kt], e.ahi[:, kt, hs[h]], e.alo[:, kt, hs[h]], kt == 0, kt == KT - 1)
            return last

        def project_step(pe, hp, item):
            for name, h, kt in STEPS_AT[item]:
                blk = NB_HEAD + 3 + ("aq", "av", "ak").index(name)
                if kt == 0:
                    if h == 0:
                        pe.wait_ge(w_split, hp * 6 + blk + 1)
                    pe.wait_ge(act_done, A.done({("aq", 1): ("T", "v", 0), ("av", 0): ("aq", 0, 1), ("av", 1): ("aq", 1, 1),
                                                 ("ak", 0): ("vtm", 0), ("ak", 1): ("vtm", 1)}[name, h], hp))
                last = project(pe, blk, name, h, [kt])
                if kt == KT - 1:
                    last.then_inc(pe_done, PE.one((name, h)))

        def mix_pe(pe, hp):
            blk = NB_HEAD + 2
            pe.wait_ge(lup_in, hp * 16 + 16)
            pe.wait_ge(act_done, A.done(("out", NU - 1, 1), hp, 1))
            for h in halves:
                nc.tensor.matmul(bank[BANKS["dec"][h]], lup[0:C, :], lora[0:C, hs[h]], start=True, stop=True).then_inc(pe_done, PE.one(("dec", h)))
            pe.wait_ge(w_split, hp * 6 + blk + 1)
            project(pe, blk, "v", 0).then_inc(pe_done, PE.one(("v", 0)))
            pe.wait_ge(act_done, A.done(("T", "r", 1), hp))
            for h in halves:
                nc.tensor.matmul(bank[BANKS["icl"][h]], lup[C:P, :], lora[C:P, hs[h]], start=True, stop=True).then_inc(pe_done, PE.one(("icl", h)))
            pe.wait_ge(vec_done, V.done(("yg", 1), hp, 1))
            project(pe, blk, "v", 1, range(KT // 2))
            for h in halves:
                pe.wait_ge(act_done, A.done(("kksq", h), hp))
                nc.tensor.matmul(bank[BANKS["kkss"][h]], ones, sq[:, hs[h]], start=True, stop=True).then_inc(pe_done, PE.one(("kkss", h)))
            project(pe, blk, "v", 1, range(KT // 2, KT)).then_inc(pe_done, PE.one(("v", 1)))
            pe.wait_ge(w_split, hp * 6 + blk + 2)
            pe.wait_ge(act_done, A.done(("sig", 1), hp))
            project(pe, blk + 1, "aq", 0).then_inc(pe_done, PE.one(("aq", 0)))
            xb = {0: (0, 1, 2, 3, 4), 1: (5, 0, 1, 2, 3)}
            for g in range(G):
                for q in range(2):
                    b = bank[xb[g][q]]
                    if q == 0:
                        pe.wait_ge(vec_done, V.done(("rt", g), hp))
                    elif g == 1:
                        pe.wait_ge(vec_done, V.done(("X1", 0, 0), hp))
                    settle(pe, pe_passed)
                    for cc in range(4):
                        c = g * GC + q * 4 + cc
                        for j in range(2):
                            last = nc.tensor.matmul(b[rows[j], cc * P:(cc + 1) * P], BK[rows[j], c, 0:C], QR[rows[j], c, :], start=True, stop=True, skip_group_check=True)
                    last.then_inc(pe_done, PE.one(("X1", g, q)))
                    project_step(pe, hp, ("X1", g, q))
                for q in range(2):
                    b = bank[xb[g][2 + q]]
                    if g == 1:
                        pe.wait_ge(vec_done, V.done(("X1", 0, 1) if q == 0 else ("X2", 0, 0), hp))
                    elif q == 1:
                        pe.wait_ge(act_done, A.done(("T", "v", 1), hp))
                    if q == 0:
                        pe.wait_ge(vec_done, V.done(("kt", g), hp))
                    settle(pe, pe_passed)
                    for cc in range(4):
                        c = g * GC + q * 4 + cc
                        for j in range(2):
                            last = nc.tensor.matmul(b[rows[j], cc * P:(cc + 1) * P], BK[rows[j], c, C:P], QR[rows[j], c, :], start=True, stop=True, skip_group_check=True)
                    last.then_inc(pe_done, PE.one(("X2", g, q)))
                    project_step(pe, hp, ("X2", g, q))
                b = bank[xb[g][4]]
                if g == 1:
                    pe.wait_ge(vec_done, V.done(("X2", 0, 1), hp))
                settle(pe, pe_passed)
                for cc in range(GC):
                    c = g * GC + cc
                    for j in range(2):
                        last = nc.tensor.matmul(b[rows[j], cc * C:(cc + 1) * C], QR[rows[j], c, 0:C], BK[rows[j], c, 0:C], start=True, stop=True, skip_group_check=True)
                last.then_inc(pe_done, PE.one(("A", g)))
                project_step(pe, hp, ("A", g))
            tm_bank = {("Vm", 0): 4, ("Bm", 0): 5, ("Km", 0): 0, ("Vm", 1): 1, ("Bm", 1): 2, ("Km", 1): 3}
            prev = {("Vm", 0): ("z", "v"), ("Bm", 0): ("X1", 1, 0), ("Km", 0): ("X1", 1, 1),
                    ("Vm", 1): ("X2", 1, 0), ("Bm", 1): ("X2", 1, 1), ("Km", 1): ("A", 1)}
            for g in range(G):
                for n, name in enumerate(("Vm", "Bm", "Km")):
                    b = bank[tm_bank[name, g]]
                    pe.wait_ge(vec_done, V.done(prev[name, g], hp))
                    settle(pe, pe_passed)
                    for cc in range(GC):
                        c = g * GC + cc
                        for j in range(2):
                            src = {"Vm": v_t[rows[j], c * C:(c + 1) * C], "Bm": BK[rows[j], c, 0:C], "Km": BK[rows[j], c, C:P]}[name]
                            eye = C_CEN if name == "Vm" else C_EYE
                            last = nc.tensor.matmul(b[rows[j], cc * C:(cc + 1) * C], src, e.consts[rows[j], eye:eye + C], start=True, stop=True, skip_group_check=True)
                    last.then_inc(pe_done, PE.one((name, g)))
                    project_step(pe, hp, (name, g))
            for m in LEVELS:
                for g in range(G):
                    if m == 2:
                        pe.wait_ge(vec_done, V.done(("ATI", g), hp))
                        pe.wait_ge(act_done, A.done(("Km", g), hp))
                    else:
                        pe.wait_ge(act_done, A.done(("T", m // 2, g), hp))
                        pe.wait_ge(vec_done, V.done(("X", m // 2, g), hp))
                    settle(pe, pe_passed)
                    for cc in range(GC):
                        c = g * GC + cc
                        for j in range(2):
                            last = nc.tensor.matmul(bank[3 * g][rows[j], cc * C:(cc + 1) * C], M1[rows[j], c, 0:C], T[rows[j], c, :], start=True, stop=True, skip_group_check=True)
                    last.then_inc(pe_done, PE.one(("X", m, g)))
                    project_step(pe, hp, ("X", m, g))
                if m == 32:
                    for u in range(2):
                        pe.wait_ge(act_done, A.done(("ak", 1), hp))
                        scores(u).then_inc(pe_done, PE.one(("sc", u)))
                for g in range(G):
                    pe.wait_ge(vec_done, V.done(("X", m, g), hp))
                    if m == 2:
                        pe.wait_ge(act_done, A.done(("Bm", 1), hp))
                    else:
                        pe.wait_ge(act_done, A.done(("TT", m // 2, g), hp))
                    if m != LEVELS[-1]:
                        settle(pe, pe_passed)
                        for cc in range(GC):
                            c = g * GC + cc
                            for j in range(2):
                                last = nc.tensor.matmul(bank[3 * g + 1][rows[j], cc * C:(cc + 1) * C], TT[rows[j], c, :], X[rows[j], c, :], start=True, stop=True, skip_group_check=True)
                        last.then_inc(pe_done, PE.one(("T", m, g)))
                        project_step(pe, hp, ("T", m, g))
                    if m == 4 and g == 0:
                        for n in range(2):
                            pe.wait_ge(act_done, A.done(("av", n), hp))
                            for i in range(4):
                                last = nc.tensor.transpose(bank[6 + n][:, i * P:(i + 1) * P], vT[:, (4 * n + i) * P:(4 * n + i + 1) * P], e.ident)
                            last.then_inc(pe_done, PE.one(("avT", n)))
                    settle(pe, pe_passed)
                    for cc in range(GC):
                        c = g * GC + cc
                        for j in range(2):
                            last = nc.tensor.matmul(bank[3 * g + 2][rows[j], cc * C:(cc + 1) * C], X[rows[j], c, :], TT[rows[j], c, :], start=True, stop=True, skip_group_check=True)
                    last.then_inc(pe_done, PE.one(("TT", m, g)))
                    project_step(pe, hp, ("TT", m, g))
            for c in range(NC_):
                if c == 0:
                    pe.wait_ge(act_done, A.done(("TT", 32, 1), hp))
                else:
                    pe.wait_ge(vec_done, V.done(("S", c - 1), hp))
                settle(pe, pe_passed)
                for j in range(2):
                    last = nc.tensor.matmul(bank[4][rows[j], 0:C], M2[rows[j], c, 0:C], Vm[rows[j], c, :], start=True, stop=c == 0)
                if c > 0:
                    for j in range(2):
                        last = nc.tensor.matmul(bank[4][rows[j], 0:C], QR[rows[j], c, 0:C], st_S[rows[j], c % 2, :], start=False, stop=True)
                last.then_inc(pe_done, PE.one(("W", c)))
                nk = unit(c)[2]
                pe.wait_ge(vec_done, V.done(("pn", c), hp))
                if c > 0:
                    pe.wait_ge(act_done, A.done(("out", c - 1, 1) if c % 2 == 0 else ("pT5" if five(c - 1) else "pT", c - 1), hp))
                for t in range(nk):
                    dst = bank[2][:, t * P:(t + 1) * P] if t < 4 else bank[7][:, 2 * P:3 * P]
                    last = nc.tensor.transpose(dst, pe_s[:, c % 2, t * P:(t + 1) * P], e.ident)
                last.then_inc(pe_done, PE.one(("pT", c)))
                pe.wait_ge(vec_done, V.done(("W", c), hp))
                settle(pe, pe_passed)
                for j in range(2):
                    last = nc.tensor.matmul(bank[4][rows[j], 0:C], TT[rows[j], c, :], Wt[rows[j], :], start=True, stop=True)
                last.then_inc(pe_done, PE.one(("U", c)))
                if c + 2 < NU:
                    if c > 0:
                        pe.wait_ge(vec_done, V.done(("ttr", c + 1), hp))
                    scores(c + 2).then_inc(pe_done, PE.one(("sc", c + 2)))
                pe.wait_ge(vec_done, V.done(("U", c), hp))
                settle(pe, pe_passed)
                for j in range(2):
                    nc.tensor.matmul(bank[4][rows[j], 0:C], Km[rows[j], c, :], Vm[rows[j], c, :], start=True, stop=False)
                for j in range(2):
                    last = nc.tensor.matmul(bank[4][rows[j], 0:C], Bm[rows[j], c, :], Ut[rows[j], :], start=False, stop=True)
                last.then_inc(pe_done, PE.one(("S", c)))
                if c > 0:
                    pe.wait_ge(act_done, A.done(("Y", c - 1), hp))
                settle(pe, pe_passed)
                for j in range(2):
                    nc.tensor.matmul(bank[6][rows[j], 0:C], Vm[rows[j], c, :], M2[rows[j], c, C:P], start=True, stop=False)
                for j in range(2):
                    last = nc.tensor.matmul(bank[6][rows[j], 0:C], Ut[rows[j], :], M1[rows[j], c, C:P], start=False, stop=c == 0)
                if c > 0:
                    for j in range(2):
                        last = nc.tensor.matmul(bank[6][rows[j], 0:C], st_S[rows[j], c % 2, :], QR[rows[j], c, C:P], start=False, stop=True)
                last.then_inc(pe_done, PE.one(("Y", c)))
                if c % 2:
                    j, i, nk = unit(c)
                    pe.wait_ge(act_done, A.done(("pT5" if five(c) else "pT", c), hp))
                    for t in range(nk):
                        last = nc.tensor.matmul(bank[7][:, 0:2 * P], vtm[:, i + 1 - nk + t, :], pT[:, t, :, :].rearrange("p j q -> p (j q)"), start=t == 0, stop=t == nk - 1)
                    last.then_inc(pe_done, PE.one(("out", c)))
                for kt in R_AT.get(c, ()):
                    if kt == 0:
                        pe.wait_ge(w_split, hp * 6 + (NB_HEAD + 7))
                    last = project(pe, NB_HEAD, "r", 0, [kt])
                    if kt == KT - 1:
                        last.then_inc(pe_done, PE.one(("r", 0)))
                h, s = e_stage(c)
                if h is not None:
                    gn_pe(pe, hp, h, s)
            for s in range(ELEN):
                if s == 1:
                    project(pe, NB_HEAD, "r", 1).then_inc(pe_done, PE.one(("r", 1)))
                if s == 3:
                    pe.wait_ge(w_split, hp * 6 + (NB_HEAD + 8))
                    project(pe, NB_HEAD + 1, "k", 0).then_inc(pe_done, PE.one(("k", 0)))
                gn_pe(pe, hp, 1, s)
                if s == 3:
                    project(pe, NB_HEAD + 1, "k", 1).then_inc(pe_done, PE.one(("k", 1)))

        def scores(u):
            j, i, nk = unit(u)
            k0, n0 = (i + 1 - nk) * P, min(nk, 4) * P
            b0 = 6 + u if u < 2 else 0
            last = nc.tensor.matmul(bank[b0][:, 0:n0], qz[:, j, i * P:(i + 1) * P], kT[:, k0:k0 + n0], start=True, stop=True)
            if nk == BANDT:
                last = nc.tensor.matmul(bank[1][:, 0:P], qz[:, j, i * P:(i + 1) * P], kT[:, k0 + n0:k0 + n0 + P], start=True, stop=True)
            return last

        def mix_act(act, hp):
            act.wait_ge(vec_done, V.done("omk", hp))
            for name in "kr":
                for h in halves:
                    nc.scalar.activation(Zb[name][:, hs[h]], bank[BANKS[name][h]], ACT.Copy, scale=param(OM_K if name == "k" else OM_R)).then_inc(act_done, A.one(("T", name, h)))
            act.wait_ge(vec_done, V.done(("z", "k"), hp))
            for h in halves:
                nc.scalar.activation(sq[:, hs[h]], k_t[:, hs[h]], ACT.Square, scale=param(KNS)).then_inc(act_done, A.one(("kksq", h)))
            for h in halves:
                act.wait_ge(pe_done, PE.done(("dec", h), hp))
                nc.scalar.activation(sig[:, hs[h]], bank[BANKS["dec"][h]], ACT.Sigmoid, bias=param(DEC_B)).then_inc(act_done, A.one(("sig", h)))
            act.wait_ge(yb_out, hp * 16 + 1)
            v_act(act, hp, 0)
            for h in halves:
                act.wait_ge(pe_done, PE.done(("icl", h), hp))
                nc.scalar.activation(a_t[:, hs[h]], bank[BANKS["icl"][h]], ACT.Sigmoid, bias=param(ICL_B)).then_inc(act_done, A.one(("a", h)))
            act.dma_start(lup[:], e.lora_up[bass.ds(hp + 1, 1)].rearrange("a p m -> p (a m)")).then_inc(lup_in, 16)
            for h in halves:
                act.wait_ge(vec_done, V.done(("kkmax", h), hp))
                nc.scalar.activation(rs_kk[:, hs[h]], rs_kk[:, hs[h]], ACT.Sqrt).then_inc(act_done, A.one(("kksd", h)))
            nc.scalar.activation(Linv, Ls, ACT.Exp, scale=EXP_HALF).then_inc(act_done, A.one("Linv"))
            nc.scalar.activation(Lam, Ls, ACT.Exp, scale=-EXP_HALF).then_inc(act_done, A.one("Lam"))
            act.wait_ge(vec_done, V.done("Lx", hp))
            nc.scalar.activation(Lamx, sig, ACT.Exp, scale=-EXP_HALF).then_inc(act_done, A.one("Lamx"))
            v_act(act, hp, 1)
            act.sem_inc(w_used, 1)
            act.dma_start(gup[:], e.gate_up2[bass.ds(hp, 1)].rearrange("a p g m -> p (a g) m")).then_inc(gup_in, 16)
            for j in range(2):
                act.dma_start(bias[:, j], e.bias_d[bass.ds(hp * 2 + j, 1)].rearrange("a p c -> p (a c)")).then_inc(bias_in[j], 16)
            for h in halves:
                act.wait_ge(pe_done, PE.done(("aq", h), hp))
                if h == 1:
                    act.sem_inc(w_used, 1)
                for j in range(2):
                    nc.scalar.activation(qz[rows[j], j, hs[h]], bank[6 + h][rows[j], :], ACT.Copy, scale=0.125).then_inc(act_done, A.one(("aq", h, j)))
            act.wait_ge(vec_done, V.done("rk", hp))
            tm_bank = {("Vm", 0): 4, ("Bm", 0): 5, ("Km", 0): 0, ("Vm", 1): 1, ("Bm", 1): 2, ("Km", 1): 3}
            for g in range(G):
                for name, dst in (("Vm", Vm), ("Bm", Bm), ("Km", Km)):
                    act.wait_ge(pe_done, PE.done((name, g), hp))
                    nc.scalar.activation(dst[:, g * GC:(g + 1) * GC, :].rearrange("p c t -> p (c t)"), bank[tm_bank[name, g]], ACT.Copy).then_inc(act_done, A.one((name, g)))
            kv_act(act, hp, "av", 0)
            for m in LEVELS:
                for g in range(G):
                    gs = slice(g * GC, (g + 1) * GC)
                    if m == 4 and g == 0:
                        kv_act(act, hp, "av", 1)
                    if m != LEVELS[-1]:
                        act.wait_ge(pe_done, PE.done(("T", m, g), hp))
                        nc.scalar.activation(T[:, gs, :].rearrange("p c t -> p (c t)"), bank[3 * g + 1], ACT.Copy).then_inc(act_done, A.one(("T", m, g)))
                    if m == 4 and g == 0:
                        for n in range(2):
                            act.wait_ge(pe_done, PE.done(("avT", n), hp))
                            nc.scalar.activation(vtm[:, 4 * n:4 * n + 4, :].rearrange("p i m -> p (i m)"), bank[6 + n], ACT.Copy).then_inc(act_done, A.one(("vtm", n)))
                    if m == 8 and g == 1:
                        kv_act(act, hp, "ak", 0)
                    act.wait_ge(pe_done, PE.done(("TT", m, g), hp))
                    nc.scalar.activation(TT[:, gs, :].rearrange("p c t -> p (c t)"), bank[3 * g + 2], ACT.Copy).then_inc(act_done, A.one(("TT", m, g)))
                    if m == 16 and g == 1:
                        kv_act(act, hp, "ak", 1)
                    if m == 32 and g == 0:
                        for u in range(2):
                            exp_act(act, hp, u)
            for c in range(NC_):
                if c > 0:
                    act.wait_ge(vec_done, V.done(("S", c - 1), hp))
                    nc.scalar.activation(st_L[:], st_S[:, c % 2, :], ACT.Copy, scale=lamC[:, c:c + 1]).then_inc(act_done, A.one(("SL", c)))
                j, i, nk = unit(c)
                act.wait_ge(pe_done, PE.done(("pT", c), hp))
                n0 = min(nk, 4)
                nc.scalar.activation(pT[:, 0:n0, j, :], bank[2][:, 0:n0 * P].rearrange("p (t q) -> p t q", q=P), ACT.Copy).then_inc(act_done, A.one(("pT", c)))
                if nk == BANDT:
                    nc.scalar.activation(pT[:, 4, j, :], bank[7][:, 2 * P:3 * P], ACT.Copy).then_inc(act_done, A.one(("pT5", c)))
                act.wait_ge(pe_done, PE.done(("Y", c), hp))
                nc.scalar.activation(yT[:, c * C:(c + 1) * C], bank[6][:, 0:C], ACT.Copy).then_inc(act_done, A.one(("Y", c)))
                if c + 2 < NU:
                    exp_act(act, hp, c + 2)
                if c % 2:
                    act.wait_ge(pe_done, PE.done(("out", c), hp))
                    for j in range(2):
                        nc.scalar.activation(yb[rows[j], i * P:(i + 1) * P], bank[7][rows[j], j * P:(j + 1) * P], ACT.Copy).then_inc(act_done, A.one(("out", c, j)))
                h, s = e_stage(c)
                if h is not None:
                    gn_act(act, hp, h, s)
            act.wait_ge(act_done, A.done(("out", NU - 1, 1), hp))
            act.dma_start(e.yb_d[bass.ds(hp, 1)].rearrange("a p t -> p (a t)"), yb[:]).then_inc(yb_out, 16)
            for s in range(ELEN):
                gn_act(act, hp, 1, s)
                if s in (1, 2):
                    name = "rk"[s - 1]
                    act.wait_ge(pe_done, PE.done((name, 1), hp))
                    act.sem_inc(w_used, 1)
                    for h in halves:
                        nc.scalar.activation(Pb[name][:, hs[h]], bank[BANKS[name][h]], ACT.Copy).then_inc(act_done, A.one(("P", name, h)))

        def v_act(act, hp, h):
            act.wait_ge(pe_done, PE.done(("v", h), hp))
            nc.scalar.activation(Pb["v"][:, hs[h]], bank[BANKS["v"][h]], ACT.Copy).then_inc(act_done, A.one(("P", "v", h)))
            nc.scalar.activation(Zb["v"][:, hs[h]], bank[BANKS["v"][h]], ACT.Copy, scale=param(OM_V)).then_inc(act_done, A.one(("T", "v", h)))

        def kv_act(act, hp, name, h):
            act.wait_ge(pe_done, PE.done((name, h), hp))
            if h == 1:
                act.sem_inc(w_used, 1)
            nc.scalar.activation({"ak": kT, "av": vT}[name][:, hs[h]], bank[6 + h], ACT.Copy).then_inc(act_done, A.one((name, h)))

        def exp_act(act, hp, u):
            nk = unit(u)[2]
            act.wait_ge(vec_done, V.done(("nmx", u), hp))
            nc.scalar.activation(pe_s[:, u % 2, 0:nk * P], pe_s[:, u % 2, 0:nk * P], ACT.Exp,
                                 bias=small[:, 2 + u % 2:3 + u % 2], accum_out=small[:, 4 + u % 2:5 + u % 2]).then_inc(act_done, A.one(("exp", u)))

        def mix_vec(vec, hp):
            tt = nc.vector.tensor_tensor
            ts = nc.vector.tensor_scalar
            stt = nc.vector.scalar_tensor_tensor
            nc.vector.tensor_copy(cur[:, 0:PP], e.par[:, bass.ds(hp * PP, PP)]).then_inc(vec_done, V.one("cur"))
            vec.wait_ge(vec_done, V.done("cur", hp))
            ts(cur[:, OM_R:OM_R + 3], cur[:, MIX_R:MIX_R + 3], -1.0, 1.0, ALU.mult, ALU.add).then_inc(vec_done, V.one("om"))
            vec.wait_ge(vec_done, V.done("om", hp))
            ts(cur[:, OM_KIS:OM_KIS + 1], param(KIS), -1.0, 1.0, ALU.mult, ALU.add).then_inc(vec_done, V.one("omk"))
            vec.wait_ge(vec_done, V.done("omk", hp))
            for name in "kr":
                vec.wait_ge(act_done, A.done(("T", name, 1), hp))
                stt(out=Zb[name][:, 1:], in0=Pb[name][:, 0:SEQ - 1], scalar=param(MIX_K if name == "k" else MIX_R), in1=Zb[name][:, 1:], op0=ALU.mult, op1=ALU.add).then_inc(vec_done, V.one(("z", name)))
            vec.wait_ge(act_done, A.done(("sig", 1), hp))
            vec.wait_ge(ya_out, hp * 32 + 1)
            for n in range(SEQ // SCAN):
                part = slice(n * SCAN, (n + 1) * SCAN)
                nc.vector.tensor_tensor_scan(Ls[:, part], e.consts[:, C_RST:C_RST + SCAN], sig[:, part], 0.0, ALU.mult, ALU.add).then_inc(vec_done, V.one(("scan", n)))
            for h in halves:
                vec.wait_ge(pe_done, PE.done(("kkss", h), hp))
                ts(rs_kk[:, hs[h]], bank[BANKS["kkss"][h]], 1e-24, None, ALU.max).then_inc(vec_done, V.one(("kkmax", h)))
            vec.wait_ge(vec_done, V.done(("scan", SEQ // SCAN - 1), hp))
            tt(sig, Ls, sig, ALU.subtract).then_inc(vec_done, V.one("Lx"))
            b_t = sq
            for h in halves:
                cols = hs[h]
                by_chunk = lambda ap: ap[:, cols].rearrange("p (c t) -> p c t", t=C)
                cs = slice(h * GC, (h + 1) * GC)
                vec.wait_ge(act_done, A.done(("kksd", h), hp))
                nc.vector.reciprocal(rs_kk[:, cols], rs_kk[:, cols]).then_inc(vec_done, V.one(("kkrs", h)))
                vec.wait_ge(vec_done, V.done(("kkrs", h), hp))
                stt(out=kk_t[:, cols], in0=k_t[:, cols], scalar=param(KNS), in1=rs_kk[:, cols], op0=ALU.mult, op1=ALU.mult).then_inc(vec_done, V.one(("kk", h)))
                vec.wait_ge(vec_done, V.done(("kk", h), hp))
                vec.wait_ge(act_done, A.done(("a", h), hp))
                tt(b_t[:, cols], kk_t[:, cols], a_t[:, cols], ALU.mult).then_inc(vec_done, V.one(("b", h)))
                vec.wait_ge(vec_done, V.done(("b", h), hp))
                vec.wait_ge(act_done, A.done("Linv", hp))
                tt(BK[:, cs, 0:C], by_chunk(b_t), by_chunk(Linv), ALU.mult).then_inc(vec_done, V.one(("bt", h)))
                vec.wait_ge(act_done, A.done("Lamx", hp))
                tt(QR[:, cs, 0:C], by_chunk(kk_t), by_chunk(Lamx), ALU.mult).then_inc(vec_done, V.one(("kq", h)))
                tt(QR[:, cs, C:P], by_chunk(r_t), by_chunk(Lam), ALU.mult).then_inc(vec_done, V.one(("rt", h)))
                ts(a_t[:, cols], a_t[:, cols], param(KIS), param(OM_KIS), ALU.mult, ALU.add).then_inc(vec_done, V.one(("am", h)))
                vec.wait_ge(vec_done, V.done(("am", h), hp))
                tt(k_t[:, cols], k_t[:, cols], a_t[:, cols], ALU.mult).then_inc(vec_done, V.one(("kp", h)))
                vec.wait_ge(vec_done, V.done(("kp", h), hp))
                tt(BK[:, cs, C:P], by_chunk(k_t), by_chunk(Linv), ALU.mult).then_inc(vec_done, V.one(("kt", h)))
            nc.vector.tensor_copy(lamC[:], Lam.rearrange("p (c t) -> p c t", t=C)[:, :, C - 1]).then_inc(vec_done, V.one("lamC"))
            mask4 = bc(mask2, 4)
            xb = {0: (0, 1, 2, 3, 4), 1: (5, 0, 1, 2, 3)}
            quad = lambda b: bank[b].rearrange("p (c t) -> p c t", t=2 * C)
            octo = lambda b: bank[b].rearrange("p (c t) -> p c t", t=C)
            for g in range(G):
                gs = slice(g * GC, (g + 1) * GC)
                if g == 1:
                    vec.wait_ge(act_done, A.done(("T", "v", 1), hp))
                    stt(out=v_t[:, 1:], in0=Pb["v"][:, 0:SEQ - 1], scalar=param(MIX_V), in1=v_t[:, 1:], op0=ALU.mult, op1=ALU.add).then_inc(vec_done, V.one(("z", "v")))
                    vec.wait_ge(vec_done, V.done(("rt", 1), hp))
                    stt(out=r_t[:], in0=r_t[:], scalar=param(BON), in1=k_t[:], op0=ALU.mult, op1=ALU.mult).then_inc(vec_done, V.one("rk"))
                    for j in range(2):
                        vec.wait_ge(bias_in[j], hp * 16 + 16)
                    nc.vector.memset(bias[0:C, :, BAND - C:], MASKED).then_inc(vec_done, V.one(("bmask", 0)))
                    vec.wait_ge(vec_done, V.done(("bmask", 0), hp))
                    nc.vector.memset(bias[C:P, :, 0:C], MASKED).then_inc(vec_done, V.one(("bmask", 1)))
                    vec.wait_ge(vec_done, V.done(("bmask", 1), hp))
                for q in range(2):
                    vec.wait_ge(pe_done, PE.done(("X1", g, q), hp))
                    tt(M1[:, g * GC + 4 * q:g * GC + 4 * q + 4, :], quad(xb[g][q]), mask4, ALU.mult).then_inc(vec_done, V.one(("X1", g, q)))
                    vec.wait_ge(vec_done, V.done(("X1", g, q), hp))
                for q in range(2):
                    vec.wait_ge(pe_done, PE.done(("X2", g, q), hp))
                    tt(M2[:, g * GC + 4 * q:g * GC + 4 * q + 4, :], quad(xb[g][2 + q]), mask4, ALU.mult).then_inc(vec_done, V.one(("X2", g, q)))
                    vec.wait_ge(vec_done, V.done(("X2", g, q), hp))
                vec.wait_ge(pe_done, PE.done(("A", g), hp))
                tt(T[:, gs, :], octo(xb[g][4]), bc(e.consts[:, C_NL1:C_NL1 + C], GC), ALU.mult).then_inc(vec_done, V.one(("A", g)))
                vec.wait_ge(vec_done, V.done(("A", g), hp))
                tt(T[:, gs, :], T[:, gs, :], eye8, ALU.add).then_inc(vec_done, V.one(("T2", g)))
                vec.wait_ge(vec_done, V.done(("T2", g), hp))
                tt(TT[:, gs, :], M1[:, gs, 0:C], bc(e.consts[:, C_NL1T:C_NL1T + C], GC), ALU.mult).then_inc(vec_done, V.one(("T2T0", g)))
                vec.wait_ge(vec_done, V.done(("T2T0", g), hp))
                tt(TT[:, gs, :], TT[:, gs, :], eye8, ALU.add).then_inc(vec_done, V.one(("T2T", g)))
                vec.wait_ge(vec_done, V.done(("T2T", g), hp))
                tt(M1[:, gs, 0:C], M1[:, gs, 0:C], eye8, ALU.add).then_inc(vec_done, V.one(("ATI", g)))
                vec.wait_ge(vec_done, V.done(("ATI", g), hp))
            for m in LEVELS:
                for g in range(G):
                    vec.wait_ge(pe_done, PE.done(("X", m, g), hp))
                    tt(X[:, g * GC:(g + 1) * GC, :], octo(3 * g), level[m], ALU.mult).then_inc(vec_done, V.one(("X", m, g)))
                    vec.wait_ge(vec_done, V.done(("X", m, g), hp))
                if m == 32:
                    for u in range(2):
                        max_vec(vec, hp, u)
                    prob_vec(vec, hp, 0)
            for c in range(NC_):
                vec.wait_ge(pe_done, PE.done(("W", c), hp))
                nc.vector.tensor_copy(Wt[:], bank[4][:, 0:C]).then_inc(vec_done, V.one(("W", c)))
                if c + 1 < NU:
                    prob_vec(vec, hp, c + 1)
                vec.wait_ge(pe_done, PE.done(("U", c), hp))
                ts(Ut[:], bank[4][:, 0:C], -1.0, None, ALU.mult).then_inc(vec_done, V.one(("U", c)))
                vec.wait_ge(pe_done, PE.done(("S", c), hp))
                if c == 0:
                    ts(st_S[:, 1, :], bank[4][:, 0:C], lamC[:, 0:1], None, ALU.mult).then_inc(vec_done, V.one(("S", 0)))
                else:
                    vec.wait_ge(act_done, A.done(("SL", c), hp))
                    stt(out=st_S[:, (c + 1) % 2, :], in0=bank[4][:, 0:C], scalar=lamC[:, c:c + 1], in1=st_L[:], op0=ALU.mult, op1=ALU.add).then_inc(vec_done, V.one(("S", c)))
                if c + 2 < NU:
                    max_vec(vec, hp, c + 2)
                h, s = e_stage(c)
                if h is not None:
                    gn_vec(vec, hp, h, s)
            for s in range(ELEN):
                gn_vec(vec, hp, 1, s)

        def max_vec(vec, hp, u):
            j, i, nk = unit(u)
            b0 = (6 + u) * HALF if u < 2 else 0
            vec.wait_ge(pe_done, PE.done(("sc", u), hp))
            settle(vec, vec_passed)
            nc.vector.tensor_tensor_reduce(out=pe_s[:, u % 2, 0:nk * P], in0=e.banks[:, b0:b0 + nk * P], in1=bias[:, j, BAND - nk * P:],
                                           scale=1.0, scalar=-3e38, op0=ALU.add, op1=ALU.max, accum_out=small[:, 6 + u % 2:7 + u % 2]).then_inc(vec_done, V.one(("ttr", u)))
            vec.wait_ge(vec_done, V.done(("ttr", u), hp))
            nc.vector.tensor_scalar(small[:, 2 + u % 2:3 + u % 2], small[:, 6 + u % 2:7 + u % 2], -1.0, None, ALU.mult).then_inc(vec_done, V.one(("nmx", u)))

        def prob_vec(vec, hp, u):
            nk = unit(u)[2]
            vec.wait_ge(act_done, A.done(("exp", u), hp))
            nc.vector.reciprocal(small[:, u % 2:u % 2 + 1], small[:, 4 + u % 2:5 + u % 2]).then_inc(vec_done, V.one(("rin", u)))
            vec.wait_ge(vec_done, V.done(("rin", u), hp))
            nc.vector.tensor_scalar(pe_s[:, u % 2, 0:nk * P], pe_s[:, u % 2, 0:nk * P], small[:, u % 2:u % 2 + 1], None, ALU.mult).then_inc(vec_done, V.one(("pn", u)))

        Plora = [rs_kk, sq, sig]

        @block.tensor
        def _(pe):
            for n in range(3):
                pe.wait_ge(w_split, n + 1)
                for h in halves:
                    if n == 2:
                        pe.wait_ge(pro_act, LA.done(("pc", 0, h)))
                    last = gemm(nc, bank[(2 * n + h) % 4], e.whi[:, n % 2], e.wlo[:, n % 2], e.ahi, e.alo, range(KT), hs[h])
                    last.then_inc(pro_pe, LP.one(("l", n, h)))
            pe.wait_ge(pro_act, LA.done(("pc", 2, 1)))
            for name, blk in (("r", NB_HEAD), ("k", NB_HEAD + 1)):
                pe.wait_ge(w_split, blk + 1)
                for h in halves:
                    project(pe, blk, name, h).then_inc(pro_pe, LP.one((name, h)))
            pe.sem_inc(pe_done, PE.n)
            pe.wait_ge(pro_act, LA.done(("sg", 1)))
            with pe.Fori(0, HP) as hp:
                mix_pe(pe, hp)
            LP.close()
            PE.close()

        @block.scalar
        def _(act):
            for n in range(3):
                for h in halves:
                    act.wait_ge(pro_pe, LP.done(("l", n, h)))
                    if h == 1:
                        act.sem_inc(w_used, 1)
                    nc.scalar.activation(Plora[n][:, hs[h]], bank[(2 * n + h) % 4], ACT.Copy).then_inc(pro_act, LA.one(("pc", n, h)))
            act.wait_ge(pro_vec, LV.done(("z", 0)))
            nc.scalar.activation(lora[0:C, :], lora[0:C, :], ACT.Tanh).then_inc(pro_act, LA.one("tanh"))
            for n in range(2):
                act.wait_ge(pro_vec, LV.done(("z", n + 1)))
                nc.scalar.activation(sg[:, n, :], sg[:, n, :], ACT.Sigmoid).then_inc(pro_act, LA.one(("sg", n)))
            act.dma_start(lup[:], e.lora_up[0]).then_inc(lup_in, 16)
            for name in "rk":
                act.wait_ge(pro_pe, LP.done((name, 1)))
                act.sem_inc(w_used, 1)
                for h in halves:
                    nc.scalar.activation(Pb[name][:, hs[h]], bank[BANKS[name][h]], ACT.Copy).then_inc(pro_act, LA.one(("P", name, h)))
            act.wait_ge(pro_act, LA.done(("P", "k", 1)))
            act.sem_inc(ya_out, 1)
            act.sem_inc(yb_out, 1)
            act.sem_inc(act_done, A.n)
            with act.Fori(0, HP) as hp:
                mix_act(act, hp)
            act.wait_ge(yb_out, HP * 16 + 1)
            act.wait_ge(ya_out, HP * 32 + 1)
            LA.close()
            A.close()

        @block.vector
        def _(vec):
            for j in range(2):
                nc.vector.memset(qz[rows[1 - j], j, :], 0.0).then_inc(pro_vec, LV.one(f"qzero{j}"))
            nc.vector.tensor_scalar(cur[:, 0:3], e.par[:, Q_LORA:Q_LORA + 3], -1.0, 1.0, ALU.mult, ALU.add).then_inc(pro_vec, LV.one("omm"))
            vec.wait_ge(pro_vec, LV.done("omm"))
            dst = [lora[:], sg[:, 0, :], sg[:, 1, :]]
            for n in range(3):
                vec.wait_ge(pro_act, LA.done(("pc", n, 1)))
                nc.vector.tensor_scalar(dst[n], Plora[n], cur[:, n:n + 1], None, ALU.mult).then_inc(pro_vec, LV.one(("t", n)))
                vec.wait_ge(pro_vec, LV.done(("t", n)))
                nc.vector.scalar_tensor_tensor(out=dst[n][:, 1:], in0=Plora[n][:, 0:SEQ - 1], scalar=e.par[:, Q_LORA + n:Q_LORA + n + 1],
                                                   in1=dst[n][:, 1:], op0=ALU.mult, op1=ALU.add).then_inc(pro_vec, LV.one(("z", n)))
            vec.wait_ge(pro_vec, LV.done(("z", 2)))
            vec.sem_inc(vec_done, V.n)
            with vec.Fori(0, HP) as hp:
                mix_vec(vec, hp)
            LV.close()
            V.close()


def merge_phase(e):
    nc = e.nc
    with ExitStack() as ctx:
        yhi = e.sb("y_hi", [P, KT, SEQ], F32R, ctx)
        ylo = e.sb("y_lo", [P, KT, SEQ], F32R, ctx)
        sg = e.sb("gates", [P, 4, SEQ], ctx=ctx)
        y_in = sems(nc, e.ctx, *[f"y_in{k}" for k in range(KT)])
        y_hi, y_lo = sems(nc, e.ctx, "y_high", "y_low")
        gate_mm, y_mm, gate_sig, y_gated, y_added = sems(nc, e.ctx, "gate_mm", "y_mm", "gate_sig", "y_gated", "y_added")
        hs = [slice(0, HALF), slice(HALF, SEQ)]
        gate_banks, y_banks = ((5, 0), (1, 4)), ((2, 3), (6, 7))
        slots = ((NB_GA) % 2, (NB_GA + 1) % 2)
        TILES = 2 * KT
        block = ctx.enter_context(nc.Block())
        start_weights(e, block, NB_GA, 2 * TILES - 2)

        @block.tensor
        def _(pe):
            def gate(u, at):
                pe.wait_ge(e.w_split, at * 2 + (NB_GA + 2 * u + 1))
                pe.wait_ge(gate_sig, at * 2 + (2 * u + 2))
                for h in range(2):
                    gemm(nc, e.ps[gate_banks[u % 2][h]], e.whi[:, slots[0]], e.wlo[:, slots[0]], e.ahi, e.alo, range(KT), hs[h]).then_inc(gate_mm, 1)

            def branch(u, slot):
                for h in range(2):
                    gemm(nc, e.ps[y_banks[u % 2][h]], e.whi[:, slot], e.wlo[:, slot], yhi, ylo, range(KT), hs[h]).then_inc(y_mm, 1)

            with pe.Fori(0, KT // 4) as i:
                for u in range(4):
                    gate(u, i * 4)
                    pe.wait_ge(y_lo, KT)
                    pe.wait_ge(e.w_split, i * 8 + (NB_GA + 2 * u + 2))
                    pe.wait_ge(y_gated, i * 8 + (2 * u + 2))
                    branch(u, slots[1])
            for j in range(KT, TILES):
                if j < TILES - 2:
                    gate(j % 4, j // 4 * 4)
                nb = min(NB_GA + 2 * j + 1, NB_GA + TILES - 2 + j)
                pe.wait_ge(y_lo, 2 * KT)
                pe.wait_ge(e.w_split, nb + 1)
                pe.wait_ge(y_gated, 2 * j + 2)
                branch(j % 4, nb % 2)

        @block.scalar
        def _(act):
            def load_y(b):
                for k in range(KT):
                    act.dma_start(ylo[:, k].bitcast(F32), (e.ya_d, e.yb_d)[b][k]).then_inc(y_in[k], 16)

            def high_y(b):
                for k in range(KT):
                    act.wait_ge(y_in[k], 16 * (b + 1))
                    nc.scalar.activation(yhi[:, k], ylo[:, k].bitcast(F32), ACT.Copy).then_inc(y_hi, 1)

            def sigmoid(n, h):
                nc.scalar.activation(sg[:, n % 4, hs[h]], e.ps[gate_banks[n % 2][h]], ACT.Sigmoid).then_inc(gate_sig, 1)

            def turn(u, at):
                act.wait_ge(y_gated, at * 2 + (2 * u + 2))
                if not isinstance(at, int) or at >= KT:
                    act.wait_ge(y_added, at * 2 + (2 * u + 2))
                for h in range(2):
                    act.wait_ge(gate_mm, at * 2 + (2 * u + h + 1))
                    if h == 1:
                        act.sem_inc(e.w_used, 1)
                    sigmoid(u + 2, h)
                act.wait_ge(y_mm, at * 2 + (2 * u + 2))
                act.sem_inc(e.w_used, 1)

            for h in range(2):
                sigmoid(0, h)
            load_y(0)
            for h in range(2):
                sigmoid(1, h)
            high_y(0)
            with act.Fori(0, KT // 4) as i:
                for u in range(4):
                    turn(u, i * 4)
            load_y(1)
            high_y(1)
            for j in range(KT, TILES):
                if j < TILES - 2:
                    turn(j % 4, j // 4 * 4)
                else:
                    act.wait_ge(y_mm, 2 * j + 2)
                    act.sem_inc(e.w_used, 1)

        @block.vector
        def _(vec):
            tt = nc.vector.tensor_tensor

            def low_y(b):
                for k in range(KT):
                    vec.wait_ge(y_hi, b * KT + k + 1)
                    tt(ylo[:, k], ylo[:, k].bitcast(F32), yhi[:, k].bitcast(F32), ALU.subtract).then_inc(y_lo, 1)

            vec.sem_inc(y_gated, 4)
            vec.sem_inc(y_added, 4)
            low_y(0)
            with vec.Fori(0, KT // 4) as i:
                for u in range(4):
                    for h in range(2):
                        m = e.mo[:, bass.ds(i * 4 + u, 1), hs[h]].rearrange("p a t -> p (a t)")
                        vec.wait_ge(gate_sig, i * 8 + (2 * u + h + 1))
                        vec.wait_ge(y_mm, i * 8 + (2 * u + h + 1))
                        tt(m, e.ps[y_banks[u % 2][h]], sg[:, u, hs[h]], ALU.mult).then_inc(y_gated, 1)
                    vec.sem_inc(y_added, 2)
            low_y(1)
            for j in range(KT, TILES):
                for h in range(2):
                    m, g = e.mo[:, j - KT, hs[h]], sg[:, j % 4, hs[h]]
                    vec.wait_ge(gate_sig, 2 * j + h + 1)
                    vec.wait_ge(y_mm, 2 * j + h + 1)
                    tt(g, e.ps[y_banks[j % 2][h]], g, ALU.mult).then_inc(y_gated, 1)
                    vec.wait_ge(y_gated, 4 + 2 * j + h + 1)
                    tt(m, m, g, ALU.add).then_inc(y_added, 1)


def project_phase(e, tag, first, per_block, split_first):
    nc = e.nc
    kts = KT // per_block
    nb = 2 * per_block
    rounds = KT // nb
    with ExitStack() as ctx:
        w_split, w_used = e.w_split, e.w_used
        sa, sv, sp_, hi_done, lo_done = sems(nc, e.ctx, f"{tag}_act", f"{tag}_vec", f"{tag}_pe", f"{tag}_hi", f"{tag}_lo")
        A = Steps(sa, [(n, h) for n in range(nb) for h in range(2)], True)
        PE = Steps(sp_, [(n, h) for n in range(nb) for h in range(2)], True)
        block = ctx.enter_context(nc.Block())
        start_weights(e, block, first, KT // per_block)
        hs = [slice(0, HALF), slice(HALF, SEQ)]

        @block.vector
        def _(vec):
            if split_first:
                for k in range(KT):
                    vec.wait_ge(hi_done, k + 1)
                    nc.vector.tensor_tensor(e.alo[:, k], e.mo[:, k], e.ahi[:, k].bitcast(F32), ALU.subtract).then_inc(lo_done, 1)

        @block.scalar
        def _(act):
            act.sem_inc(sa, A.n)
            if split_first:
                for k in range(KT):
                    nc.scalar.activation(e.ahi[:, k], e.mo[:, k], ACT.Copy).then_inc(hi_done, 1)
                act.wait_ge(lo_done, KT)
            with act.Fori(0, rounds) as i:
                for n in range(nb):
                    for h in range(2):
                        act.wait_ge(PE.sem, PE.done((n, h), i))
                        if h == 1 and n % per_block == per_block - 1:
                            act.sem_inc(w_used, 1)
                        dst = e.mo[:, bass.ds(i * nb + n, 1), hs[h]].rearrange("p a t -> p (a t)")
                        nc.scalar.activation(dst, e.ps[2 * n + h], ACT.Copy).then_inc(sa, A.one((n, h)))
            A.close()

        @block.tensor
        def _(pe):
            pe.sem_inc(sp_, PE.n)
            with pe.Fori(0, rounds) as i:
                for n in range(nb):
                    s, off = n // per_block, n % per_block * kts
                    slot = (first + s) % 2
                    pe.wait_ge(w_split, i * 2 + (first + s + 1))
                    pe.wait_ge(A.sem, A.done((n, 1), i, 1))
                    if split_first:
                        for k in range(kts):
                            pe.wait_ge(lo_done, k + 1)
                            for h in range(2):
                                last = mm3(nc, e.ps[2 * n + h], e.whi[:, slot, off + k], e.wlo[:, slot, off + k], e.ahi[:, k, hs[h]], e.alo[:, k, hs[h]], k == 0, k == kts - 1)
                                if k == kts - 1:
                                    last.then_inc(sp_, PE.one((n, h)))
                        continue
                    for h in range(2):
                        gemm(nc, e.ps[2 * n + h], e.whi[:, slot, off:off + kts], e.wlo[:, slot, off:off + kts], e.ahi, e.alo, range(kts), hs[h]).then_inc(sp_, PE.one((n, h)))
            PE.close()


def finish_phase(e, tag, g_row, x_in, x_out, gain):
    nc = e.nc
    with ExitStack() as ctx:
        tok = e.sb(f"{tag}_tok", [P, NT, D], ctx=ctx)
        xr = e.sb(f"{tag}_x", [P, NT, D], ctx=ctx)
        junk = e.sb(f"{tag}_squares", [P, D], ctx=ctx)
        gpost = e.sb(f"{tag}_gain", [P, D], ctx=ctx)
        st = e.sb(f"{tag}_stats", [P, 32], ctx=ctx)
        sa, sv, sp_, pool_sum, g_in = sems(nc, e.ctx, f"{tag}_act", f"{tag}_vec", f"{tag}_pe", f"{tag}_pool", f"{tag}_g_in")
        x_ld, x_st = e.x_loaded, e.x_stored
        ld_value, st_value = 16 * (g_row + 2), 16 * (g_row + 1)
        names = lambda *parts: sum((Norm.steps("n", part, g, NT) for part, g in parts), []) if gain is not None else []
        quad = lambda g: range(4 * g, 4 * g + 4)
        a_sq = lambda g: [("psq", i) for i in quad(g)]
        A = Steps(sa, a_sq(0) + [("psd", 0)] + a_sq(1) + [("psd", 1)] + names(("sq", 0), ("sd", 0), ("sq", 1), ("sd", 1), ("hi", 0), ("hi", 1)))
        v_res = lambda g: [("pms", g), ("prs", g)] + [("g", i) for i in quad(g)] + [("res", i) for i in quad(g)[::2]]
        V = Steps(sv, v_res(0) + v_res(1)
                  + names(("rs", 0), ("xn", 0), ("rs", 1), ("xn", 1), ("lo", 0), ("lo", 1)))
        PE = Steps(sp_, [("tok", i) for i in range(NT)] + names(("T", 0), ("T", 1)))
        R = Steps(pool_sum, [("res", i) for i in range(1, NT, 2)])
        norm = Norm(e, "n", tok, NT, st, junk[:], gain, e.ahi, e.alo, A, V, PE, xn=xr)

        def in_banks(i):
            return e.banks[:, i % 4 * D:(i % 4 + 1) * D]

        def summed(eng, i):
            if i % 2:
                eng.wait_ge(pool_sum, R.done(("res", i)))
            else:
                eng.wait_ge(sv, V.done(("res", i)))

        def squares_ready(act, i):
            summed(act, i)
            if i == 0:
                act.wait_ge(sa, A.done(("psq", NT - 1)))

        block = ctx.enter_context(nc.Block())

        @block.sync
        def _(sp):
            sp.dma_start(gpost[:], bass.AP(tensor=e.g_rows.tensor, offset=g_row * D, ap=[[0, P], [1, D]])).then_inc(g_in, 16)
            for i in range(NT):
                sp.dma_start(xr[:, i], x_in[i * P:(i + 1) * P, :]).then_inc(x_ld[i], 16)
            for i in range(NT):
                summed(sp, i)
                sp.dma_start(x_out[i * P:(i + 1) * P, :], tok[:, i]).then_inc(x_st[i], 16)
            for i in range(NT):
                sp.wait_ge(x_st[i], st_value)

        @block.tensor
        def _(pe):
            for i in range(NT):
                if i >= 4:
                    pe.wait_ge(sv, V.done(("g", i - 4)))
                for kt in range(KT):
                    last = nc.tensor.transpose(in_banks(i)[:, kt * P:(kt + 1) * P], e.mo[:, kt, i * P:(i + 1) * P], e.ident)
                last.then_inc(sp_, PE.one(("tok", i)))
            if gain is not None:
                pe.wait_ge(sv, V.done(("g", NT - 1)))
                for g in range(2):
                    norm.transposes(pe, g)
            PE.close()

        @block.scalar
        def _(act):
            def post_squares(g):
                for i in quad(g):
                    act.wait_ge(sp_, PE.done(("tok", i)))
                    if i:
                        act.wait_ge(sa, A.done(("psq", i - 1)))
                    nc.scalar.activation(junk[:], in_banks(i), ACT.Square, accum_out=st[:, 16 + i:17 + i]).then_inc(sa, A.one(("psq", i)))

            def post_roots(g):
                act.wait_ge(sv, V.done(("pms", g)))
                nc.scalar.activation(st[:, 24 + 4 * g:28 + 4 * g], st[:, 16 + 4 * g:20 + 4 * g], ACT.Sqrt).then_inc(sa, A.one(("psd", g)))

            post_squares(0)
            post_roots(0)
            post_squares(1)
            post_roots(1)
            if gain is not None:
                for g in range(2):
                    norm.squares(act, g, squares_ready)
                    norm.roots(act, g)
                for g in range(2):
                    norm.high(act, g)
            A.close()

        @block.vector
        def _(vec):
            def post_scales(g):
                part = st[:, 16 + 4 * g:20 + 4 * g]
                vec.wait_ge(sa, A.done(("psq", 4 * g + 3)))
                nc.vector.tensor_scalar(part, part, 1.0 / D, EPS, ALU.mult, ALU.add).then_inc(sv, V.one(("pms", g)))
                vec.wait_ge(sa, A.done(("psd", g)))
                nc.vector.reciprocal(part, st[:, 24 + 4 * g:28 + 4 * g]).then_inc(sv, V.one(("prs", g)))
                vec.wait_ge(sv, V.done(("prs", g)))

            def gains_and_sums(g):
                for i in quad(g):
                    nc.vector.scalar_tensor_tensor(out=tok[:, i], in0=in_banks(i), scalar=st[:, 16 + i:17 + i], in1=gpost[:],
                                                   op0=ALU.mult, op1=ALU.mult).then_inc(sv, V.one(("g", i)))
                for i in quad(g)[::2]:
                    vec.wait_ge(x_ld[i], ld_value)
                    vec.wait_ge(sv, V.done(("g", i)))
                    nc.vector.tensor_tensor(tok[:, i], tok[:, i], xr[:, i], ALU.add).then_inc(sv, V.one(("res", i)))

            post_scales(0)
            vec.wait_ge(g_in, 16)
            gains_and_sums(0)
            post_scales(1)
            gains_and_sums(1)
            if gain is not None:
                for g in range(2):
                    norm.scales(vec, g)
                    norm.normalise(vec, g)
                for g in range(2):
                    norm.low(vec, g)
            V.close()

        @block.gpsimd
        def _(pool):
            for i in range(1, NT, 2):
                pool.wait_ge(x_ld[i], ld_value)
                pool.wait_ge(sv, V.done(("g", i)))
                nc.gpsimd.tensor_tensor(tok[:, i], tok[:, i], xr[:, i], ALU.add).then_inc(pool_sum, R.one(("res", i)))
            R.close()


def cross_phase(e):
    nc = e.nc
    with ExitStack() as ctx:
        sb = lambda name, shape, dt=F32: e.sb(name, shape, dt, ctx)
        mt = sb("mem_tok", [P, 2, D])
        mhi = sb("mem_hi", [P, KT, MEM], F32R)
        mlo = sb("mem_lo", [P, KT, MEM], F32R)
        km = sb("mem_k", [P, MH, MEM])
        vmc = sb("mem_v_cm", [P, MH, MEM])
        vm = sb("mem_v_tok", [P, 2, MH * P])
        q = sb("cross_q", [P, MH, SEQ])
        o = sb("cross_o", [P, MH, SEQ])
        pr = sb("cross_probs", [P, 4, MEM])
        pT = sb("cross_probs_T", [P, 2, MEM])
        small = sb("cross_small", [P, 4, 4])
        junk = sb("cross_squares", [P, D])
        st = sb("cross_stats", [P, 16])
        w_split, w_used = e.w_split, e.w_used
        m_in = sems(nc, e.ctx, "mem_in0", "mem_in1")
        sa, sv, sp_ = sems(nc, e.ctx, "cross_act", "cross_vec", "cross_pe")
        names = lambda *parts: sum((Norm.steps("m", part, 0, 2) for part in parts), [])
        NUC = MH * NT
        kvq = []
        for n in range(MH):
            kvq += [("q", n, 0), ("q", n, 1), ("kv", 2 * n), ("kv", 2 * n + 1)]
        a_names = names("sq", "sd") + kvq[:2] + names("hi") + kvq[2:] + ["vm0", "vm1"]
        v_names = names("rs", "xn", "lo")
        p_names = kvq[:2] + names("T") + kvq[2:] + ["vm0", "vm1"]
        LAST = NUC + 4
        is_unit = lambda u: 0 <= u < NUC
        for u in range(LAST):
            p_names += [("s", u)] * is_unit(u) + [("pT", u - 3)] * is_unit(u - 3) + [("out", u - 4)] * is_unit(u - 4)
            v_names += [("mx", u), ("nmx", u)] * is_unit(u) + [("rin", u - 2), ("pn", u - 2)] * is_unit(u - 2)
            a_names += [("exp", u - 1)] * is_unit(u - 1) + [("pT", u - 3)] * is_unit(u - 3) + [("out", u - 4)] * is_unit(u - 4)
            if is_unit(u - 4) and (u - 4) % NT == NT - 1:
                v_names += [("hi", (u - 4) // NT), ("lo", (u - 4) // NT)]
        A, V, PE = Steps(sa, a_names), Steps(sv, v_names), Steps(sp_, p_names)
        norm = Norm(e, "m", mt, 2, st, junk[:], e.par[:, Q_MEM:Q_MEM + KT], mhi, mlo, A, V, PE, 4, 4)
        hs = [slice(0, HALF), slice(HALF, SEQ)]
        block = ctx.enter_context(nc.Block())
        start_weights(e, block, NB_MEM, 3 * MH, both=False)

        @block.tensor
        def _(pe):
            at = NB_MEM
            for n in range(MH):
                pe.wait_ge(w_split, at + 1)
                if n >= 2:
                    pe.wait_ge(A.sem, A.done(("q", n - 2, 1)))
                for h in range(2):
                    gemm(nc, e.ps[2 * (n % 2) + h], e.whi[:, at % 2], e.wlo[:, at % 2], e.ahi, e.alo, range(KT), hs[h]).then_inc(sp_, PE.one(("q", n, h)))
                at += 1
                if n == 0:
                    norm.transposes(pe, 0)
                for m in (2 * n, 2 * n + 1):
                    pe.wait_ge(w_split, at + 1)
                    if m == 0:
                        pe.wait_ge(V.sem, V.done(("m", "lo", KT - 1, 0)))
                    if m >= 4:
                        pe.wait_ge(A.sem, A.done(("kv", m - 4)))
                    gemm(nc, e.ps[4 + m % 4][:, 0:MEM], e.whi[:, at % 2], e.wlo[:, at % 2], mhi, mlo, range(KT), slice(0, MEM)).then_inc(sp_, PE.one(("kv", m)))
                    at += 1
            for g in range(2):
                pe.wait_ge(A.sem, A.done(("kv", 7)))
                for n in range(MH):
                    last = nc.tensor.transpose(e.ps[4 + g][:, n * P:(n + 1) * P], vmc[:, n, g * P:(g + 1) * P], e.ident)
                last.then_inc(sp_, PE.one(f"vm{g}"))
            for u in range(LAST):
                if is_unit(u):
                    hd, i = u // NT, u % NT
                    if u == 0:
                        pe.wait_ge(A.sem, A.done(("q", MH - 1, 1)))
                    if u >= 4:
                        pe.wait_ge(A.sem, A.done(("exp", u - 4)))
                    nc.tensor.matmul(e.ps[u % 4][:, 0:MEM], q[:, hd, i * P:(i + 1) * P], km[:, hd, :], start=True, stop=True).then_inc(sp_, PE.one(("s", u)))
                v = u - 3
                if is_unit(v):
                    pe.wait_ge(V.sem, V.done(("pn", v)))
                    pe.wait_ge(A.sem, A.done(("pT", v - 2) if v >= 2 else "vm1"))
                    for t in range(2):
                        last = nc.tensor.transpose(e.ps[4 + v % 2][:, t * P:(t + 1) * P], pr[:, v % 4, t * P:(t + 1) * P], e.ident)
                    last.then_inc(sp_, PE.one(("pT", v)))
                v = u - 4
                if is_unit(v):
                    hd = v // NT
                    pe.wait_ge(A.sem, A.done(("pT", v)))
                    if v >= 2:
                        pe.wait_ge(A.sem, A.done(("out", v - 2)))
                    for t in range(2):
                        last = nc.tensor.matmul(e.ps[6 + v % 2][:, 0:P], vm[:, t, hd * P:(hd + 1) * P], pT[:, v % 2, t * P:(t + 1) * P], start=t == 0, stop=t == 1)
                    last.then_inc(sp_, PE.one(("out", v)))
            PE.close()

        @block.scalar
        def _(act):
            for i in range(2):
                act.dma_start(mt[:, i], e.mem[i * P:(i + 1) * P, :]).then_inc(m_in[i], 16)
            norm.squares(act, 0, lambda eng, i: eng.wait_ge(m_in[i], 16))
            norm.roots(act, 0)
            for n in range(MH):
                for h in range(2):
                    act.wait_ge(PE.sem, PE.done(("q", n, h)))
                    if h == 1:
                        act.sem_inc(w_used, 1)
                    nc.scalar.activation(q[:, n, hs[h]], e.ps[2 * (n % 2) + h], ACT.Copy, scale=float(P) ** -0.5).then_inc(sa, A.one(("q", n, h)))
                if n == 0:
                    norm.high(act, 0)
                for m in (2 * n, 2 * n + 1):
                    act.wait_ge(PE.sem, PE.done(("kv", m)))
                    act.sem_inc(w_used, 1)
                    dst = km[:, m] if m < 4 else vmc[:, m - 4]
                    nc.scalar.activation(dst, e.ps[4 + m % 4][:, 0:MEM], ACT.Copy).then_inc(sa, A.one(("kv", m)))
            for g in range(2):
                act.wait_ge(PE.sem, PE.done(f"vm{g}"))
                nc.scalar.activation(vm[:, g], e.ps[4 + g], ACT.Copy).then_inc(sa, A.one(f"vm{g}"))
            for u in range(LAST):
                v = u - 1
                if is_unit(v):
                    act.wait_ge(V.sem, V.done(("nmx", v)))
                    if v >= 4:
                        act.wait_ge(PE.sem, PE.done(("pT", v - 4)))
                    nc.scalar.activation(pr[:, v % 4], e.ps[v % 4][:, 0:MEM], ACT.Exp, bias=small[:, v % 4, 1:2],
                                         accum_out=small[:, v % 4, 2:3]).then_inc(sa, A.one(("exp", v)))
                v = u - 3
                if is_unit(v):
                    act.wait_ge(PE.sem, PE.done(("pT", v)))
                    if v >= 2:
                        act.wait_ge(PE.sem, PE.done(("out", v - 2)))
                    nc.scalar.activation(pT[:, v % 2], e.ps[4 + v % 2][:, 0:MEM], ACT.Copy).then_inc(sa, A.one(("pT", v)))
                v = u - 4
                if is_unit(v):
                    hd, i = v // NT, v % NT
                    act.wait_ge(PE.sem, PE.done(("out", v)))
                    nc.scalar.activation(o[:, hd, i * P:(i + 1) * P], e.ps[6 + v % 2][:, 0:P], ACT.Copy).then_inc(sa, A.one(("out", v)))
            A.close()

        @block.vector
        def _(vec):
            norm.scales(vec, 0)
            norm.normalise(vec, 0)
            low_block(vec, e, (NB_MEM + 1) % 2, NB_MEM + 2)
            norm.low(vec, 0)
            b = NB_MEM + 2
            pairs = (3 * MH - 1) // 2
            with vec.Fori(0, pairs) as i:
                for s in range(2):
                    low_block(vec, e, (b + s) % 2, i * 2 + (b + s + 1))
            low_block(vec, e, (b + 2 * pairs) % 2, b + 2 * pairs + 1)
            for u in range(LAST):
                if is_unit(u):
                    vec.wait_ge(PE.sem, PE.done(("s", u)))
                    nc.vector.reduce_max(small[:, u % 4, 0:1], e.ps[u % 4][:, 0:MEM], mybir.AxisListType.X).then_inc(sv, V.one(("mx", u)))
                    vec.wait_ge(V.sem, V.done(("mx", u)))
                    nc.vector.tensor_scalar(small[:, u % 4, 1:2], small[:, u % 4, 0:1], -1.0, None, ALU.mult).then_inc(sv, V.one(("nmx", u)))
                v = u - 2
                if is_unit(v):
                    vec.wait_ge(A.sem, A.done(("exp", v)))
                    nc.vector.reciprocal(small[:, v % 4, 3:4], small[:, v % 4, 2:3]).then_inc(sv, V.one(("rin", v)))
                    vec.wait_ge(V.sem, V.done(("rin", v)))
                    nc.vector.tensor_scalar(pr[:, v % 4], pr[:, v % 4], small[:, v % 4, 3:4], None, ALU.mult).then_inc(sv, V.one(("pn", v)))
                v = u - 4
                if is_unit(v) and v % NT == NT - 1:
                    hd = v // NT
                    vec.wait_ge(A.sem, A.done(("out", v)))
                    nc.vector.tensor_copy(e.ahi[:, hd], o[:, hd]).then_inc(sv, V.one(("hi", hd)))
                    vec.wait_ge(V.sem, V.done(("hi", hd)))
                    nc.vector.tensor_tensor(e.alo[:, hd], o[:, hd], e.ahi[:, hd].bitcast(F32), ALU.subtract).then_inc(sv, V.one(("lo", hd)))
            V.close()


def ffn_phase(e):
    nc = e.nc
    with ExitStack() as ctx:
        ghi = e.sb("hidden_hi", [P, KT, SEQ], F32R, ctx)
        glo = e.sb("hidden_lo", [P, KT, SEQ], F32R, ctx)
        sg = e.sb("silu", [P, 2, SEQ], ctx=ctx)
        w_split, w_used = e.w_split, e.w_used
        hs = [slice(0, HALF), slice(HALF, SEQ)]
        S = []
        for n in range(len(FGROUPS)):
            s = sems(nc, e.ctx, *[f"ffn_{x}{n}" for x in ("in_act", "in_vec", "in_pe", "out_vec", "out_pe")])
            kh = [(k, h) for k in range(2) for h in range(2)]
            S.append((Steps(s[0], [("silu",) + x for x in kh], True),
                      Steps(s[1], [(m,) + x for x in kh for m in ("prod", "hi", "lo")], True),
                      Steps(s[2], [(m, k, h) for k in range(2) for m in ("gate", "up") for h in range(2)], True),
                      Steps(s[3], [("acc",) + x for x in kh], True),
                      Steps(s[4], [("out",) + x for x in kh], True)))
        block = ctx.enter_context(nc.Block())
        start_weights(e, block, NB_FFN, 2 * FT + KT * len(FGROUPS))

        @block.tensor
        def _(pe):
            at = NB_FFN
            for n, (f0, nf) in enumerate(FGROUPS):
                A, V, PE, OV, OPE = S[n]
                pe.sem_inc(PE.sem, PE.n)
                with pe.Fori(0, nf // 2) as i:
                    for k in range(2):
                        for m, name in enumerate(("gate", "up")):
                            pe.wait_ge(w_split, i * 4 + (at + 2 * k + m + 1))
                            pe.wait_ge(A.sem, A.done(("silu", k, 1), i, 1)) if m == 0 else pe.wait_ge(V.sem, V.done(("prod", k, 1), i, 1))
                            for h in range(2):
                                gemm(nc, e.ps[4 * k + 2 * m + h], e.whi[:, (at + m) % 2], e.wlo[:, (at + m) % 2], e.ahi, e.alo, range(KT), hs[h]).then_inc(PE.sem, PE.one((name, k, h)))
                PE.close()
                at += 2 * nf
                pe.wait_ge(V.sem, V.done(("lo", 1, 1), nf // 2 - 1))
                pe.sem_inc(OPE.sem, OPE.n)
                with pe.Fori(0, KT // 2) as i:
                    for k in range(2):
                        pe.wait_ge(w_split, i * 2 + (at + k + 1))
                        pe.wait_ge(OV.sem, OV.done(("acc", k, 1), i, 1))
                        for h in range(2):
                            gemm(nc, e.ps[2 * k + h], e.whi[:, (at + k) % 2], e.wlo[:, (at + k) % 2], ghi, glo, range(nf), hs[h]).then_inc(OPE.sem, OPE.one(("out", k, h)))
                OPE.close()
                at += KT
                pe.wait_ge(OV.sem, OV.done(("acc", 1, 1), KT // 2 - 1))

        @block.scalar
        def _(act):
            for n, (f0, nf) in enumerate(FGROUPS):
                A, V, PE, OV, OPE = S[n]
                act.sem_inc(A.sem, A.n)
                with act.Fori(0, nf // 2) as i:
                    for k in range(2):
                        act.wait_ge(V.sem, V.done(("lo", k, 1), i, 1))
                        for h in range(2):
                            act.wait_ge(PE.sem, PE.done(("gate", k, h), i))
                            if h == 1:
                                act.sem_inc(w_used, 1)
                            nc.scalar.activation(sg[:, k, hs[h]], e.ps[4 * k + h], ACT.Silu).then_inc(A.sem, A.one(("silu", k, h)))
                        act.wait_ge(PE.sem, PE.done(("up", k, 1), i))
                        act.sem_inc(w_used, 1)
                A.close()
                with act.Fori(0, KT // 2) as i:
                    for k in range(2):
                        act.wait_ge(OPE.sem, OPE.done(("out", k, 1), i))
                        act.sem_inc(w_used, 1)

        @block.vector
        def _(vec):
            tt = nc.vector.tensor_tensor
            for n, (f0, nf) in enumerate(FGROUPS):
                A, V, PE, OV, OPE = S[n]
                vec.sem_inc(V.sem, V.n)
                vec.sem_inc(OV.sem, OV.n)
                if n > 0:
                    vec.wait_ge(S[n - 1][4].sem, S[n - 1][4].done(("out", 1, 1), KT // 2 - 1))
                with vec.Fori(0, nf // 2) as i:
                    for k in range(2):
                        for h in range(2):
                            vec.wait_ge(A.sem, A.done(("silu", k, h), i))
                            vec.wait_ge(PE.sem, PE.done(("up", k, h), i))
                            g = sg[:, k, hs[h]]
                            hi, lo = (t[:, bass.ds(i * 2 + k, 1), hs[h]].rearrange("p a t -> p (a t)") for t in (ghi, glo))
                            tt(g, e.ps[4 * k + 2 + h], g, ALU.mult).then_inc(V.sem, V.one(("prod", k, h)))
                            vec.wait_ge(V.sem, V.done(("prod", k, h), i))
                            nc.vector.tensor_copy(hi, g).then_inc(V.sem, V.one(("hi", k, h)))
                            vec.wait_ge(V.sem, V.done(("hi", k, h), i))
                            tt(lo, g, hi.bitcast(F32), ALU.subtract).then_inc(V.sem, V.one(("lo", k, h)))
                V.close()
                with vec.Fori(0, KT // 2) as i:
                    for k in range(2):
                        for h in range(2):
                            m = e.mo[:, bass.ds(i * 2 + k, 1), hs[h]].rearrange("p a t -> p (a t)")
                            vec.wait_ge(OPE.sem, OPE.done(("out", k, h), i))
                            if n == 0:
                                nc.vector.tensor_copy(m, e.ps[2 * k + h]).then_inc(OV.sem, OV.one(("acc", k, h)))
                            else:
                                tt(m, e.ps[2 * k + h], m, ALU.add).then_inc(OV.sem, OV.one(("acc", k, h)))
                OV.close()


def blocks_of(np, w):
    k, n = w.shape
    return w.reshape(k // P, P, n // P, P).transpose(2, 1, 0, 3)


def lay_out(np, i):
    a = {k: np.ascontiguousarray(v[0]) if k not in ("x", "mem") else v[0] for k, v in i.items()}
    win = a["w_in"]
    w = D
    col = lambda s, n: blocks_of(np, win[:, s:s + n])
    r, k, v = (col(w * n, w) for n in range(3))
    lora = np.zeros((D, 3 * P), win.dtype)
    lora[:, 0:288] = win[:, 3072:3360]
    aq, ak, av, ga, gb = (col(3360 + w * n, w) for n in range(5))
    ahead = [np.concatenate([r[1:], ga[0:1]]), np.concatenate([k[1:], ga[1:2]])]
    heads = np.stack([v, aq, av, ak] + ahead, 1).reshape(6 * HP, P, KT, P)
    gates = np.concatenate([ga, gb])
    branches = np.concatenate([blocks_of(np, a["w_branch_a"]), blocks_of(np, a["w_branch_b"])])
    merge = np.stack([gates[2:], branches[:-2]], 1).reshape(4 * KT - 4, P, KT, P)
    wo = blocks_of(np, a["w_o_mem"])
    wo = wo.reshape(4, 2, P, MH, P).transpose(0, 2, 1, 3, 4).reshape(4, P, KT, P)
    cross = np.concatenate([blocks_of(np, a["w_q_mem"])[:, None], blocks_of(np, a["w_kv_mem"]).reshape(MH, 2, P, KT, P)], 1)
    cross = cross.reshape(3 * MH, P, KT, P)
    gate = blocks_of(np, a["w_ffn_in"][:, :FFN])
    up = blocks_of(np, a["w_ffn_in"][:, FFN:])
    down = blocks_of(np, a["w_ffn_out"])
    ffn = []
    for f0, nf in FGROUPS:
        ffn.append(np.stack([gate[f0:f0 + nf], up[f0:f0 + nf]], 1).reshape(2 * nf, P, KT, P))
        d = np.zeros((KT, P, KT, P), win.dtype)
        d[:, :, :nf] = down[:, :, f0:f0 + nf]
        ffn.append(d)
    wblocks = np.concatenate([blocks_of(np, lora), r[0:1], k[0:1], heads, merge, branches[-2:],
                              blocks_of(np, a["w_out"]), cross, wo] + ffn)
    lora_up = np.zeros((HP + 1, P, P), win.dtype)
    lora_up[:HP] = np.concatenate([a["decay_up"], a["iclr_up"]]).reshape(P, HP, P).transpose(1, 0, 2)
    gu = np.zeros((2, P, w), win.dtype)
    gu[0], gu[1, :32] = a["gate_up"][:P], a["gate_up"][P:]
    gate_up2 = gu.reshape(2, P, HP, P).transpose(2, 1, 0, 3)
    sm = a["shift_mix"]
    rows = np.stack([sm[0:w], sm[w:2 * w], sm[2 * w:3 * w], a["decay_base"], a["iclr_base"], a["key_norm_scale"],
                     a["key_iclr_scale"], a["bonus_scale"].reshape(-1), a["lnx_w"], a["lnx_b"]])
    par = np.zeros((P, Q_N), win.dtype)
    par[:, :Q_PRE] = rows.reshape(PP, HP, P).transpose(2, 1, 0).reshape(P, HP * PP)
    for at, name in ((Q_PRE, "g_pre_mix"), (Q_CROSS, "g_pre_cross"), (Q_FFN, "g_pre_ffn"), (Q_MEM, "g_mem")):
        par[:, at:at + KT] = a[name].reshape(KT, P).T
    par[:, Q_LORA] = sm[3072:3200]
    par[:, Q_LORA + 1] = sm[3200:3328]
    par[:32, Q_LORA + 2] = sm[3328:3360]
    return {
        "x": a["x"], "mem": a["mem"], "wblocks": wblocks, "lora_up": lora_up, "gate_up2": gate_up2, "params": par,
        "consts": constants(np), "rel_rev": a["rel_bias"][:, ::-1],
        "g_rows": np.stack([a["g_post_mix"], a["g_post_cross"], a["g_post_ffn"]]),
    }


def constants(np):
    c = np.zeros((P, C_N), np.float32)
    s, t = np.arange(P)[:, None] % C, np.arange(C)[None, :]
    c[:, C_ID:C_ID + P] = np.eye(P)
    c[:, C_MASK:C_MASK + C] = s < t
    c[:, C_MASK + C:C_MASK + P] = s <= t
    c[:, C_EYE:C_EYE + C] = s == t
    lower = lambda row, colm, m: (row // (2 * m) == colm // (2 * m)) & (row // m % 2 == 1) & (colm // m % 2 == 0)
    c[:, C_NL1:C_NL1 + C] = -1.0 * lower(s, t, 1)
    c[:, C_NL1T:C_NL1T + C] = -1.0 * lower(t, s, 1)
    for n, m in enumerate(LEVELS):
        c[:, C_LV + C * n:C_LV + C * (n + 1)] = 1.0 * (s == t) - lower(s, t, m)
    c[:, C_ONES:C_ONES + P] = np.arange(P)[:, None] // C == np.arange(P)[None, :] // C
    c[:, C_CEN:C_CEN + C] = (s == t) - 1.0 / C
    c[:, C_RST:C_RST + SCAN] = np.arange(SCAN)[None, :] % C != 0
    return c


def kernel(**inputs):
    import numpy as np
    from concourse import bacc
    from concourse.bass_utils import run_bass_kernel_spmd

    laid = lay_out(np, {k: np.asarray(v) for k, v in inputs.items()})
    nc = bacc.Bacc("TRN2", target_bir_lowering=False, num_devices=1)
    arrays, args = {}, []
    for name, a in laid.items():
        arrays[f"in_{name}"] = np.ascontiguousarray(a)
        args.append(nc.dram_tensor(f"in_{name}", a.shape, mybir.dt.from_np(a.dtype), kind="ExternalInput").ap())
    out = nc.dram_tensor("out", (SEQ, D), F32, kind="ExternalOutput").ap()
    hybrid_block(nc, *args, out)
    r = run_bass_kernel_spmd(nc, [arrays], core_ids=[0])
    return r.results[0]["out"].reshape(1, SEQ, D)
```
